# Optimizing a Trainium2 kernel written in Bass

```python
import jax, jax.numpy as jnp
from jax import lax
import numpy as np

D_MODEL = 1024
BATCH = 1
SEQ = 256
DEPTH = 2

N_MIXERS = 2
N_A = (DEPTH + 1) // 2
N_B = DEPTH // 2
EPS = 1e-6

CHUNK = 128
A_WIDTH = 2 * D_MODEL
A_GROUPS = 8
A_GDIM = A_WIDTH // A_GROUPS

B_WIDTH = 3 * D_MODEL // 2
B_HEADS = 6
B_HDIM = B_WIDTH // B_HEADS
B_CONV = 4
LRU_C = 8.0

D_FF = 3 * D_MODEL
FFN_CONV = 3


def rms_norm(x, g):
    xf = x.astype(jnp.float32)
    y = xf * lax.rsqrt(jnp.mean(xf * xf, axis=-1, keepdims=True) + EPS)
    return (y * g.astype(jnp.float32)).astype(x.dtype)

def causal_dwconv(x, w, b):
    k, c = w.shape
    y = lax.conv_general_dilated(
        x, w.astype(x.dtype)[:, None, :], window_strides=(1,), padding=[(k - 1, 0)],
        dimension_numbers=("NWC", "WIO", "NWC"), feature_group_count=c)
    return y + b.astype(x.dtype)

def mixer_a(h, w_in, v_gain, w_s, b_s, w_out):
    bsz, s, _ = h.shape
    z = jax.nn.gelu(h @ w_in)
    u, v = jnp.split(z, 2, axis=-1)
    v = rms_norm(v, v_gain)
    v = v.reshape(bsz, s // CHUNK, CHUNK, A_GROUPS, A_GDIM)
    ws = jnp.tril(w_s).astype(v.dtype)
    sv = jnp.einsum("gts,bcsgd->bctgd", ws, v) + b_s.T.astype(v.dtype)[:, :, None]
    y = u * sv.reshape(bsz, s, A_WIDTH)
    return y @ w_out

def _lin_rec_op(c1, c2):
    a1, b1 = c1
    a2, b2 = c2
    return a1 * a2, a2 * b1 + b2

def mixer_b(h, w_in, conv_w, conv_b, w_a, b_a, w_x, b_x, lam, w_out):
    bsz, s, _ = h.shape
    g, xb = jnp.split(h @ w_in, 2, axis=-1)
    g = jax.nn.gelu(g)
    xb = causal_dwconv(xb, conv_w, conv_b)
    xh = xb.reshape(bsz, s, B_HEADS, B_HDIM)
    r = jax.nn.sigmoid(jnp.einsum("bshd,hde->bshe", xh, w_a) + b_a).reshape(bsz, s, B_WIDTH)
    i = jax.nn.sigmoid(jnp.einsum("bshd,hde->bshe", xh, w_x) + b_x).reshape(bsz, s, B_WIDTH)
    log_a = LRU_C * r.astype(jnp.float32) * jax.nn.log_sigmoid(lam.astype(jnp.float32))
    a = jnp.exp(log_a)
    mult = jnp.sqrt(-jnp.expm1(2.0 * log_a))
    bterm = mult * (i * xb).astype(jnp.float32)
    _, hs = lax.associative_scan(_lin_rec_op, (a, bterm), axis=1)
    y = hs.astype(h.dtype) * g
    return y @ w_out

def conv_ffn(h, w_up, conv_w, conv_b, w_down):
    up = causal_dwconv(h @ w_up, conv_w, conv_b)
    gate, val = jnp.split(up, 2, axis=-1)
    return (jax.nn.gelu(gate) * val) @ w_down

def first_inputs(seed: int = 0) -> dict:
    key = jax.random.key(seed)
    ks = jax.random.split(key, 24)
    nrm = jax.random.normal
    f32 = jnp.float32

    x = nrm(ks[0], (BATCH, SEQ, D_MODEL), f32)
    norm_mix = 1.0 + 0.05 * nrm(ks[1], (DEPTH, D_MODEL), f32)
    norm_ffn = 1.0 + 0.05 * nrm(ks[2], (DEPTH, D_MODEL), f32)
    norm_final = 1.0 + 0.05 * nrm(ks[3], (D_MODEL,), f32)

    a_w_in = nrm(ks[4], (N_A, D_MODEL, 2 * A_WIDTH), f32) * D_MODEL ** -0.5
    a_v_gain = 1.0 + 0.05 * nrm(ks[5], (N_A, A_WIDTH), f32)
    a_w_s = nrm(ks[6], (N_A, A_GROUPS, CHUNK, CHUNK), f32) * (0.5 * CHUNK ** -0.5)
    a_b_s = 1.0 + 0.1 * nrm(ks[7], (N_A, A_GROUPS, CHUNK), f32)
    a_w_out = nrm(ks[8], (N_A, A_WIDTH, D_MODEL), f32) * A_WIDTH ** -0.5

    b_w_in = nrm(ks[9], (N_B, D_MODEL, 2 * B_WIDTH), f32) * D_MODEL ** -0.5
    b_conv_w = nrm(ks[10], (N_B, B_CONV, B_WIDTH), f32) * B_CONV ** -0.5
    b_conv_b = 0.01 * nrm(ks[11], (N_B, B_WIDTH), f32)
    b_w_a = nrm(ks[12], (N_B, B_HEADS, B_HDIM, B_HDIM), f32) * B_HDIM ** -0.5
    b_b_a = 0.01 * nrm(ks[13], (N_B, B_HEADS, B_HDIM), f32)
    b_w_x = nrm(ks[14], (N_B, B_HEADS, B_HDIM, B_HDIM), f32) * B_HDIM ** -0.5
    b_b_x = 0.01 * nrm(ks[15], (N_B, B_HEADS, B_HDIM), f32)
    a0 = jax.random.uniform(ks[16], (N_B, B_WIDTH), f32, 0.9, 0.999)
    s0 = a0 ** (1.0 / LRU_C)
    b_lambda = jnp.log(s0) - jnp.log1p(-s0)
    b_w_out = nrm(ks[17], (N_B, B_WIDTH, D_MODEL), f32) * B_WIDTH ** -0.5

    f_w_up = nrm(ks[18], (DEPTH, D_MODEL, 2 * D_FF), f32) * D_MODEL ** -0.5
    f_conv_w = nrm(ks[19], (DEPTH, FFN_CONV, 2 * D_FF), f32) * FFN_CONV ** -0.5
    f_conv_b = 0.01 * nrm(ks[20], (DEPTH, 2 * D_FF), f32)
    f_w_down = nrm(ks[21], (DEPTH, D_FF, D_MODEL), f32) * D_FF ** -0.5

    return {"x": x, "norm_mix": norm_mix, "norm_ffn": norm_ffn, "norm_final": norm_final,
            "a_w_in": a_w_in, "a_v_gain": a_v_gain, "a_w_s": a_w_s, "a_b_s": a_b_s, "a_w_out": a_w_out,
            "b_w_in": b_w_in, "b_conv_w": b_conv_w, "b_conv_b": b_conv_b, "b_w_a": b_w_a, "b_b_a": b_b_a,
            "b_w_x": b_w_x, "b_b_x": b_b_x, "b_lambda": b_lambda, "b_w_out": b_w_out,
            "f_w_up": f_w_up, "f_conv_w": f_conv_w, "f_conv_b": f_conv_b, "f_w_down": f_w_down}

def first_block(x, norm_mix, norm_ffn, norm_final,
              a_w_in, a_v_gain, a_w_s, a_b_s, a_w_out,
              b_w_in, b_conv_w, b_conv_b, b_w_a, b_b_a, b_w_x, b_b_x, b_lambda, b_w_out,
              f_w_up, f_conv_w, f_conv_b, f_w_down):
    for i in range(DEPTH):
        h = rms_norm(x, norm_mix[i])
        j = i // N_MIXERS
        if i % N_MIXERS == 0:
            x = x + mixer_a(h, a_w_in[j], a_v_gain[j], a_w_s[j], a_b_s[j], a_w_out[j])
        else:
            x = x + mixer_b(h, b_w_in[j], b_conv_w[j], b_conv_b[j], b_w_a[j], b_b_a[j],
                            b_w_x[j], b_b_x[j], b_lambda[j], b_w_out[j])
        h = rms_norm(x, norm_ffn[i])
        x = x + conv_ffn(h, f_w_up[i], f_conv_w[i], f_conv_b[i], f_w_down[i])
    return rms_norm(x, norm_final)


DEPTH_2 = 1

N_ATTN_HEADS = 8
ATTN_HEAD_DIM = 64
KV_LATENT = 256
N_IDX_HEADS = 8
IDX_HEAD_DIM = 32
TOPK_MAX = 256
Q_BLOCK = 128
N_RWKV_HEADS = 8
RWKV_HEAD_DIM = 64
DECAY_LORA = 64
AAA_LORA = 64
GATE_LORA = 160
N_GROUPS = 4
EXPERTS_PER_GROUP = 8
N_EXPERTS = N_GROUPS * EXPERTS_PER_GROUP
D_EXPERT = 512
TOP_K_EXPERTS = 2
NORM_EPS = 1e-6
GN_EPS = 64e-5
ATTN_W = N_ATTN_HEADS * ATTN_HEAD_DIM
RWKV_W = N_RWKV_HEADS * RWKV_HEAD_DIM
IDX_Q_W = N_IDX_HEADS * IDX_HEAD_DIM
SHIFT_W = 3 * RWKV_W + DECAY_LORA + AAA_LORA + GATE_LORA
IN_SPLITS = (ATTN_W, KV_LATENT, IDX_Q_W, IDX_HEAD_DIM, N_IDX_HEADS, SHIFT_W, D_MODEL, D_MODEL)
IN_W = ATTN_W + KV_LATENT + IDX_Q_W + IDX_HEAD_DIM + N_IDX_HEADS + SHIFT_W + 2 * D_MODEL


def _split(x, sizes):
    idx = np.cumsum(sizes)[:-1].tolist()
    return jnp.split(x, idx, axis=-1)

def _rmsnorm(x, g):
    xf = x.astype(jnp.float32)
    y = xf * lax.rsqrt(jnp.mean(xf * xf, axis=-1, keepdims=True) + NORM_EPS)
    return (y * g.astype(jnp.float32)).astype(x.dtype)

def _dsa_attention(q, k, v, q_idx, k_idx, w_idx):
    B, S = q.shape[0], q.shape[1]
    top_k = min(TOPK_MAX, S // 4)
    nb = S // Q_BLOCK
    f32 = jnp.float32
    slopes = 2.0 ** (-8.0 * jnp.arange(1, N_ATTN_HEADS + 1, dtype=f32) / N_ATTN_HEADS)
    key_pos = jnp.arange(S)
    k_idx_f = k_idx.astype(f32)
    idx_scale = (IDX_HEAD_DIM ** -0.5) * (N_IDX_HEADS ** -0.5)

    def blocks(a):
        return jnp.moveaxis(a.reshape((B, nb, Q_BLOCK) + a.shape[2:]), 1, 0)

    def one_block(args):
        qb, qib, wib, start = args
        t = start + jnp.arange(Q_BLOCK)
        dots = jnp.einsum('bthd,bsd->bths', qib.astype(f32), k_idx_f)
        score = jnp.einsum('bths,bth->bts', jax.nn.relu(dots), wib.astype(f32)) * idx_scale
        causal = key_pos[None, :] <= t[:, None]
        score = jnp.where(causal[None], score, -jnp.inf)
        _, sel = lax.top_k(score, top_k)
        k_sel = jax.vmap(lambda kb, ib: kb[ib])(k, sel)
        v_sel = jax.vmap(lambda vb, ib: vb[ib])(v, sel)
        logits = jnp.einsum('bthd,btkhd->bthk', qb.astype(f32), k_sel.astype(f32)) * (ATTN_HEAD_DIM ** -0.5)
        dist = (t[None, :, None] - sel).astype(f32)
        logits = logits - slopes[None, None, :, None] * dist[:, :, None, :]
        valid = sel <= t[None, :, None]
        logits = jnp.where(valid[:, :, None, :], logits, -jnp.inf)
        p = jax.nn.softmax(logits, axis=-1)
        o = jnp.einsum('bthk,btkhd->bthd', p, v_sel.astype(f32))
        return o.astype(q.dtype)

    starts = jnp.arange(nb) * Q_BLOCK
    out = lax.map(one_block, (blocks(q), blocks(q_idx), blocks(w_idx), starts))
    return jnp.moveaxis(out, 0, 1).reshape(B, S, ATTN_W)

def _rwkv7_time_mix(p_shift, mu, w0, w2, a0, a2, g2, k_k, k_a, r_k, ln_w, ln_b):
    B, S = p_shift.shape[0], p_shift.shape[1]
    H, N = N_RWKV_HEADS, RWKV_HEAD_DIM
    f32 = jnp.float32
    prev = jnp.pad(p_shift[:, :-1], ((0, 0), (1, 0), (0, 0)))
    mixed = p_shift + (prev - p_shift) * mu
    r, k, v, wl, al, gl = _split(mixed, (RWKV_W, RWKV_W, RWKV_W, DECAY_LORA, AAA_LORA, GATE_LORA))
    w = -jax.nn.softplus(-(w0 + jnp.tanh(wl) @ w2)) - 0.5
    decay = jnp.exp(-jnp.exp(w.astype(f32)))
    a = jax.nn.sigmoid(a0 + al @ a2)
    g = jax.nn.sigmoid(gl) @ g2
    heads = lambda z: z.reshape(B, S, H, N).astype(f32)
    kk = heads(k * k_k)
    kk = kk / jnp.maximum(jnp.sqrt(jnp.sum(kk * kk, axis=-1, keepdims=True)), 1e-12)
    k = k * (1.0 + (a - 1.0) * k_a)
    r_h, k_h, v_h, a_h, d_h = heads(r), heads(k), heads(v), heads(a), heads(decay)

    def step(state, inp):
        r_t, d_t, k_t, v_t, kk_t, b_t = inp
        sa = jnp.einsum('bhij,bhj->bhi', state, -kk_t)
        state = state * d_t[:, :, None, :] + sa[..., None] * b_t[:, :, None, :] + v_t[..., None] * k_t[:, :, None, :]
        y = jnp.einsum('bhij,bhj->bhi', state, r_t)
        return state, y

    xs = tuple(jnp.moveaxis(z, 1, 0) for z in (r_h, d_h, k_h, v_h, kk, kk * a_h))
    _, y = lax.scan(step, jnp.zeros((B, H, N, N), f32), xs)
    y = jnp.moveaxis(y, 0, 1)
    mean = jnp.mean(y, axis=-1, keepdims=True)
    var = jnp.mean(jnp.square(y - mean), axis=-1, keepdims=True)
    y = ((y - mean) * lax.rsqrt(var + GN_EPS)).reshape(B, S, RWKV_W) * ln_w + ln_b
    bonus = (jnp.sum(r_h * k_h * r_k, axis=-1, keepdims=True) * v_h).reshape(B, S, RWKV_W)
    return ((y + bonus) * g).astype(p_shift.dtype)

def _hier_moe(xt, wg_router, we_router, e_bias, w_gate, w_up, w_down):
    T, D = xt.shape
    f32 = jnp.float32
    p_group = jax.nn.softmax((xt @ wg_router).astype(f32), axis=-1)
    g_sel = jnp.argmax(p_group, axis=-1)
    p_gsel = jnp.max(p_group, axis=-1)
    e_logits = (xt @ we_router).astype(f32).reshape(T, N_GROUPS, EXPERTS_PER_GROUP) + e_bias.astype(f32).reshape(N_GROUPS, EXPERTS_PER_GROUP)
    e_in = jnp.take_along_axis(e_logits, g_sel[:, None, None], axis=1)[:, 0]
    top_v, top_i = lax.top_k(e_in, TOP_K_EXPERTS)
    w_top = jax.nn.softmax(top_v, axis=-1) * p_gsel[:, None]
    expert_id = g_sel[:, None] * EXPERTS_PER_GROUP + top_i
    combine = jnp.sum(jax.nn.one_hot(expert_id, N_EXPERTS, dtype=f32) * w_top[..., None], axis=1)

    def body(acc, ew):
        wg, wu, wd, cw = ew
        hdn = jax.nn.silu(xt @ wg) * (xt @ wu)
        return acc + cw[:, None] * (hdn @ wd).astype(f32), None

    acc, _ = lax.scan(body, jnp.zeros((T, D), f32), (w_gate, w_up, w_down, combine.T))
    return acc.astype(xt.dtype)

def second_inputs(seed: int = 0) -> dict:
    key = jax.random.key(seed)
    ks = iter(jax.random.split(key, 40))
    nrm = lambda shape, scale: jax.random.normal(next(ks), shape, jnp.float32) * scale
    L = DEPTH_2
    return {
        "x": nrm((BATCH, SEQ, D_MODEL), 1.0),
        "c": nrm((BATCH, D_MODEL), 1.0),
        "ada_w": nrm((L, D_MODEL, 6 * D_MODEL), 0.5 * D_MODEL ** -0.5),
        "ada_b": nrm((L, 6 * D_MODEL), 0.02),
        "mix_norm_g": 1.0 + nrm((L, D_MODEL), 0.02),
        "w_in": nrm((L, D_MODEL, IN_W), D_MODEL ** -0.5),
        "kv_norm_g": 1.0 + nrm((L, KV_LATENT), 0.02),
        "w_kv_up": nrm((L, KV_LATENT, 2 * ATTN_W), KV_LATENT ** -0.5),
        "q_norm_g": 1.0 + nrm((L, ATTN_HEAD_DIM), 0.02),
        "k_norm_g": 1.0 + nrm((L, ATTN_HEAD_DIM), 0.02),
        "rwkv_mu": jax.random.uniform(next(ks), (L, SHIFT_W), jnp.float32, 0.2, 0.8),
        "rwkv_w0": -1.0 + nrm((L, RWKV_W), 0.5),
        "rwkv_w2": nrm((L, DECAY_LORA, RWKV_W), 0.5 * DECAY_LORA ** -0.5),
        "rwkv_a0": nrm((L, RWKV_W), 0.1),
        "rwkv_a2": nrm((L, AAA_LORA, RWKV_W), 0.5 * AAA_LORA ** -0.5),
        "rwkv_g2": nrm((L, GATE_LORA, RWKV_W), GATE_LORA ** -0.5),
        "rwkv_k_k": 0.85 + nrm((L, RWKV_W), 0.02),
        "rwkv_k_a": 1.0 + nrm((L, RWKV_W), 0.02),
        "rwkv_r_k": nrm((L, N_RWKV_HEADS, RWKV_HEAD_DIM), 0.1),
        "rwkv_ln_w": 1.0 + nrm((L, RWKV_W), 0.02),
        "rwkv_ln_b": nrm((L, RWKV_W), 0.02),
        "w_branch_attn": nrm((L, ATTN_W, D_MODEL), ATTN_W ** -0.5),
        "w_branch_rwkv": nrm((L, RWKV_W, D_MODEL), RWKV_W ** -0.5),
        "w_out": nrm((L, D_MODEL, D_MODEL), D_MODEL ** -0.5),
        "moe_norm_g": 1.0 + nrm((L, D_MODEL), 0.02),
        "router_group_w": nrm((L, D_MODEL, N_GROUPS), D_MODEL ** -0.5),
        "router_expert_w": nrm((L, D_MODEL, N_EXPERTS), D_MODEL ** -0.5),
        "router_expert_bias": nrm((L, N_EXPERTS), 0.01),
        "expert_w_gate": nrm((L, N_EXPERTS, D_MODEL, D_EXPERT), D_MODEL ** -0.5),
        "expert_w_up": nrm((L, N_EXPERTS, D_MODEL, D_EXPERT), D_MODEL ** -0.5),
        "expert_w_down": nrm((L, N_EXPERTS, D_EXPERT, D_MODEL), D_EXPERT ** -0.5),
    }

def second_block(x, c, ada_w, ada_b, mix_norm_g, w_in, kv_norm_g, w_kv_up, q_norm_g, k_norm_g,
              rwkv_mu, rwkv_w0, rwkv_w2, rwkv_a0, rwkv_a2, rwkv_g2, rwkv_k_k, rwkv_k_a, rwkv_r_k,
              rwkv_ln_w, rwkv_ln_b, w_branch_attn, w_branch_rwkv, w_out, moe_norm_g,
              router_group_w, router_expert_w, router_expert_bias, expert_w_gate, expert_w_up,
              expert_w_down):
    B, S, D = x.shape
    h = x
    for l in range(DEPTH_2):
        mod = jax.nn.silu(c) @ ada_w[l] + ada_b[l]
        sh1, sc1, gt1, sh2, sc2, gt2 = jnp.split(mod[:, None, :], 6, axis=-1)

        xn = _rmsnorm(h, mix_norm_g[l]) * (1.0 + sc1) + sh1
        proj = xn @ w_in[l]
        q_a, kv_lat, q_i, k_i, w_i, p_shift, gate_a, gate_r = _split(proj, IN_SPLITS)
        q = _rmsnorm(q_a.reshape(B, S, N_ATTN_HEADS, ATTN_HEAD_DIM), q_norm_g[l])
        kv = _rmsnorm(kv_lat, kv_norm_g[l]) @ w_kv_up[l]
        k_lin, v_lin = jnp.split(kv, 2, axis=-1)
        k = _rmsnorm(k_lin.reshape(B, S, N_ATTN_HEADS, ATTN_HEAD_DIM), k_norm_g[l])
        v = v_lin.reshape(B, S, N_ATTN_HEADS, ATTN_HEAD_DIM)
        o_attn = _dsa_attention(q, k, v, q_i.reshape(B, S, N_IDX_HEADS, IDX_HEAD_DIM), k_i, w_i)
        o_rwkv = _rwkv7_time_mix(p_shift, rwkv_mu[l], rwkv_w0[l], rwkv_w2[l], rwkv_a0[l], rwkv_a2[l],
                                 rwkv_g2[l], rwkv_k_k[l], rwkv_k_a[l], rwkv_r_k[l], rwkv_ln_w[l], rwkv_ln_b[l])
        merged = jax.nn.sigmoid(gate_a) * (o_attn @ w_branch_attn[l]) + jax.nn.sigmoid(gate_r) * (o_rwkv @ w_branch_rwkv[l])
        h = h + gt1 * (merged @ w_out[l])

        xn2 = _rmsnorm(h, moe_norm_g[l]) * (1.0 + sc2) + sh2
        moe = _hier_moe(xn2.reshape(B * S, D), router_group_w[l], router_expert_w[l], router_expert_bias[l],
                        expert_w_gate[l], expert_w_up[l], expert_w_down[l])
        h = h + gt2 * moe.reshape(B, S, D)
    return h


def setup_inputs(seed=0):
    out = dict(first_inputs(seed))
    for name, value in second_inputs(seed + 1).items():
        if name != "x":
            out[name + "_2"] = value
    return out


def reference(
    x, norm_mix, norm_ffn, norm_final, a_w_in, a_v_gain, a_w_s, a_b_s, a_w_out, b_w_in,
    b_conv_w, b_conv_b, b_w_a, b_b_a, b_w_x, b_b_x, b_lambda, b_w_out, f_w_up, f_conv_w,
    f_conv_b, f_w_down, c_2, ada_w_2, ada_b_2, mix_norm_g_2, w_in_2, kv_norm_g_2, w_kv_up_2,
    q_norm_g_2, k_norm_g_2, rwkv_mu_2, rwkv_w0_2, rwkv_w2_2, rwkv_a0_2, rwkv_a2_2, rwkv_g2_2,
    rwkv_k_k_2, rwkv_k_a_2, rwkv_r_k_2, rwkv_ln_w_2, rwkv_ln_b_2, w_branch_attn_2,
    w_branch_rwkv_2, w_out_2, moe_norm_g_2, router_group_w_2, router_expert_w_2,
    router_expert_bias_2, expert_w_gate_2, expert_w_up_2, expert_w_down_2,
):
    x = first_block(
        x, norm_mix, norm_ffn, norm_final, a_w_in, a_v_gain, a_w_s, a_b_s, a_w_out, b_w_in,
        b_conv_w, b_conv_b, b_w_a, b_b_a, b_w_x, b_b_x, b_lambda, b_w_out, f_w_up, f_conv_w,
        f_conv_b, f_w_down,
    )
    return second_block(
        x, c_2, ada_w_2, ada_b_2, mix_norm_g_2, w_in_2, kv_norm_g_2, w_kv_up_2, q_norm_g_2,
        k_norm_g_2, rwkv_mu_2, rwkv_w0_2, rwkv_w2_2, rwkv_a0_2, rwkv_a2_2, rwkv_g2_2,
        rwkv_k_k_2, rwkv_k_a_2, rwkv_r_k_2, rwkv_ln_w_2, rwkv_ln_b_2, w_branch_attn_2,
        w_branch_rwkv_2, w_out_2, moe_norm_g_2, router_group_w_2, router_expert_w_2,
        router_expert_bias_2, expert_w_gate_2, expert_w_up_2, expert_w_down_2,
    )


_drawn_inputs = setup_inputs


def setup_inputs(seed=0):
    import zlib

    import numpy as np

    out = dict(_drawn_inputs(seed))
    spreads = {}
    factors = {'a_v_gain': 3.206,
     'b_b_a': 8.0,
     'b_b_x': 8.0,
     'f_conv_b': 3.536,
     'mix_norm_g_2': 4.774,
     'kv_norm_g_2': 28.986,
     'q_norm_g_2': 37.89,
     'k_norm_g_2': 29.286,
     'rwkv_w2_2': 4.584,
     'rwkv_a0_2': 8.0,
     'rwkv_a2_2': 2.764,
     'rwkv_k_k_2': 64.0,
     'rwkv_k_a_2': 8.0,
     'rwkv_ln_w_2': 64.0,
     'rwkv_ln_b_2': 64.0,
     'moe_norm_g_2': 15.716,
     'router_expert_bias_2': 37.432,
     'rwkv_w0_2': 4.731}
    for name, (base, spread) in spreads.items():
        noise = np.random.default_rng([zlib.crc32(name.encode()), seed]).standard_normal(out[name].shape)
        drawn = base * np.exp(spread * noise) if base else spread * noise
        out[name] = __import__('jax').numpy.asarray(drawn.astype(out[name].dtype))
    for name, factor in factors.items():
        out[name] = (out[name] * factor).astype(out[name].dtype)
    return out
```

```python
from contextlib import ExitStack

import numpy as np

import concourse.bass as bass
from concourse import mybir

ALU = mybir.AluOpType
ACT = mybir.ActivationFunctionType
F32 = mybir.dt.float32
I32 = mybir.dt.int32
U32 = mybir.dt.uint32
AX = mybir.AxisListType

P = 128
SEQ = 256
C = SEQ // P
D = 1024
KD = D // P
A_W = 2048
A_G = 8
B_W = 1536
KB = B_W // P
B_H = 6
FF = 3072
KF = FF // P
EPS = 1e-6
TILE = 8 * 512
RING = 4

AH = 8
HD = 64
IH = 8
IHD = 32
TOPK = 64
NG = 4
NE = 32
EPG = NE // NG
DE = 512
SLOT = 64
MAX_ITEMS = 40
KAPPA = float(np.exp(-0.5))
FAR = -1e30

ROWS = {}


def _rows():
    groups = [
        [("norm_mix", 16), ("norm_ffn", 16), ("a_gain", 16), ("cvec", 8), ("mix_g", 8), ("bcw", 48)],
        [("fcw0_0", 48), ("fcw0_1", 48), ("moe_g", 8), ("k_k", 4), ("k_a", 4), ("w0", 4), ("a0", 4)],
        [("fcw0_2", 48), ("fcb0", 48), ("lam", 12), ("bcb", 12)],
        [("fcw1_0", 48), ("fcw1_1", 48), ("bba", 12), ("bbx", 12)],
        [("fcw1_2", 48), ("fcb1", 48), ("mu", 14), ("mu_tail", 1), ("r_k", 4), ("kv_g", 2), ("q_g", 1), ("k_g", 1)],
        [("sh1", 8), ("sc1", 8), ("sh2", 8), ("sc2", 8)],
    ]
    for g, group in enumerate(groups):
        at = 0
        for name, n in group:
            ROWS[name] = (g, at, n)
            at += n
    return groups


ROW_GROUPS = _rows()
NCOLS = len(ROW_GROUPS) * P

CONSTS = {}


def _constants():
    s = np.arange(P)[:, None]
    t = np.arange(P)[None, :]
    parts = []

    def put(name, a):
        a = np.broadcast_to(np.asarray(a, np.float32), (P, np.asarray(a).shape[-1]))
        at = sum(x.shape[1] for x in parts)
        CONSTS[name] = (at, a.shape[1])
        parts.append(a)

    put("ident", s == t)
    put("ones", np.ones((1, P)))
    put("before", s < t)
    put("head_ones", s // HD == t // HD)
    put("keep", np.concatenate([s < t, s <= t, s < t, s <= t], 1))
    put("level", np.concatenate([(s >> i == t >> i) & ((t >> (i - 1)) % 2 == 1) & ((s >> (i - 1)) % 2 == 0)
                                 for i in range(1, 8)], 1))
    put("dist", np.concatenate([s + c * P - np.arange(SEQ)[None, :] for c in range(C)], 1))
    put("iota", np.arange(MAX_ITEMS)[None, :])
    put("steps", ((1 + np.arange(3)) * SLOT)[None, :])
    put("pairs", (2 * np.arange(4))[None, :])
    put("first_item", (SLOT * np.arange(NE))[None, :])
    put("extra_item", (SLOT * (NE - 1 - np.arange(NE)))[None, :])
    return np.ascontiguousarray(np.concatenate(parts, 1), np.float32)


class Plan:

    def __init__(self):
        self.groups, self.uses, self.fulls, self.tiles, self.body = {}, [0] * 8, [0] * 8, 0, None

    def group(self, key, bank, closes_tile=False):
        self.uses[bank] += 1
        if closes_tile:
            self.tiles += 1
            full = ("tile", self.tiles)
        else:
            self.fulls[bank] += 1
            full = ("bank", self.fulls[bank])
        self.groups[key] = [bank, self.uses[bank] - 1, full, 0, 0]
        if self.body is not None:
            self.body.append(key)

    def tile(self):
        self.tiles += 1

    def loop(self, times, body):
        uses, fulls, tiles = list(self.uses), list(self.fulls), self.tiles
        self.body = []
        body()
        for key in self.body:
            g = self.groups[key]
            g[3] = self.uses[g[0]] - uses[g[0]]
            g[4] = self.tiles - tiles if g[2][0] == "tile" else self.fulls[g[0]] - fulls[g[0]]
        self.body = None
        for b in range(8):
            self.uses[b] += (times - 1) * (self.uses[b] - uses[b])
            self.fulls[b] += (times - 1) * (self.fulls[b] - fulls[b])
        self.tiles += (times - 1) * (self.tiles - tiles)


def at_turn(value, stride, i):
    return value if i is None else i * stride + value


class Steps:

    def __init__(self, eng, sem):
        self.eng, self.sem, self.n, self.i, self.per = eng, sem, 0, None, 0

    def __call__(self, instruction):
        instruction.then_inc(self.sem, 1)
        self.n += 1

    def join(self):
        self.eng.wait_ge(self.sem, at_turn(self.n, self.per, self.i))

    def enter(self, i, per):
        self.i, self.per, self.start = i, per, self.n

    def leave(self, times):
        assert self.n - self.start == self.per, (self.n - self.start, self.per)
        self.n += (times - 1) * self.per
        self.i = None

SCRATCH = {"xs": (MAX_ITEMS * SLOT, D), "mod": (6 * D,)}


def make_plan():
    p = Plan()
    T = {}

    def norm(n):
        for b in range(4):
            p.group(("norm", n, b), b)

    def ada(q):
        T["ada", q] = p.tiles
        for _ in range(3):
            p.tile()
        p.group(("ada", q), 7, closes_tile=True)

    def ffn(l):
        T["up", l] = p.tiles

        def body():
            for u in range(2):
                for h in range(2):
                    p.group(("gate", l, u, h), 4 * u + 2 * h, closes_tile=h == 1)
                    p.group(("val", l, u, h), 4 * u + 2 * h + 1, closes_tile=h == 1)
        p.loop(3, body)
        T["down", l] = p.tiles
        for n in range(2):
            p.tile()
            p.tile()
            p.group(("down", l, n, 0), 2 * n)
            p.group(("down", l, n, 1), 2 * n + 1, closes_tile=True)

    p.group(("rows", 0), 4)
    norm(0)
    T["av"] = p.tiles
    for j in range(4):
        for c in range(C):
            p.group(("av", j, c), 4 + (2 * j + c) % 4, closes_tile=c == 1)
    for g in range(1, 5):
        p.group(("rows", g), g - 1)
    for q in range(2):
        p.group(("ws", q), q)
    T["au"] = p.tiles
    for j in range(4):
        for h in range(2):
            p.group(("au", j, h), (2 * j + h) % 4, closes_tile=h == 1)
    for m in range(8):
        p.group(("sv", m), 4 + m % 4)
    T["ao"] = p.tiles
    for n in range(2):
        p.tile()
        p.group(("ao", n, 0), 2 * n)
        p.group(("ao", n, 1), 2 * n + 1, closes_tile=True)
    ada(0)
    norm(1)
    ffn(0)
    ada(1)
    norm(2)
    T["bx"] = p.tiles
    for q in range(6):
        p.group(("bx", q), q, closes_tile=q % 2 == 1)
    T["bgate"] = p.tiles
    for h in range(B_H):
        p.group(("br", h), (6 + 2 * h) % 8, closes_tile=h == B_H - 1)
        p.group(("bi", h), (7 + 2 * h) % 8, closes_tile=h == B_H - 1)
    T["bg"] = p.tiles
    for q in range(6):
        p.group(("bg", q), 2 + q, closes_tile=q % 2 == 1)
    T["bo"] = p.tiles
    p.tile()
    p.tile()
    for n in range(2):
        p.group(("bo", n, 0), 2 * n)
        p.group(("bo", n, 1), 2 * n + 1, closes_tile=n == 1)
    ada(2)
    norm(3)
    ffn(1)
    def gates(j, *at):
        T["gate", j] = p.tiles
        for h in range(2):
            p.group(("ga", 2 * j + h), at[h], closes_tile=h == 1)

    p.group(("rows", 5), 4)
    norm(4)
    for name, q in (("lora", 0), ("lora", 1), ("r", 0), ("r", 1), ("k", 0), ("k", 1), ("v", 0), ("v", 1)):
        if (name, q) == ("lora", 0):
            T["lora"] = p.tiles
            p.group(("kw", 0), 5)
        if name in "rkv" and q == 0:
            T[name] = p.tiles
        p.group((name, q), {"lora": 6, "r": 0, "k": 2, "v": 4}[name] + q, closes_tile=q == 1)
    for q in range(2):
        p.group(("zw", q), 6 + q)
    for q in range(2):
        p.group(("za", q), q)
    for c in range(C):
        p.group(("gg", c), 2 + c)
    T["q"] = p.tiles
    for c in range(C):
        p.group(("q", c), 4 + c, closes_tile=c == 1)
    T["kv"] = p.tiles
    p.group(("kv", 0), 6)
    p.group(("qi", 0), 7, closes_tile=True)
    for q in range(2):
        p.group(("kn", q), q)
    gates(0, 7, 0)
    for q in range(2):
        p.group(("qt", q), 2 + q)
    p.group(("kvt", 0), 4)
    gates(1, 1, 2)
    T["kvup"] = p.tiles
    for c in range(C):
        p.group(("kr", c), 5 + c)
    for c in range(C):
        p.group(("vr", c), 7 if c == 0 else 0, closes_tile=c == 1)
    p.group(("wi", 0), 1)
    for c in range(C):
        for b in range(4):
            p.group(("dot", c, b), 2 + b if c == 0 else (6 + b) % 8)
    for q in range(2):
        p.group(("kt", q), 2 + q)
    gates(2, 0, 1)
    gates(3, 6, 7)
    for c in range(C):
        for g in range(4):
            p.group(("lg", c, g), 4 + (g % 2))
            if g > 0:
                p.group(("pt", c, g - 1), 6 + (g - 1) % 2)
        p.group(("pt", c, 3), 7)
    for c in range(C):
        p.group(("o", c), 2 + c)
    for q in range(2):
        p.group(("oat", q), 4 + q)
    for c in range(C):
        p.group(("vt", c), 6 + c)
    p.group(("bt", 0), 0)
    p.group(("ktt", 0), 1)
    p.group(("bonus", 0), 2)
    for c in range(C):
        for h in range(8):
            p.group(("mt", c, h), 4 + h % 4)
        for hf in range(2):
            p.group(("t1", c, 1, hf), hf)
        for lv in range(2, 8):
            for hf in range(2):
                p.group(("t1", c, lv, hf), hf)
            for hf in range(2):
                if lv < 7:
                    p.group(("xa", c, lv, hf), 2 + hf)
                p.group(("xb", c, lv, hf), 4 + hf)
        for par in range(2):
            p.group(("rh", c, par), 6 + par)
        p.group(("sa", c), 0)
        for par in range(2):
            p.group(("y", c, par), 2 + par)
        if c == 0:
            p.group(("z", 0), 4)
    for q in range(2):
        p.group(("ort", q), 6 + q)
    T["branch"] = p.tiles
    for b in range(2):
        for q in range(4):
            p.group(("br", b, q), (4 * b + q) % 8, closes_tile=q == 3)
    T["mo"] = p.tiles
    for n in range(2):
        p.group(("mo", n, 0), 2 * n)
        p.group(("mo", n, 1), 2 * n + 1, closes_tile=True)
    norm(5)
    p.group(("route", 0), 4)
    p.group(("count", 0), 5)
    return p, T


def build(nc, x, w, out, scratch):
    plan, T = make_plan()
    _constants()
    ctx = ExitStack()
    with ctx:
        def sb(name, shape, dt=F32):
            return ctx.enter_context(nc.sbuf_tensor(name, shape, dt))

        def sem(name):
            return ctx.enter_context(nc.semaphore(name))

        NCONST = sum(n for _, n in CONSTS.values())
        ARENA = 26880
        big = sb("big", [P, RING * TILE + ARENA])
        X = sb("X", [P, C, D])
        xn = sb("xn", [P, C, D])
        hT = sb("hT", [P, KD, SEQ])
        cols = sb("cols", [P, NCOLS])
        const = sb("const", [P, NCONST])
        small = sb("small", [P, 256])
        banks = [ctx.enter_context(nc.psum_tensor(f"bank{b}", [P, 512], F32)) for b in range(8)]

        def con(name, parts=P):
            at, n = CONSTS[name]
            return const[0:parts, at:at + n]

        def col(name, k=0, n=1):
            g, at, _ = ROWS[name]
            return cols[:, g * P + at + k:g * P + at + k + n]

        def col_at(name, k):
            g, at, _ = ROWS[name]
            return cols[:, bass.ds(k + (g * P + at), 1)]

        ident = con("ident")
        ring = [big[:, s * TILE:(s + 1) * TILE] for s in range(RING)]
        arena = big[:, RING * TILE:RING * TILE + ARENA]

        def area(at, *shape):
            n = int(np.prod(shape))
            assert at + n <= ARENA, (at, n)
            v = arena[:, at:at + n]
            if len(shape) == 2:
                v = v.rearrange("p (a b) -> p a b", b=shape[1])
            if len(shape) == 3:
                v = v.rearrange("p (a b c) -> p a b c", b=shape[1], c=shape[2])
            return v

        V = area(0, C, A_W)
        uT = area(4096, 16, SEQ)
        bsb = area(8192, A_G, P)
        ws_in = area(9216, A_G, P)
        wsT = area(10240, A_G * P)
        wsr = area(11264, C, A_G * P)
        sv_tmp = area(13312, 4, SEQ)
        v_junk = area(14336, A_W)
        rowbuf = area(16384, 5, P)
        adab = area(17024, 3, 512)
        ffT = area(0, KF, SEQ)
        conv_g = area(6144, 4, 512)
        conv_v = area(8192, 4, 512)
        gelu_g = area(10240, 4, 512)
        xbT = area(0, KB, SEQ)
        Rt = area(3072, KB, SEQ)
        It = area(6144, KB, SEQ)
        At = area(9216, KB, SEQ)
        Tt = area(12288, KB, SEQ)
        Gt = area(18560, KB, SEQ)
        lamt = area(21632, 4, KB)
        ssq = small[:, 0:2]
        var = small[:, 2:4]
        std = small[:, 4:6]
        rstd = small[:, 6:8]
        vsq = small[:, 8:10]
        vvar = small[:, 10:12]
        vstd = small[:, 12:14]
        vrstd = small[:, 14:16]
        sil = small[:, 16:24]
        s8 = small[:, 24:36]

        ld_x, ld_ident, ld_const, ld_ws, ld_bs, ld_adab = sem("ld_x"), sem("ld_ident"), sem("ld_const"), sem("ld_ws"), sem("ld_bs"), sem("ld_adab")
        ld_rows = [sem(f"ld_rows{g}") for g in range(5)]
        rows_zero = sem("rows_zero")
        tile_loaded = [sem(f"tile_loaded{s}") for s in range(RING)]
        tile_used = sem("tile_used")
        bank_full = [sem(f"bank_full{b}") for b in range(8)]
        bank_free = [sem(f"bank_free{b}") for b in range(8)]
        act_steps, dve_steps, pool_steps = sem("act_steps"), sem("dve_steps"), sem("pool_steps")
        norm_sq, norm_var, norm_std, norm_rstd = sem("norm_sq"), sem("norm_var"), sem("norm_std"), sem("norm_rstd")
        xn_ready = [sem(f"xn_ready{c}") for c in range(C)]
        v_sq, v_var, v_std = sem("v_sq"), sem("v_var"), sem("v_std")
        ws_scaled, y_ready = sem("ws_scaled"), sem("y_ready")
        silu_ready = sem("silu_ready")
        conv_g0, conv_v0, gelu_done, ff_ready = sem("conv_g0"), sem("conv_v0"), sem("gelu_done"), sem("ff_ready")
        bx0, b_log, b_exp, b_gated, b_m2, b_mult, b_y = (sem("bx0"), sem("b_log"), sem("b_exp"), sem("b_gated"),
                                                          sem("b_m2"), sem("b_mult"), sem("b_y"))
        lam_exp = sem("lam_exp")
        st_mod, st_out = sem("st_mod"), sem("st_out")

        mix = area(0, 15, SEQ)
        sw = area(4096, 4, SEQ)
        cum = area(5120, 4, SEQ)
        em = area(6144, 4, SEQ)
        kx = area(7168, 4, SEQ)
        sq = area(8192, 4, SEQ)
        aS = area(9216, 4, SEQ)
        QR = area(10240, 8, 2, P)
        Kh = area(12288, 4, SEQ)
        vtok = area(13312, C, 512)
        btok = area(14336, 512)
        ktok = area(14848, 512)
        gtok = area(15360, C, 512)
        ytok = area(16384, C, 512)
        satok = area(17408, C, 512)
        rhtok = area(18432, 512)
        zst = area(18944, 4, HD)
        XT = area(19200, C, 8, P)
        Xm = area(21248, 8, P)
        T1 = area(22272, 8, P)
        CT = area(23296, 8, P)
        lnw = area(24320, 512)
        lnb = area(24832, 512)
        rw = area(25344, KD, 36)
        rbias = area(25632, NE)
        gt1b = area(25856, D)
        MT = area(0, 8, 512)
        gates = area(4096, 16, SEQ)
        mergT = area(0, 8, SEQ)
        orT = area(10240, 4, SEQ)
        gfb = area(13312, D)
        kw_sb = area(16384, SEQ)
        kirep = area(16640, SEQ)
        qiT = area(16896, 2, SEQ)
        qn = area(17408, C, 512)
        kvn = area(18432, C, SEQ)
        kvnT = area(18944, 2, SEQ)
        qT = area(19456, 4, SEQ)
        kT = area(20480, 4, SEQ)
        Vt = area(21504, C, 512)
        rel = area(22528, 2, 512)
        sc = area(23552, C, SEQ)
        Pb = area(13312, 2, 2, SEQ)
        pT = area(14336, 2, 4, P)
        wa2 = area(22784, 512)
        g2 = area(23296, 2, 512)
        oaT = xn[:, 0, :].rearrange("p (m t) -> p m t", t=SEQ)
        work = xn[:, 1, 0:512].rearrange("p (c s) -> p c s", c=C)
        neg = xn[:, 1, 512:1024].rearrange("p (c s) -> p c s", c=C)
        otok = qn
        gm1, gm2 = small[:, 36:44], small[:, 44:52]
        omu = small[:, 52:67]
        cmid, dmid, epc = small[:, 68:76], small[:, 76:84], small[:, 84:92]
        qst, kst, kvst = small[:, 92:108], small[:, 108:124], small[:, 124:126]
        gq8 = small[:, 126:127]
        wi = small[:, 128:144]
        m8 = small[:, 144:160]
        nmax, psum_, prec = small[:, 160:176], small[:, 176:192], small[:, 192:208]
        bonus = small[:, 208:224]
        gn_a, gn_b = small[:, 224:232], small[:, 232:240]
        rkbd = small[:, 240:248].rearrange("p (m h) -> p m h", h=2)
        slots = [big[:, s * TILE:(s + 1) * TILE] for s in range(6)]
        xsl = area(8192, D)
        xgT = area(10240, KD, P)
        sg = area(11264, 2, 256)
        hd = area(11776, 2, 256)
        hTe = area(12288, 2, 256)
        ysb = area(12800, 2, 512)
        gt2b = area(13824, D)
        yk = area(14848, 4, D)
        lg = area(19000, C, 36)
        gtmp = area(19080, C, 8)
        oh = area(19100, 2, C, NE)
        elm = area(19228, C, NE)
        etmp = area(19292, C, NE)
        dest = area(19356, C, NE)
        rsm = area(19420, 64)
        cnt4 = area(19500, NE, 3)
        icl = area(19628, 3, NE)
        itm = area(19724, 8, NE)
        fidx = area(21004, 48)
        idx = area(21052, 4).bitcast(U32)
        eid = area(21056, MAX_ITEMS + 2).bitcast(I32)
        msum = area(21100, C, NE)

        ld_mod, ld_gfb, ld_mx, ld_ln, ld_gt1, ld_gt2, ld_rep = (sem("ld_mod"), sem("ld_gfb"), sem("ld_mx"), sem("ld_ln"),
                                                                sem("ld_gt1"), sem("ld_gt2"), sem("ld_rep"))
        ld_route = sem("ld_route")
        x_final, gm_ready, mix0, lora_act, cum_ready, exp_ready = (sem("x_final"), sem("gm_ready"), sem("mix0"),
                                                                   sem("lora_act"), sem("cum_ready"), sem("exp_ready"))
        kx2, qr_ready = sem("kx2"), sem("qr_ready")
        q_sq, q_var, q_root, k_sq, k_var, k_root = (sem("q_sq"), sem("q_var"), sem("q_root"), sem("k_sq"), sem("k_var"),
                                                    sem("k_root"))
        rel_used, score_sum, score_masked, neg_raw, neg_ready = (
            sem("rel_used"), sem("score_sum"), sem("score_masked"), sem("neg_raw"), sem("neg_ready"))
        lg_ready, p_ready = sem("lg_ready"), sem("p_ready")
        ct_ready, x_first, mt_clear = sem("ct_ready"), sem("x_first"), sem("mt_clear")
        gn_var, gn_root, or_rows, merg = sem("gn_var"), sem("gn_root"), sem("or_rows"), sem("merg")
        xs_zero, xs_cleared, ge_exp, ge_in, two_in, two_exp, picks, idx_ready, scattered = (
            sem("xs_zero"), sem("xs_cleared"), sem("ge_exp"), sem("ge_in"), sem("two_in"), sem("two_exp"), sem("picks"),
            sem("idx_ready"), sem("scattered"))
        e_w = [sem(f"expert_w{s}") for s in range(6)]
        e_x = sem("expert_x")
        st_y = [sem(f"st_y{u}") for u in range(2)]
        expert_used, tx_full, xg_ready, sg_ready, hd_ready, ht_full, ht_ready, y_copied = (
            sem("expert_used"), sem("tx_full"), sem("xg_ready"), sem("sg_ready"), sem("hd_ready"), sem("ht_full"),
            sem("ht_ready"), sem("y_copied"))
        gathered, fin_c, eid_ready = sem("gathered"), sem("fin_c"), sem("eid_ready")
        pv_used, y_sb, xg_half, fin_steps = sem("pv_used"), sem("y_sb"), sem("xg_half"), sem("fin_steps")

        def head_of(g, j):
            return 4 * (g // 2) + g % 2 + 2 * j

        def bank(key):
            return banks[plan.groups[key][0]]

        def wait_free(eng, key, i=None):
            b, use, _, du, _ = plan.groups[key]
            if use > 0:
                eng.wait_ge(bank_free[b], at_turn(use, du, i))

        def wait_full(eng, key, i=None):
            b, _, (kind, value), _, df = plan.groups[key]
            eng.wait_ge(tile_used if kind == "tile" else bank_full[b], at_turn(value, df, i))

        def wait_drained(eng, key, i=None):
            b, use, _, du, _ = plan.groups[key]
            eng.wait_ge(bank_free[b], at_turn(use + 1, du, i))

        def fills(matmul, key):
            b, _, (kind, _), _, _ = plan.groups[key]
            matmul.then_inc(tile_used if kind == "tile" else bank_full[b], 1)

        def drains(instruction, key):
            instruction.then_inc(bank_free[plan.groups[key][0]], 1)

        def wait_tile(eng, t, i=None):
            eng.wait_ge(tile_loaded[t % RING], at_turn(32 * (t // RING + 1), 32, i))

        block = ctx.enter_context(nc.Block())

        @block.sync
        def _(sp):
            sp.dma_start(X[:, 0, :], x[0, 0:P, :]).then_inc(ld_x, 16)
            sp.dma_start(ident, w["constants"][:, 0:P]).then_inc(ld_ident, 16)
            sp.dma_start(X[:, 1, :], x[0, P:SEQ, :]).then_inc(ld_x, 16)

            def row_loads(g, names):
                for name, src in names:
                    _, at, n = ROWS[name]
                    sp.dma_start(rowbuf[at:at + n, g, :], src).then_inc(ld_rows[g], 16)

            def rows_of(v):
                return v.rearrange("(k p) -> k p", p=P)

            sp.wait_ge(rows_zero, 1)
            row_loads(0, [("norm_mix", w["norm_mix"].rearrange("l (k p) -> (l k) p", p=P)),
                          ("norm_ffn", w["norm_ffn"].rearrange("l (k p) -> (l k) p", p=P)),
                          ("a_gain", rows_of(w["a_v_gain"][0])),
                          ("cvec", w["c_2"].rearrange("a (k p) -> (a k) p", p=P)),
                          ("mix_g", rows_of(w["mix_norm_g_2"][0])),
                          ("bcw", w["b_conv_w"][0].rearrange("t (k p) -> (t k) p", p=P))])

            def small_loads():
                fcw, fcb = w["f_conv_w"], w["f_conv_b"]
                sp.dma_start(const[:, P:], w["constants"][:, P:]).then_inc(ld_const, 16)
                sp.dma_start(ws_in, w["a_w_s"][0].rearrange("g t s -> t g s")).then_inc(ld_ws, 16)
                sp.dma_start(bsb, w["a_b_s"][0].partition_broadcast(P)).then_inc(ld_bs, 16)
                row_loads(1, [("fcw0_0", rows_of(fcw[0, 0])), ("fcw0_1", rows_of(fcw[0, 1])),
                              ("moe_g", rows_of(w["moe_norm_g_2"][0])), ("k_k", rows_of(w["rwkv_k_k_2"][0])),
                              ("k_a", rows_of(w["rwkv_k_a_2"][0])), ("w0", rows_of(w["rwkv_w0_2"][0])),
                              ("a0", rows_of(w["rwkv_a0_2"][0]))])
                row_loads(2, [("fcw0_2", rows_of(fcw[0, 2])), ("fcb0", rows_of(fcb[0])),
                              ("lam", rows_of(w["b_lambda"][0])), ("bcb", rows_of(w["b_conv_b"][0]))])
                row_loads(3, [("fcw1_0", rows_of(fcw[1, 0])), ("fcw1_1", rows_of(fcw[1, 1])),
                              ("bba", w["b_b_a"][0].rearrange("h (k p) -> (h k) p", p=P)),
                              ("bbx", w["b_b_x"][0].rearrange("h (k p) -> (h k) p", p=P))])
                mu = w["rwkv_mu_2"][0]
                row_loads(4, [("fcw1_2", rows_of(fcw[1, 2])), ("fcb1", rows_of(fcb[1])),
                              ("mu", rows_of(mu[0:14 * P])),
                              ("r_k", w["rwkv_r_k_2"][0].rearrange("(m h) n -> m (h n)", h=2)),
                              ("kv_g", rows_of(w["kv_norm_g_2"][0]))])
                at = ROWS["mu_tail"][1]
                sp.dma_start(rowbuf[at:at + 1, 4, 0:32], mu[14 * P:14 * P + 32].unsqueeze(0)).then_inc(ld_rows[4], 16)
                for name, src in (("q_g", w["q_norm_g_2"]), ("k_g", w["k_norm_g_2"])):
                    at = ROWS[name][1]
                    for h in range(2):
                        sp.dma_start(rowbuf[at:at + 1, 4, h * HD:(h + 1) * HD], src).then_inc(ld_rows[4], 16)
                for j in range(4):
                    sp.dma_start(adab[32 * j:32 * j + 1, :, :],
                                 w["ada_b_2"].rearrange("a (q j n) -> a j q n", j=4, n=512)[:, j]).then_inc(ld_adab, 16)

            def load(t, first, second, i=None):
                if t >= RING:
                    sp.wait_ge(tile_used, at_turn(t - RING + 1, RING, i))
                for dst, src in (first, second):
                    sp.dma_start(dst, src).then_inc(tile_loaded[t % RING], 16)

            def block_of(wt, k0, n0):
                v = wt.rearrange("(k p) n -> p k n", p=P)
                n = bass.ds(n0, 512)
                return v[:, k0:k0 + 4, n], v[:, k0 + 4:k0 + 8, n]

            def load_block(t, wt, k0, n0, i=None):
                s = ring[t % RING].rearrange("p (k n) -> p k n", n=512)
                a, b = block_of(wt, k0, n0)
                load(t, (s[:, 0:4, :], a), (s[:, 4:8, :], b), i)

            def load_ada(q):
                v = w["ada_w_2"][0].rearrange("(k p) n -> p k n", p=P)[:, :, 2048 * q:2048 * q + 2048]
                for j in range(4):
                    t = T["ada", q] + j
                    s = ring[t % RING].rearrange("p (k n) -> p k n", n=2048)
                    load(t, (s[:, 0, :], v[:, 2 * j, :]), (s[:, 1, :], v[:, 2 * j + 1, :]))

            def load_ffn(l):
                with sp.Fori(0, 3) as i:
                    for u in range(2):
                        for v in range(2):
                            load_block(T["up", l] + 2 * u + v, w["f_w_up"][l], 0,
                                       i * 1024 + (u * 512 + v * FF), i)
                for n in range(2):
                    for kk in range(3):
                        load_block(T["down", l] + 3 * n + kk, w["f_w_down"][l], 8 * kk, 512 * n)

            for j in range(4):
                load_block(T["av"] + j, w["a_w_in"][0], 0, A_W + 512 * j)
                if j == 1:
                    small_loads()
            for j in range(4):
                load_block(T["au"] + j, w["a_w_in"][0], 0, 512 * j)
            for n in range(2):
                for kh in range(2):
                    load_block(T["ao"] + 2 * n + kh, w["a_w_out"][0], 8 * kh, 512 * n)
            load_ada(0)
            load_ffn(0)
            load_ada(1)
            for j in range(3):
                load_block(T["bx"] + j, w["b_w_in"][0], 0, B_W + 512 * j)
            for j, wt in enumerate((w["b_w_a"][0], w["b_w_x"][0])):
                s = ring[(T["bgate"] + j) % RING][:, 0:12 * 256].rearrange("p (k e) -> p k e", e=256)
                v = wt.rearrange("h (k p) e -> p (h k) e", p=P)
                load(T["bgate"] + j, (s[:, 0:6, :], v[:, 0:6, :]), (s[:, 6:12, :], v[:, 6:12, :]))
            for j in range(3):
                load_block(T["bg"] + j, w["b_w_in"][0], 0, 512 * j)
            for n in range(2):
                load_block(T["bo"] + n, w["b_w_out"][0], 0, 512 * n)
            s = ring[(T["bo"] + 2) % RING].rearrange("p (k n) -> p k n", n=512)
            v = w["b_w_out"][0].rearrange("(k p) n -> p k n", p=P)
            load(T["bo"] + 2, (s[:, 0:4, :], v[:, 8:12, 0:512]), (s[:, 4:8, :], v[:, 8:12, 512:1024]))
            load_ada(2)
            load_ffn(1)
            wi2 = w["w_in_2"][0].rearrange("(k p) n -> p k n", p=P)
            at = {"q": 0, "kv": 512, "kw": 1024, "r": 1064, "lora": 1064 + 1536, "gate": 1064 + 1824}
            s = ring[T["lora"] % RING][:, 0:8 * 328].rearrange("p (k n) -> p k n", n=328)
            load(T["lora"], (s[:, :, 0:40], wi2[:, :, at["kw"]:at["kw"] + 40]),
                 (s[:, :, 40:328], wi2[:, :, at["lora"]:at["lora"] + 288]))
            for j, name in enumerate("rkv"):
                load_block(T[name], w["w_in_2"][0], 0, at["r"] + 512 * j)
            load_block(T["q"], w["w_in_2"][0], 0, at["q"])
            load_block(T["kv"], w["w_in_2"][0], 0, at["kv"])

            def load_wide(t, wt, K):
                s = ring[t % RING][:, 0:K * D].rearrange("p (k n) -> p k n", n=D)
                v = wt.rearrange("(k p) n -> p k n", p=P)
                load(t, (s[:, 0:K // 2, :], v[:, 0:K // 2, :]), (s[:, K // 2:K, :], v[:, K // 2:K, :]))

            for j in range(2):
                load_block(T["gate", j], w["w_in_2"][0], 0, at["gate"] + 512 * j)
            load_wide(T["kvup"], w["w_kv_up_2"][0], 2)
            for j in range(2, 4):
                load_block(T["gate", j], w["w_in_2"][0], 0, at["gate"] + 512 * j)
            load_wide(T["branch"], w["w_branch_attn_2"][0], 4)
            load_wide(T["branch"] + 1, w["w_branch_rwkv_2"][0], 4)
            for n in range(2):
                load_block(T["mo"] + n, w["w_out_2"][0], 0, 512 * n)
            eg = w["expert_w_gate_2"][0].rearrange("e (k p) n -> e p k n", p=P)
            eu = w["expert_w_up_2"][0].rearrange("e (k p) n -> e p k n", p=P)
            ed = w["expert_w_down_2"][0].rearrange("e (k p) n -> e p k n", p=P)
            xs = scratch["xs"].rearrange("(i s) n -> i s n", s=2 * SLOT)

            def load_expert(s, e):
                q = s % 3
                v = (eg, eu, ed)[q][e].rearrange("e p k n -> p (e k) n")
                dst = slots[s].rearrange("p (k n) -> p k n", n=512 if q < 2 else D)
                h = 4 if q < 2 else 2
                for part in (slice(0, h), slice(h, 2 * h)):
                    sp.dma_start(dst[:, part, :], v[:, part, :]).then_inc(e_w[s], 16)

            last_tile = T["mo"] + 1
            for s in sorted(range(6), key=lambda s: last_tile if s >= RING else last_tile - (last_tile - s) % RING):
                sp.wait_ge(tile_used, last_tile + 1 if s >= RING else last_tile + 1 - (last_tile - s) % RING)
                load_expert(s, bass.ds(s // 3, 1))
            sp.wait_ge(scattered, 64)
            sp.dma_start(xsl, xs[0:1].rearrange("i s n -> (i s) n")).then_inc(e_x, 16)
            sp.wait_ge(eid_ready, 1)
            more = nc.sync.value_load(eid[0:1, MAX_ITEMS + 1:MAX_ITEMS + 2], min_val=NE // 2 - 1,
                                      max_val=MAX_ITEMS // 2 - 1)
            with sp.Fori(0, more) as i:
                for u in range(2):
                    e = nc.sync.value_load(eid[0:1, bass.ds(i * 2 + (u + 2), 1)], min_val=0, max_val=NE - 1)
                    for q in range(3):
                        sp.wait_ge(expert_used, i * 6 + (3 * u + q + 1))
                        load_expert(3 * u + q, bass.ds(e, 1))
                        if (u, q) == (0, 0):
                            sp.dma_start(xsl, xs[bass.ds(i + 1, 1)].rearrange("i s n -> (i s) n")).then_inc(e_x, 16)
            for c in range(C):
                sp.wait_ge(fin_c, c + 1)
                sp.dma_start(out[0, c * P:(c + 1) * P, :], X[:, c, :]).then_inc(st_out, 16)
            sp.wait_ge(st_out, 32)

        @block.gpsimd
        def _(pool):
            step = Steps(pool, pool_steps)
            nc.gpsimd.memset(rowbuf, 0.0).then_inc(rows_zero, 1)
            for hf in range(2):
                for h in range(3 * hf, 3 * hf + 3):
                    wait_drained(pool, ("bi", h))
                    wait_drained(pool, ("bx", h))
                ms = slice(6 * hf, 6 * hf + 6)
                nc.gpsimd.tensor_tensor(It[:, ms, :], It[:, ms, :], xbT[:, ms, :], ALU.mult).then_inc(b_gated, 1)
            wait_drained(pool, ("rows", 4))
            pool.dma_start(wa2[0:HD, :], w["rwkv_w2_2"][0]).then_inc(ld_mx, 16)
            pool.dma_start(wa2[HD:P, :], w["rwkv_a2_2"][0]).then_inc(ld_mx, 16)
            pool.dma_start(g2[:, 0, :], w["rwkv_g2_2"][0, 0:P, :]).then_inc(ld_mx, 16)
            pool.dma_start(g2[0:32, 1, :], w["rwkv_g2_2"][0, P:P + 32, :]).then_inc(ld_mx, 16)
            pool.dma_start(lnw, w["rwkv_ln_w_2"][0].partition_broadcast(P)).then_inc(ld_ln, 16)
            pool.dma_start(lnb, w["rwkv_ln_b_2"][0].partition_broadcast(P)).then_inc(ld_ln, 16)
            pool.dma_start(rw[:, :, 0:NG],
                           w["router_group_w_2"][0].rearrange("(k p) n -> p k n", p=P)).then_inc(ld_route, 16)
            pool.dma_start(rw[:, :, NG:NG + NE],
                           w["router_expert_w_2"][0].rearrange("(k p) n -> p k n", p=P)).then_inc(ld_route, 16)
            pool.dma_start(rbias, w["router_expert_bias_2"][0].partition_broadcast(P)).then_inc(ld_route, 16)
            wait_drained(pool, ("bi", 0))
            nc.gpsimd.memset(gt1b, 0.0).then_inc(xs_zero, 1)
            pool.wait_ge(xs_zero, 1)
            for j in range(MAX_ITEMS * SLOT // P):
                pool.dma_start(scratch["xs"][j * P:(j + 1) * P, :], gt1b).then_inc(xs_cleared, 16)
            wait_drained(pool, ("ada", 2))
            mod = scratch["mod"]
            for j in range(4):
                pool.dma_start(mod.rearrange("(a q j n) -> a j q n", a=1, j=4, n=512)[:, j],
                               adab[32 * j:32 * j + 1, :, :]).then_inc(st_mod, 16)
            pool.wait_ge(st_mod, 64)
            pool.wait_ge(b_y, 2)
            pool.dma_start(gfb, w["norm_final"].partition_broadcast(P)).then_inc(ld_gfb, 16)
            pool.dma_start(rowbuf[0:16, 0, :], mod[0:2 * D].rearrange("(k p) -> k p", p=P)).then_inc(ld_mod, 16)
            pool.dma_start(rowbuf[16:32, 0, :], mod[3 * D:5 * D].rearrange("(k p) -> k p", p=P)).then_inc(ld_mod, 16)
            pool.wait_ge(xs_cleared, 16 * (MAX_ITEMS * SLOT // P))
            pool.dma_start(gt1b, mod[2 * D:3 * D].partition_broadcast(P)).then_inc(ld_gt1, 16)
            wait_drained(pool, ("kw", 0))
            for b in range(4):
                pool.dma_start(kirep[32 * b:32 * b + 32, :], kw_sb[0:32, :]).then_inc(ld_rep, 16)
            for c in range(C):
                S = (c + 1) * P
                pool.wait_ge(score_sum, c + 1)
                nc.gpsimd.affine_select(sc[:, c, 0:S], sc[:, c, 0:S], [[-1, S]], ALU.is_ge, -3e38, base=c * P,
                                        channel_multiplier=1).then_inc(score_masked, 1)
            for c in range(C):
                S = (c + 1) * P
                pool.wait_ge(neg_raw, c + 1)
                nc.gpsimd.affine_select(neg[:, c, 0:S], neg[:, c, 0:S], [[-1, S]], ALU.is_ge, FAR, base=c * P,
                                        channel_multiplier=1).then_inc(neg_ready, 1)
            for c in range(C):
                wait_drained(pool, ("vt", c))
            wait_full(pool, ("bonus", 0))
            pool.wait_ge(qr_ready, 1)
            nc.gpsimd.memset(MT, 0.0).then_inc(mt_clear, 1)
            for c in range(C):
                for lv in range(1, 8):
                    for hf in range(2):
                        hs = slice(4 * hf, 4 * hf + 4)
                        if lv == 1:
                            wait_drained(pool, ("mt", c, 4 * hf + 3))
                        if lv > 1 or c > 0:
                            wait_full(pool, ("t1", c, lv - 1, hf) if lv > 1 else ("t1", c - 1, 7, hf))
                        if lv == 2:
                            wait_drained(pool, ("t1", c, 1, hf))
                            pool.wait_ge(x_first, 2 * c + hf + 1)
                        mask = con("level")[:, (lv - 1) * P:lv * P].unsqueeze(1).to_broadcast([P, 4, P])
                        nc.gpsimd.tensor_tensor(CT[:, hs, :], MT[:, hs, 0:P], mask, ALU.mult).then_inc(ct_ready, 1)
            pool.wait_ge(merg, 4)
            pool.dma_start(gt2b, mod[5 * D:6 * D].partition_broadcast(P)).then_inc(ld_gt2, 16)
            pool.wait_ge(idx_ready, 1)
            for c in range(C):
                pool.wait_ge(xn_ready[c], 6)
            pool.wait_ge(xs_cleared, 16 * (MAX_ITEMS * SLOT // P))
            for j in range(2):
                for c in range(C):
                    nc.gpsimd.indirect_dma_start(
                        scratch["xs"], bass.IndirectOffsetOnAxis(ap=idx[:, 2 * j + c:2 * j + c + 1], axis=0),
                        xn[:, c, :], None).then_inc(scattered, 16)
            pool.wait_ge(y_copied, 1)
            for c in range(C):
                for j in range(2):
                    nc.gpsimd.indirect_dma_start(
                        yk[:, 2 * j + c, :], None, scratch["xs"],
                        bass.IndirectOffsetOnAxis(ap=idx[:, 2 * j + c:2 * j + c + 1], axis=0)).then_inc(gathered, 16)
                pool.wait_ge(gathered, 32 * (c + 1))

        @block.scalar
        def _(act):
            step = Steps(act, act_steps)
            def norm(n, ready, gain, bias=None, s=None, before_out=None):
                s = n if s is None else s
                ready(act)
                nc.scalar.activation(xn[:, 0, :], X[:, 0, :], ACT.Square, accum_out=ssq[:, 0:1]).then_inc(norm_sq, 1)
                act.wait_ge(norm_var, s + 1)
                nc.scalar.activation(std, var, ACT.Sqrt).then_inc(norm_std, 1)
                act.wait_ge(norm_rstd, s + 1)
                nc.scalar.activation(xn[:, 0, :], X[:, 0, :], ACT.Identity,
                                     scale=rstd[:, 0:1]).then_inc(xn_ready[0], 1)
                if before_out:
                    before_out()
                for b in (1, 3):
                    key = ("norm", n, b)
                    wait_full(act, key)
                    for kk in range(2):
                        last = nc.scalar.activation(hT[:, 2 * b + kk, :], bank(key)[:, kk * SEQ:(kk + 1) * SEQ],
                                                    ACT.Identity, scale=gain(2 * b + kk),
                                                    bias=bias(2 * b + kk) if bias else 0.0)
                    drains(last, key)

            def after(*keys):
                return lambda eng: [wait_drained(eng, k) for k in keys]

            def ffn(l):
                with act.Fori(0, 3) as i:
                    for q in range(4):
                        u, h = divmod(q, 2)
                        for key, first, signal, base in ((("gate", l, u, h), conv_g, conv_g0, 0),
                                                         (("val", l, u, h), conv_v, conv_v0, KF)):
                            wait_full(act, key, i)
                            for b in range(2):
                                m = i * 8 + (base + 2 * q + b)
                                last = nc.scalar.activation(
                                    first[:, q, b * SEQ:(b + 1) * SEQ], bank(key)[:, b * SEQ:(b + 1) * SEQ],
                                    ACT.Identity, scale=col_at(f"fcw{l}_2", m), bias=col_at(f"fcb{l}", m))
                            last.then_inc(signal, 1)
                        wait_drained(act, ("gate", l, u, h), i)
                        nc.scalar.activation(gelu_g[:, q, :], conv_g[:, q, :],
                                             ACT.Gelu_apprx_tanh).then_inc(gelu_done, 1)

            wait_drained(act, ("rows", 0))
            norm(0, lambda eng: eng.wait_ge(ld_x, 32), lambda k: col("norm_mix", k))
            for j in range(4):
                for c in range(C):
                    key = ("av", j, c)
                    wait_full(act, key)
                    drains(nc.scalar.activation(V[:, c, 512 * j:512 * j + 512], bank(key)[:, :],
                                                ACT.Gelu_apprx_tanh), key)
            for c in range(C):
                wait_drained(act, ("av", 3, c))
                if c:
                    act.wait_ge(v_sq, c)
                nc.scalar.activation(v_junk, V[:, c, :], ACT.Square, accum_out=vsq[:, c:c + 1]).then_inc(v_sq, 1)
            act.wait_ge(v_var, 1)
            nc.scalar.activation(vstd, vvar, ACT.Sqrt).then_inc(v_std, 1)
            nc.scalar.activation(sil, col("cvec", 0, 8), ACT.Silu).then_inc(silu_ready, 1)
            for j in range(4):
                for h in range(2):
                    key = ("au", j, h)
                    wait_full(act, key)
                    drains(nc.scalar.activation(uT[:, 4 * j + 2 * h:4 * j + 2 * h + 2, :],
                                                bank(key).rearrange("p (a t) -> p a t", a=2),
                                                ACT.Gelu_apprx_tanh), key)
            norm(1, after(("ao", 0, 0), ("ao", 1, 0)), lambda k: col("norm_ffn", k))
            ffn(0)
            norm(2, after(("down", 0, 0, 0), ("down", 0, 1, 0)), lambda k: col("norm_mix", 8 + k))
            act.wait_ge(lam_exp, 1)
            nc.scalar.activation(lamt[:, 1, :], lamt[:, 0, :], ACT.Exp).then_inc(lam_exp, 1)
            for q in range(6):
                key = ("bx", q)
                wait_full(act, key)
                for b in range(2):
                    m = 2 * q + b
                    last = nc.scalar.activation(xbT[:, m, :], bank(key)[:, b * SEQ:(b + 1) * SEQ], ACT.Identity,
                                                scale=col("bcw", 36 + m), bias=col("bcb", m))
                last.then_inc(bx0, 1)
            for h in range(B_H):
                for name, dst, bias in (("br", Rt, "bba"), ("bi", It, "bbx")):
                    key = (name, h)
                    wait_full(act, key)
                    for b in range(2):
                        last = nc.scalar.activation(dst[:, 2 * h + b, :], bank(key)[:, b * SEQ:(b + 1) * SEQ],
                                                    ACT.Sigmoid, bias=col(bias, 2 * h + b))
                    drains(last, key)
            for hf in range(2):
                ms = slice(6 * hf, 6 * hf + 6)
                act.wait_ge(b_log, hf + 1)
                nc.scalar.activation(At[:, ms, :], Rt[:, ms, :], ACT.Exp)
                nc.scalar.activation(Tt[:, ms, :], Rt[:, ms, :], ACT.Tanh, scale=-1.0).then_inc(b_exp, 1)
            for hf in range(2):
                ms = slice(6 * hf, 6 * hf + 6)
                act.wait_ge(b_m2, hf + 1)
                nc.scalar.activation(Tt[:, ms, :], Tt[:, ms, :], ACT.Sqrt).then_inc(b_mult, 1)
            for q in range(6):
                key = ("bg", q)
                wait_full(act, key)
                drains(nc.scalar.activation(Gt[:, 2 * q:2 * q + 2, :], bank(key).rearrange("p (a t) -> p a t", a=2),
                                            ACT.Gelu_apprx_tanh), key)
            norm(3, after(("bo", 0, 0), ("bo", 1, 0)), lambda k: col("norm_ffn", 8 + k))
            ffn(1)
            for n in range(2):
                wait_drained(act, ("down", 1, n, 0))
            nc.scalar.activation(xn[:, 0, :], X[:, 0, :], ACT.Square, accum_out=ssq[:, 0:1]).then_inc(norm_sq, 1)
            act.wait_ge(norm_var, 5)
            nc.scalar.activation(std, var, ACT.Sqrt).then_inc(norm_std, 1)
            norm(4, lambda eng: (eng.wait_ge(x_final, 1), eng.wait_ge(norm_sq, 5)), lambda k: gm1[:, k:k + 1], lambda k: col("sh1", k), s=5,
                 before_out=lambda: act.wait_ge(gm_ready, 3))
            wait_full(act, ("kw", 0))
            drains(nc.scalar.copy(kw_sb[0:40, :], banks[5][0:40, 0:SEQ]), ("kw", 0))
            for key, ms in ((("lora", 0), (12, 13)), (("lora", 1), (14,)), (("r", 0), (0, 1)), (("r", 1), (2, 3)),
                            (("k", 0), (4, 5)), (("k", 1), (6, 7)), (("v", 0), (8, 9)), (("v", 1), (10, 11))):
                wait_full(act, key)
                for b, m in enumerate(ms):
                    r = slice(0, 32 if m == 14 else P)
                    last = nc.scalar.activation(mix[r, m, :], bank(key)[r, b * SEQ:(b + 1) * SEQ], ACT.Identity,
                                                scale=omu[r, m:m + 1])
                last.then_inc(mix0, 1)
            for q in range(2):
                wait_drained(act, ("lora", q))
            nc.scalar.activation(mix[0:HD, 12, :], mix[0:HD, 12, :], ACT.Tanh).then_inc(lora_act, 1)
            nc.scalar.activation(mix[:, 13, :], mix[:, 13, :], ACT.Sigmoid).then_inc(lora_act, 1)
            nc.scalar.activation(mix[0:32, 14, :], mix[0:32, 14, :], ACT.Sigmoid).then_inc(lora_act, 1)
            for name, dst, bias in (("zw", sw, "w0"), ("za", aS, "a0")):
                for q in range(2):
                    key = (name, q)
                    wait_full(act, key)
                    for b in range(2):
                        m = 2 * q + b
                        last = nc.scalar.activation(dst[:, m, :], bank(key)[:, b * SEQ:(b + 1) * SEQ], ACT.Sigmoid,
                                                    bias=col(bias, m))
                    drains(last, key)
            for c in range(C):
                key = ("gg", c)
                wait_full(act, key)
                drains(nc.scalar.copy(gtok[:, c, :], bank(key)[:, :]), key)
            for c in range(C):
                wait_full(act, ("q", c))
                nc.scalar.activation(qn[:, c, :], bank(("q", c))[:, :], ACT.Square).then_inc(q_sq, 1)
            wait_full(act, ("kv", 0))
            for c in range(C):
                nc.scalar.activation(kvn[:, c, :], banks[6][:, c * SEQ:(c + 1) * SEQ], ACT.Square,
                                     accum_out=kvst[:, c:c + 1]).then_inc(q_sq, 1)
            wait_full(act, ("qi", 0))
            drains(nc.scalar.copy(qiT, banks[7].rearrange("p (a t) -> p a t", a=2)), ("qi", 0))
            act.wait_ge(cum_ready, 1)
            nc.scalar.activation(em, cum, ACT.Exp, scale=KAPPA).then_inc(exp_ready, 1)
            nc.scalar.activation(sw, sw, ACT.Exp, scale=-KAPPA).then_inc(exp_ready, 1)
            act.wait_ge(exp_ready, 1)
            nc.scalar.activation(cum, cum, ACT.Exp, scale=-KAPPA).then_inc(exp_ready, 1)
            nc.scalar.activation(dmid, cmid, ACT.Exp, scale=-KAPPA).then_inc(exp_ready, 1)
            act.wait_ge(q_var, 1)
            nc.scalar.activation(qst, qst, ACT.Sqrt).then_inc(q_root, 1)
            nc.scalar.activation(kvst, kvst, ACT.Sqrt).then_inc(q_root, 1)
            act.wait_ge(kx2, 1)
            for q in range(2):
                key = ("kn", q)
                wait_full(act, key)
                drains(nc.scalar.activation(sq[:, 2 * q:2 * q + 2, :], bank(key).rearrange("p (a t) -> p a t", a=2),
                                            ACT.Sqrt), key)
            def open_gates(j):
                for q in (2 * j, 2 * j + 1):
                    key = ("ga", q)
                    wait_full(act, key)
                    drains(nc.scalar.activation(gates[:, 2 * q:2 * q + 2, :],
                                                bank(key).rearrange("p (a t) -> p a t", a=2), ACT.Sigmoid), key)

            act.wait_ge(qr_ready, 1)
            open_gates(0)
            open_gates(1)
            wait_drained(act, ("qt", 0))
            wait_drained(act, ("qt", 1))
            for c in range(C):
                wait_full(act, ("kr", c))
                nc.scalar.activation(qn[:, c, :], bank(("kr", c))[:, :], ACT.Square).then_inc(k_sq, 1)
            for c in range(C):
                key = ("vr", c)
                wait_full(act, key)
                drains(nc.scalar.copy(Vt[:, c, :], bank(key)[:, :]), key)
            act.wait_ge(k_var, 1)
            nc.scalar.activation(kst, kst, ACT.Sqrt).then_inc(k_root, 1)
            for c in range(C):
                S = (c + 1) * P
                for b in range(4):
                    key = ("dot", c, b)
                    n = 4 * c + b
                    wait_full(act, key)
                    if n in (4, 5):
                        act.wait_ge(score_sum, 1) if n == 5 else act.wait_ge(rel_used, 3)
                    elif n >= 2:
                        act.wait_ge(rel_used, 3 * ((n - 2) // 4) + (n - 2) % 4 + 1)
                    drains(nc.scalar.activation(rel[:, n % 2, :].rearrange("p (a s) -> p a s", a=2)[:, :, 0:S],
                                         bank(key).rearrange("p (a s) -> p a s", a=2)[:, :, 0:S], ACT.Relu,
                                         scale=float(IHD ** -0.5 * IH ** -0.5)), key)
            open_gates(2)
            open_gates(3)
            for c in range(C):
                S = (c + 1) * P
                for g in range(4):
                    n = 4 * c + g
                    act.wait_ge(lg_ready, n + 1)
                    for j in range(2):
                        h = head_of(g, j)
                        last = nc.scalar.activation(Pb[:, n % 2, j, 0:S], Pb[:, n % 2, j, 0:S], ACT.Exp,
                                                    bias=nmax[:, 8 * c + h:8 * c + h + 1],
                                                    accum_out=psum_[:, 8 * c + h:8 * c + h + 1])
                        last.then_inc(p_ready, 1)
                    key = ("pt", c, g)
                    wait_full(act, key)
                    if n >= 2:
                        act.wait_ge(pv_used, n - 1)
                    w_ = 2 * (c + 1) * P
                    drains(nc.scalar.copy(pT[:, n % 2, 0:2 * (c + 1), :],
                                          bank(key)[:, 0:w_].rearrange("p (a t) -> p a t", t=P)), key)
            for q in range(2):
                key = ("oat", q)
                wait_full(act, key)
                drains(nc.scalar.copy(oaT[:, 2 * q:2 * q + 2, :], bank(key).rearrange("p (a t) -> p a t", a=2)), key)
            for c in range(C):
                key = ("vt", c)
                wait_full(act, key)
                drains(nc.scalar.copy(vtok[:, c, :], bank(key)[:, :]), key)
            for key, dst in ((("bt", 0), btok), (("ktt", 0), ktok)):
                wait_full(act, key)
                drains(nc.scalar.copy(dst, bank(key)[:, :]), key)
            wait_full(act, ("bonus", 0))
            drains(nc.scalar.copy(bonus, banks[2][:, 0:16]), ("bonus", 0))
            for c in range(C):
                for lv in range(2, 8):
                    for hf in range(2):
                        key = ("t1", c, lv, hf)
                        wait_full(act, key)
                        if lv > 2:
                            wait_full(act, ("xb", c, lv - 1, hf))
                        elif c > 0:
                            wait_full(act, ("xb", c - 1, 7, hf))
                        drains(nc.scalar.copy(T1[:, 4 * hf:4 * hf + 4, :],
                                              bank(key).rearrange("p (a t) -> p a t", a=4)), key)
                wait_full(act, ("sa", c))
                drains(nc.scalar.copy(satok[:, c, :], banks[0][:, :]), ("sa", c))
                for par in range(2):
                    key = ("y", c, par)
                    wait_full(act, key)
                    drains(nc.scalar.copy(ytok[:, c, :].rearrange("p (a h n) -> p h a n", h=2, n=HD)[:, par],
                                          bank(key)[:, 0:256].rearrange("p (a n) -> p a n", a=4)), key)
                act.wait_ge(gn_var, c + 1)
                nc.scalar.activation(gn_b, gn_b, ACT.Sqrt).then_inc(gn_root, 1)
            for q in range(2):
                key = ("ort", q)
                wait_full(act, key)
                drains(nc.scalar.copy(orT[:, 2 * q:2 * q + 2, :], bank(key).rearrange("p (a t) -> p a t", a=2)), key)
            norm(5, after(("mo", 0, 0), ("mo", 1, 0)), lambda k: gm2[:, k:k + 1], lambda k: col("sh2", k), s=6)
            act.wait_ge(ge_in, 1)
            nc.scalar.activation(gtmp[:, :, 0:NG], gtmp[:, :, 0:NG], ACT.Exp).then_inc(ge_exp, 1)
            act.wait_ge(two_in, 1)
            nc.scalar.activation(rsm[:, 4:6], rsm[:, 4:6], ACT.Exp).then_inc(two_exp, 1)
            for u in range(2):
                nc.scalar.sem_inc(st_y[u], 32)
            act.wait_ge(eid_ready, 1)
            pairs = nc.scalar.value_load(eid[0:1, MAX_ITEMS:MAX_ITEMS + 1], min_val=NE // 2, max_val=MAX_ITEMS // 2)
            ys = scratch["xs"].rearrange("(i s) n -> i s n", s=SLOT)
            with act.Fori(0, pairs) as i:
                for u in range(2):
                    act.wait_ge(expert_used, i * 6 + (3 * u + 1))
                    nc.scalar.activation(sg[:, u, :], banks[2][:, 0:256], ACT.Silu).then_inc(sg_ready, 1)
                    act.wait_ge(ht_full, i * 2 + (u + 1))
                    nc.scalar.copy(hTe[:, u, :], banks[4 + u][:, 0:256]).then_inc(ht_ready, 1)
                    act.wait_ge(expert_used, i * 6 + (3 * u + 3))
                    act.wait_ge(st_y[u], i * 32 + 32)
                    nc.scalar.copy(ysb[:, u, :], banks[6 + u][:, :]).then_inc(y_sb, 1)
                    act.wait_ge(y_sb, i * 2 + (u + 1))
                    for n in range(2):
                        act.dma_start(ys[bass.ds(i * 2 + u, 1), :, 512 * n:512 * n + 512].rearrange("i s n -> (i s) n"),
                                      ysb[n * SLOT:(n + 1) * SLOT, u, :]).then_inc(st_y[u], 16)
            for u in range(2):
                act.wait_ge(st_y[u], pairs * 32 + 32)
            nc.scalar.sem_inc(y_copied, 1)

        @block.vector
        def _(dve):
            step = Steps(dve, dve_steps)

            def norm(n, ready, gain, bias=None, s=None, before_out=None):
                s = n if s is None else s
                ready(dve)
                step(nc.vector.tensor_tensor_reduce(xn[:, 1, :], X[:, 1, :], X[:, 1, :], 1.0, 0.0, ALU.mult, ALU.add,
                                                    ssq[:, 1:2]))
                step.join()
                dve.wait_ge(norm_sq, s + 1)
                nc.vector.tensor_scalar(var, ssq, 1.0 / D, EPS, ALU.mult, ALU.add).then_inc(norm_var, 1)
                dve.wait_ge(norm_std, s + 1)
                nc.vector.reciprocal(rstd, std).then_inc(norm_rstd, 1)
                dve.wait_ge(norm_rstd, s + 1)
                nc.vector.tensor_scalar(xn[:, 1, :], X[:, 1, :], rstd[:, 1:2], None, ALU.mult).then_inc(xn_ready[1], 1)
                if before_out:
                    before_out()
                for b in (0, 2):
                    key = ("norm", n, b)
                    wait_full(dve, key)
                    for kk in range(2):
                        dst, src = hT[:, 2 * b + kk, :], bank(key)[:, kk * SEQ:(kk + 1) * SEQ]
                        k = 2 * b + kk
                        if bias:
                            last = nc.vector.tensor_scalar(dst, src, gain(k), bias(k), ALU.mult, ALU.add)
                        else:
                            last = nc.vector.tensor_scalar(dst, src, gain(k), None, ALU.mult)
                    drains(last, key)

            def after(*keys):
                return lambda eng: [wait_drained(eng, k) for k in keys]

            def add_to_x(keys):
                for (n, c), key in keys:
                    wait_full(dve, key)
                    xs = X[:, c, 512 * n:512 * n + 512]
                    drains(nc.vector.tensor_tensor(xs, bank(key)[:, :], xs, ALU.add), key)

            def ada(q):
                key = ("ada", q)
                wait_full(dve, key)
                if q == 0:
                    dve.wait_ge(ld_adab, 64)
                for j in range(4):
                    r = slice(32 * j, 32 * j + 1)
                    last = nc.vector.tensor_tensor(adab[r, q, :], bank(key)[r, :], adab[r, q, :], ALU.add)
                drains(last, key)

            def ffn(l):
                with dve.Fori(0, 3) as i:
                    step.enter(i, 24)
                    for q in range(4):
                        u, h = divmod(q, 2)
                        for name, y, signal, base in (("gate", conv_g, conv_g0, 0), ("val", conv_v, conv_v0, KF)):
                            key = (name, l, u, h)
                            dve.wait_ge(signal, at_turn(12 * l + q + 1, 4, i))
                            for tap in (1, 0):
                                sh = 2 - tap
                                for b in range(2):
                                    m = i * 8 + (base + 2 * q + b)
                                    to = y[:, q, b * SEQ + sh:(b + 1) * SEQ]
                                    last = nc.vector.scalar_tensor_tensor(
                                        to, bank(key)[:, b * SEQ:(b + 1) * SEQ - sh], col_at(f"fcw{l}_{tap}", m), to,
                                        ALU.mult, ALU.add)
                                    if (tap, b) == (0, 1):
                                        drains(last, key)
                                    else:
                                        step(last)
                                if tap == 1:
                                    step.join()
                        dve.wait_ge(gelu_done, at_turn(12 * l + q + 1, 4, i))
                        wait_drained(dve, ("val", l, u, h), i)
                        nc.vector.tensor_tensor(ffT[:, bass.ds(i * 8 + 2 * q, 2), :],
                                                gelu_g[:, q, :].rearrange("p (a t) -> p a t", a=2),
                                                conv_v[:, q, :].rearrange("p (a t) -> p a t", a=2),
                                                ALU.mult).then_inc(ff_ready, 1)
                    step.leave(3)
                add_to_x([((n, c), ("down", l, n, c)) for n in range(2) for c in range(C)])

            def rows_to_cols(g):
                key = ("rows", g)
                wait_full(dve, key)
                drains(nc.vector.tensor_copy(cols[:, g * P:(g + 1) * P], bank(key)[:, 0:P]), key)

            rows_to_cols(0)
            wait_drained(dve, ("rows", 0))
            norm(0, lambda eng: eng.wait_ge(ld_x, 32), lambda k: col("norm_mix", k))
            dve.wait_ge(v_sq, 2)
            nc.vector.tensor_scalar(vvar, vsq, 1.0 / A_W, EPS, ALU.mult, ALU.add).then_inc(v_var, 1)
            dve.wait_ge(v_std, 1)
            step(nc.vector.reciprocal(vrstd, vstd))
            for g in range(1, 5):
                rows_to_cols(g)
            dve.wait_ge(ld_const, 16)
            keep = con("keep")[:, P:2 * P].unsqueeze(1).to_broadcast([P, 4, P])
            for q in range(2):
                key = ("ws", q)
                wait_full(dve, key)
                drains(nc.vector.tensor_tensor(wsT[:, q * 512:(q + 1) * 512].rearrange("p (g t) -> p g t", g=4),
                                               bank(key).rearrange("p (g t) -> p g t", g=4), keep, ALU.mult), key)
            step.join()
            for q in range(2):
                wait_drained(dve, ("ws", q))
            for c in range(C):
                nc.vector.tensor_scalar(wsr[:, c, :], wsT, vrstd[:, c:c + 1], None, ALU.mult).then_inc(ws_scaled, 1)
            dve.wait_ge(ld_bs, 16)
            for m in range(16):
                key = ("sv", m // 2)
                if m % 2 == 0:
                    wait_full(dve, key)
                    if m >= 4:
                        dve.wait_ge(y_ready, m // 2 - 1)
                ins = nc.vector.scalar_tensor_tensor(
                    sv_tmp[:, m % 4, :].rearrange("p (c t) -> p c t", c=C),
                    bank(key)[:, (m % 2) * SEQ:(m % 2 + 1) * SEQ].rearrange("p (c t) -> p c t", c=C),
                    col("a_gain", m), bsb[:, m // 2, :].unsqueeze(1).to_broadcast([P, C, P]), ALU.mult, ALU.add)
                if m % 2:
                    drains(ins, key)
                else:
                    step(ins)
                if m % 2:
                    step.join()
                    wait_drained(dve, key)
                    if m % 4 == 1:
                        wait_drained(dve, ("au", m // 4, 0))
                    else:
                        wait_drained(dve, ("au", m // 4, 1))
                    nc.vector.tensor_tensor(uT[:, m - 1:m + 1, :], sv_tmp[:, m % 4 - 1:m % 4 + 1, :], uT[:, m - 1:m + 1, :],
                                            ALU.mult).then_inc(y_ready, 1)
            add_to_x([((n, c), ("ao", n, c)) for n in range(2) for c in range(C)])
            norm(1, after(("ao", 0, 1), ("ao", 1, 1)), lambda k: col("norm_ffn", k), before_out=lambda: ada(0))
            ffn(0)
            norm(2, after(("down", 0, 0, 1), ("down", 0, 1, 1)), lambda k: col("norm_mix", 8 + k), before_out=lambda: ada(1))
            lam = col("lam", 0, KB)
            step(nc.vector.tensor_scalar(lamt[:, 0, :], lam, -1.0, None, ALU.mult))
            step.join()
            nc.vector.tensor_tensor(lamt[:, 0, :], lamt[:, 0, :], lam, ALU.min).then_inc(lam_exp, 1)
            dve.wait_ge(lam_exp, 2)
            step(nc.vector.tensor_scalar(lamt[:, 2, :], lamt[:, 1, :], 2.0, None, ALU.add))
            step.join()
            step(nc.vector.reciprocal(lamt[:, 2, :], lamt[:, 2, :]))
            step.join()
            step(nc.vector.tensor_tensor(lamt[:, 1, :], lamt[:, 1, :], lamt[:, 2, :], ALU.mult))
            step.join()
            step(nc.vector.tensor_tensor(lamt[:, 2, :], lamt[:, 1, :], lamt[:, 1, :], ALU.mult))
            step(nc.vector.memset(lamt[:, 3, :], 1.0 / 17))
            for j in range(7, -1, -1):
                step.join()
                step(nc.vector.tensor_tensor(lamt[:, 3, :], lamt[:, 3, :], lamt[:, 2, :], ALU.mult))
                step.join()
                step(nc.vector.tensor_scalar(lamt[:, 3, :], lamt[:, 3, :], 1.0 / (2 * j + 1), None, ALU.add))
            step(nc.vector.tensor_scalar(lamt[:, 0, :], lam, 0.0, 8.0, ALU.min, ALU.mult))
            step.join()
            step(nc.vector.tensor_tensor(lamt[:, 3, :], lamt[:, 3, :], lamt[:, 1, :], ALU.mult))
            step.join()
            step(nc.vector.scalar_tensor_tensor(s8, lamt[:, 3, :], -16.0, lamt[:, 0, :], ALU.mult, ALU.add))
            step.join()
            for q in range(6):
                key = ("bx", q)
                dve.wait_ge(bx0, q + 1)
                for tap in (2, 1, 0):
                    sh = 3 - tap
                    for b in range(2):
                        m = 2 * q + b
                        to = xbT[:, m, sh:SEQ]
                        last = nc.vector.scalar_tensor_tensor(to, bank(key)[:, b * SEQ:(b + 1) * SEQ - sh],
                                                              col("bcw", 12 * tap + m), to, ALU.mult, ALU.add)
                        if (tap, b) == (0, 1):
                            drains(last, key)
                        else:
                            step(last)
                    if tap:
                        step.join()
            for h in range(B_H):
                wait_drained(dve, ("br", h))
                for b in range(2):
                    m = 2 * h + b
                    last = nc.vector.tensor_scalar(Rt[:, m, :], Rt[:, m, :], s8[:, m:m + 1], None, ALU.mult)
                if h % 3 == 2:
                    last.then_inc(b_log, 1)
            for hf in range(2):
                ms = slice(6 * hf, 6 * hf + 6)
                dve.wait_ge(b_exp, hf + 1)
                step(nc.vector.tensor_tensor(Gt[:, ms, :], At[:, ms, :], At[:, ms, :], ALU.mult))
                step.join()
                nc.vector.scalar_tensor_tensor(Tt[:, ms, :], Gt[:, ms, :], 1.0, Tt[:, ms, :], ALU.add,
                                               ALU.mult).then_inc(b_m2, 1)
            for hf in range(2):
                ms = slice(6 * hf, 6 * hf + 6)
                dve.wait_ge(b_mult, hf + 1)
                dve.wait_ge(b_gated, hf + 1)
                step(nc.vector.tensor_tensor(It[:, ms, :], It[:, ms, :], Tt[:, ms, :], ALU.mult))
                step.join()
                for m in range(6 * hf, 6 * hf + 6):
                    step(nc.vector.tensor_tensor_scan(Rt[:, m, :], At[:, m, :], It[:, m, :], 0.0, ALU.mult, ALU.add))
                step.join()
                for q in range(3 * hf, 3 * hf + 3):
                    wait_drained(dve, ("bg", q))
                nc.vector.tensor_tensor(Rt[:, ms, :], Rt[:, ms, :], Gt[:, ms, :], ALU.mult).then_inc(b_y, 1)
            add_to_x([((n, c), ("bo", n, c)) for n in range(2) for c in range(C)])
            norm(3, after(("bo", 0, 1), ("bo", 1, 1)), lambda k: col("norm_ffn", 8 + k), before_out=lambda: ada(2))
            ffn(1)
            key = ("rows", 5)
            for n in range(2):
                wait_drained(dve, ("down", 1, n, 1))
            step(nc.vector.tensor_tensor_reduce(xn[:, 1, :], X[:, 1, :], X[:, 1, :], 1.0, 0.0, ALU.mult, ALU.add,
                                                ssq[:, 1:2]))
            step.join()
            dve.wait_ge(norm_sq, 5)
            nc.vector.tensor_scalar(var, ssq, 1.0 / D, EPS, ALU.mult, ALU.add).then_inc(norm_var, 1)
            dve.wait_ge(norm_std, 5)
            nc.vector.reciprocal(rstd, std).then_inc(norm_rstd, 1)
            dve.wait_ge(norm_rstd, 5)
            dve.wait_ge(ld_gfb, 16)
            for c in range(C):
                for n in range(2):
                    wait_drained(dve, ("down", 1, n, c))
                nc.vector.scalar_tensor_tensor(X[:, c, :], X[:, c, :], rstd[:, c:c + 1], gfb, ALU.mult,
                                               ALU.mult).then_inc(x_final, 1)
            wait_full(dve, key)
            drains(nc.vector.tensor_copy(cols[:, 5 * P:5 * P + 32], bank(key)[:, 0:32]), key)
            wait_drained(dve, key)
            nc.vector.scalar_tensor_tensor(gm1, col("sc1", 0, 8), 1.0, col("mix_g", 0, 8), ALU.add,
                                           ALU.mult).then_inc(gm_ready, 1)
            nc.vector.scalar_tensor_tensor(gm2, col("sc2", 0, 8), 1.0, col("moe_g", 0, 8), ALU.add,
                                           ALU.mult).then_inc(gm_ready, 1)
            nc.vector.tensor_scalar(omu, col("mu", 0, 15), -1.0, 1.0, ALU.mult, ALU.add).then_inc(gm_ready, 1)
            dve.wait_ge(gm_ready, 3)
            norm(4, lambda eng: eng.wait_ge(x_final, 2), lambda k: gm1[:, k:k + 1], lambda k: col("sh1", k), s=5)
            for n, (key, ms) in enumerate(((("lora", 0), (12, 13)), (("lora", 1), (14,)), (("r", 0), (0, 1)),
                                           (("r", 1), (2, 3)), (("k", 0), (4, 5)), (("k", 1), (6, 7)),
                                           (("v", 0), (8, 9)), (("v", 1), (10, 11)))):
                dve.wait_ge(mix0, n + 1)
                for b, m in enumerate(ms):
                    r = slice(0, 32 if m == 14 else P)
                    last = nc.vector.scalar_tensor_tensor(mix[r, m, 1:SEQ], bank(key)[r, b * SEQ:(b + 1) * SEQ - 1],
                                                          col("mu", m)[r], mix[r, m, 1:SEQ], ALU.mult, ALU.add)
                drains(last, key)
            step(nc.vector.memset(rkbd, 0.0))
            step(nc.vector.tensor_scalar(gq8, col("q_g"), HD ** -0.5, None, ALU.mult))
            step.join()
            for h in range(2):
                step(nc.vector.tensor_copy(rkbd[h * HD:(h + 1) * HD, :, h], col("r_k", 0, 4)[h * HD:(h + 1) * HD]))
            for q in range(2):
                wait_drained(dve, ("k", q))
            for m in range(4):
                step(nc.vector.tensor_scalar(kx[:, m, :], mix[:, 4 + m, :], col("k_k", m), None, ALU.mult))
            step.join()
            nc.vector.tensor_tensor(sq, kx, kx, ALU.mult).then_inc(kx2, 1)
            for q in range(2):
                wait_drained(dve, ("zw", q))
            for m in range(4):
                for c in range(C):
                    t = slice(c * P, (c + 1) * P)
                    step(nc.vector.tensor_tensor_scan(cum[:, m, t], con("ones"), sw[:, m, t], 0.0, ALU.mult, ALU.add))
            step.join()
            cum8 = cum.rearrange("p m (c t) -> p (m c) t", c=C)
            step(nc.vector.tensor_copy(cmid, cum8[:, :, P // 2 - 1]))
            step.join()
            step(nc.vector.tensor_tensor(cum8, cum8, cmid.unsqueeze(2).to_broadcast([P, 8, P]), ALU.subtract))
            step.join()
            nc.vector.tensor_tensor(sw, cum, sw, ALU.subtract).then_inc(cum_ready, 1)
            for q in range(2):
                wait_drained(dve, ("za", q))
            for m in range(4):
                step(nc.vector.tensor_scalar(Kh[:, m, :], aS[:, m, :], -1.0, col("k_a", m), ALU.add, ALU.mult))
            step.join()
            step(nc.vector.scalar_tensor_tensor(mix[:, 4:8, :], Kh, 1.0, mix[:, 4:8, :], ALU.add, ALU.mult))
            dve.wait_ge(q_sq, 4)
            step(nc.vector.tensor_reduce(qst, qn.rearrange("p c (h n) -> p (c h) n", n=HD), AX.X, ALU.add))
            step(nc.vector.tensor_scalar(kvst, kvst, 1.0 / 256, EPS, ALU.mult, ALU.add))
            step.join()
            nc.vector.tensor_scalar(qst, qst, 1.0 / HD, EPS, ALU.mult, ALU.add).then_inc(q_var, 1)
            dve.wait_ge(q_root, 2)
            step(nc.vector.reciprocal(qst, qst))
            step(nc.vector.reciprocal(kvst, kvst))
            step.join()
            for c in range(C):
                key = ("q", c)
                drains(nc.vector.tensor_tensor(qn[:, c, :].rearrange("p (h n) -> p h n", n=HD),
                                               bank(key).rearrange("p (h n) -> p h n", n=HD),
                                               qst[:, 8 * c:8 * c + 8].unsqueeze(2).to_broadcast([P, 8, HD]), ALU.mult), key)
            for c in range(C):
                ins = nc.vector.tensor_scalar(kvn[:, c, :], banks[6][:, c * SEQ:(c + 1) * SEQ], kvst[:, c:c + 1], None,
                                              ALU.mult)
                if c:
                    drains(ins, ("kv", 0))
            for q in range(2):
                wait_drained(dve, ("kn", q))
            step(nc.vector.tensor_scalar(sq, sq, 1e-12, None, ALU.max))
            step.join()
            step(nc.vector.reciprocal(sq, sq))
            step.join()
            step(nc.vector.tensor_tensor(kx, kx, sq, ALU.mult))
            step.join()
            step(nc.vector.tensor_tensor(aS, aS, kx, ALU.mult))
            dve.wait_ge(exp_ready, 4)
            QRv = QR.rearrange("p (m c) a t -> p a m c t", c=C)
            v3 = lambda a: a.rearrange("p m (c t) -> p m c t", c=C)
            q8 = lambda a: a.rearrange("p m (c t) -> p (m c) t", c=C)
            step(nc.vector.tensor_copy(epc, q8(cum)[:, :, P - 1]))
            step(nc.vector.tensor_tensor(QR[:, :, 0, :], q8(kx), q8(sw), ALU.mult))
            step(nc.vector.tensor_tensor(QR[:, :, 1, :], q8(mix[:, 0:4, :]), q8(cum), ALU.mult))
            step.join()
            step(nc.vector.tensor_tensor(aS, aS, em, ALU.mult))
            step(nc.vector.tensor_tensor(Kh, mix[:, 4:8, :], em, ALU.mult))
            nc.vector.tensor_tensor(sq, mix[:, 0:4, :], mix[:, 4:8, :], ALU.mult).then_inc(qr_ready, 1)
            for q in range(2):
                key = ("qt", q)
                wait_full(dve, key)
                drains(nc.vector.tensor_scalar(qT[:, 2 * q:2 * q + 2, :], bank(key).rearrange("p (a t) -> p a t", a=2),
                                               gq8, None, ALU.mult), key)
            key = ("kvt", 0)
            wait_full(dve, key)
            for k in range(2):
                last = nc.vector.tensor_scalar(kvnT[:, k, :], bank(key)[:, k * SEQ:(k + 1) * SEQ], col("kv_g", k), None,
                                               ALU.mult)
            drains(last, key)
            dve.wait_ge(k_sq, 2)
            step(nc.vector.tensor_reduce(kst, qn.rearrange("p c (h n) -> p (c h) n", n=HD), AX.X, ALU.add))
            step.join()
            nc.vector.tensor_scalar(kst, kst, 1.0 / HD, EPS, ALU.mult, ALU.add).then_inc(k_var, 1)
            dve.wait_ge(k_root, 1)
            step(nc.vector.reciprocal(kst, kst))
            step.join()
            for c in range(C):
                key = ("kr", c)
                drains(nc.vector.tensor_tensor(qn[:, c, :].rearrange("p (h n) -> p h n", n=HD),
                                               bank(key).rearrange("p (h n) -> p h n", n=HD),
                                               kst[:, 8 * c:8 * c + 8].unsqueeze(2).to_broadcast([P, 8, HD]), ALU.mult), key)
            key = ("wi", 0)
            wait_full(dve, key)
            drains(nc.vector.tensor_copy(wi, bank(key)[:, 0:16]), key)
            wait_drained(dve, key)
            for c in range(C):
                S = (c + 1) * P
                for b in range(4):
                    n = 4 * c + b
                    wait_drained(dve, ("dot", c, b))
                    for j in range(2):
                        h = b + 4 * j
                        src = rel[:, n % 2, j * SEQ:j * SEQ + S]
                        wih = wi[:, 8 * c + h:8 * c + h + 1]
                        if (b, j) == (0, 0):
                            ins = nc.vector.tensor_scalar(sc[:, c, 0:S], src, wih, None, ALU.mult)
                        else:
                            ins = nc.vector.scalar_tensor_tensor(sc[:, c, 0:S], src, wih, sc[:, c, 0:S], ALU.mult,
                                                                 ALU.add)
                        if (b, j) == (3, 1):
                            ins.then_inc(score_sum, 1)
                            dve.wait_ge(score_sum, c + 1)
                        elif j == 0:
                            step(ins)
                            step.join()
                        else:
                            ins.then_inc(rel_used, 1)
                            dve.wait_ge(rel_used, 3 * c + b + 1)
            for q in range(2):
                key = ("kt", q)
                wait_full(dve, key)
                drains(nc.vector.tensor_scalar(kT[:, 2 * q:2 * q + 2, :], bank(key).rearrange("p (a t) -> p a t", a=2),
                                               col("k_g"), None, ALU.mult), key)
            for c in range(C):
                S = (c + 1) * P
                dve.wait_ge(score_masked, c + 1)
                for r in range(TOPK // 8):
                    src = (sc if r == 0 else work)[:, c, 0:S]
                    step(nc.vector.max(m8[:, 0:8], src))
                    step.join()
                    step(nc.vector.match_replace(work[:, c, 0:S], m8[:, 0:8], src, -3.4e38))
                    step.join()
                step(nc.vector.tensor_scalar(neg[:, c, 0:S], work[:, c, 0:S], -3.2e38, None, ALU.is_lt))
                step.join()
                nc.vector.tensor_scalar(neg[:, c, 0:S], neg[:, c, 0:S], -1.0, -FAR, ALU.add,
                                        ALU.mult).then_inc(neg_raw, 1)
            for c in range(C):
                S = (c + 1) * P
                dve.wait_ge(neg_ready, c + 1)
                for g in range(4):
                    n = 4 * c + g
                    key = ("lg", c, g)
                    wait_full(dve, key)
                    if n >= 2:
                        wait_full(dve, ("pt", (n - 2) // 4, (n - 2) % 4))
                    for j in range(2):
                        h = head_of(g, j)
                        slope = 2.0 ** (-8.0 * (h + 1) / AH)
                        ins = nc.vector.scalar_tensor_tensor(Pb[:, n % 2, j, 0:S], con("dist")[:, c * SEQ:c * SEQ + S],
                                                             -slope, bank(key)[:, j * SEQ:j * SEQ + S], ALU.mult,
                                                             ALU.add)
                        if j:
                            drains(ins, key)
                        else:
                            step(ins)
                    step.join()
                    wait_drained(dve, key)
                    for j in range(2):
                        h = head_of(g, j)
                        at = 8 * c + h
                        step(nc.vector.tensor_tensor_reduce(Pb[:, n % 2, j, 0:S], Pb[:, n % 2, j, 0:S], neg[:, c, 0:S],
                                                            1.0, -3.3e38, ALU.add, ALU.max, nmax[:, at:at + 1]))
                    step.join()
                    for j in range(2):
                        at = 8 * c + head_of(g, j)
                        ins = nc.vector.tensor_scalar(nmax[:, at:at + 1], nmax[:, at:at + 1], -1.0, None, ALU.mult)
                        if j:
                            ins.then_inc(lg_ready, 1)
                        else:
                            step(ins)
            dve.wait_ge(p_ready, 16)
            step(nc.vector.reciprocal(prec, psum_))
            step.join()
            for c in range(C):
                key = ("o", c)
                wait_full(dve, key)
                drains(nc.vector.tensor_tensor(otok[:, c, :].rearrange("p (h n) -> p h n", n=HD),
                                               bank(key).rearrange("p (h n) -> p h n", n=HD),
                                               prec[:, 8 * c:8 * c + 8].unsqueeze(2).to_broadcast([P, 8, HD]), ALU.mult), key)
            dve.wait_ge(mt_clear, 1)
            keep_u = con("keep").bitcast(U32)
            id4 = ident.unsqueeze(1).to_broadcast([P, 4, P])
            for c in range(C):
                for h in range(8):
                    key = ("mt", c, h)
                    wait_full(dve, key)
                    drains(nc.vector.copy_predicated(MT[:, h, :], keep_u, bank(key)[:, :]), key)
                for hf in range(2):
                    hs = slice(4 * hf, 4 * hf + 4)
                    key = ("t1", c, 1, hf)
                    wait_full(dve, key)
                    drains(nc.vector.tensor_tensor(Xm[:, hs, :], id4, bank(key).rearrange("p (a t) -> p a t", a=4),
                                                   ALU.subtract), key)
                    nc.vector.tensor_tensor(XT[:, c, hs, :], id4, CT[:, hs, :], ALU.subtract).then_inc(x_first, 1)
                for lv in range(2, 8):
                    for hf in range(2):
                        hs = slice(4 * hf, 4 * hf + 4)
                        for name, dst in (("xa", Xm[:, hs, :]), ("xb", XT[:, c, hs, :])):
                            if lv == 7 and name == "xa":
                                continue
                            key = (name, c, lv, hf)
                            wait_full(dve, key)
                            if lv == 2:
                                dve.wait_ge(x_first, 2 * c + hf + 1)
                                wait_drained(dve, ("t1", c, 1, hf))
                            else:
                                wait_drained(dve, (name, c, lv - 1, hf))
                            drains(nc.vector.tensor_tensor(dst, dst, bank(key).rearrange("p (a t) -> p a t", a=4),
                                                           ALU.subtract), key)
                for par in range(2):
                    key = ("rh", c, par)
                    wait_full(dve, key)
                    drains(nc.vector.tensor_scalar(rhtok.rearrange("p (a h n) -> p h a n", h=2, n=HD)[:, par],
                                                   bank(key)[:, 0:256].rearrange("p (a n) -> p a n", a=4), -1.0, None,
                                                   ALU.mult), key)
                if c == 0:
                    key = ("z", 0)
                    wait_full(dve, key)
                    for m in range(4):
                        ins = nc.vector.tensor_scalar(zst[:, m, :], banks[4][:, m * HD:(m + 1) * HD],
                                                      epc[:, 2 * m:2 * m + 1], dmid[:, 2 * m + 1:2 * m + 2], ALU.mult,
                                                      ALU.mult)
                    drains(ins, key)
                for par in range(2):
                    wait_drained(dve, ("y", c, par))
                Y = ytok[:, c, :]
                Y8 = Y.rearrange("p (h n) -> p h n", n=HD)
                V8 = vtok[:, c, :].rearrange("p (h n) -> p h n", n=HD)
                R8 = rhtok.rearrange("p (h n) -> p h n", n=HD)
                spread = lambda a: a.unsqueeze(2).to_broadcast([P, 8, HD])
                step(nc.vector.tensor_reduce(gn_a, Y8, AX.X, ALU.add))
                step.join()
                step(nc.vector.tensor_scalar(gn_a, gn_a, 1.0 / HD, None, ALU.mult))
                step.join()
                step(nc.vector.tensor_tensor(Y8, Y8, spread(gn_a), ALU.subtract))
                step.join()
                wait_full(dve, ("sa", c))
                step(nc.vector.tensor_tensor(rhtok, Y, Y, ALU.mult))
                step.join()
                step(nc.vector.tensor_reduce(gn_b, R8, AX.X, ALU.add))
                step.join()
                nc.vector.tensor_scalar(gn_b, gn_b, 1.0 / HD, 64e-5, ALU.mult, ALU.add).then_inc(gn_var, 1)
                dve.wait_ge(gn_root, c + 1)
                step(nc.vector.reciprocal(gn_a, gn_b))
                step.join()
                step(nc.vector.tensor_tensor(Y8, Y8, spread(gn_a), ALU.mult))
                wait_drained(dve, ("bonus", 0))
                step(nc.vector.tensor_tensor(R8, V8, spread(bonus.rearrange("p (c h) -> p c h", c=C)[:, c]), ALU.mult))
                step.join()
                dve.wait_ge(ld_ln, 32)
                step(nc.vector.tensor_tensor(Y, Y, lnw, ALU.mult))
                step(nc.vector.tensor_tensor(rhtok, rhtok, lnb, ALU.add))
                step.join()
                step(nc.vector.tensor_tensor(Y, Y, rhtok, ALU.add))
                step.join()
                nc.vector.tensor_tensor(Y, Y, gtok[:, c, :], ALU.mult).then_inc(or_rows, 1)
            for b in range(2):
                for q in range(4):
                    key = ("br", b, q)
                    wait_full(dve, key)
                    g = gates[:, 8 * b + 2 * q:8 * b + 2 * q + 2, :]
                    drains(nc.vector.tensor_tensor(g, bank(key).rearrange("p (a t) -> p a t", a=2), g, ALU.mult), key)
                    if b:
                        wait_drained(dve, key)
                        wait_drained(dve, ("br", 0, q))
                        nc.vector.tensor_tensor(mergT[:, 2 * q:2 * q + 2, :], gates[:, 2 * q:2 * q + 2, :], g,
                                                ALU.add).then_inc(merg, 1)
            dve.wait_ge(ld_gt1, 16)
            for n in range(2):
                for c in range(C):
                    key = ("mo", n, c)
                    wait_full(dve, key)
                    ns = slice(512 * n, 512 * n + 512)
                    step(nc.vector.tensor_tensor(ytok[:, c, :], bank(key)[:, :], gt1b[:, ns], ALU.mult))
                    step.join()
                    drains(nc.vector.tensor_tensor(X[:, c, ns], X[:, c, ns], ytok[:, c, :], ALU.add), key)
                    wait_drained(dve, key)
            norm(5, after(("mo", 0, 1), ("mo", 1, 1)), lambda k: gm2[:, k:k + 1], lambda k: col("sh2", k), s=6)

            def run(ins):
                step(ins)
                step.join()

            dve.wait_ge(ld_route, 48)
            key = ("route", 0)
            wait_full(dve, key)
            drains(nc.vector.tensor_copy(lg, bank(key)[:, 0:72].rearrange("p (c n) -> p c n", c=C)), key)
            wait_drained(dve, key)
            io = con("iota")
            b3 = lambda a, n: a.unsqueeze(2).to_broadcast([P, C, n])
            io_c = lambda n: io[:, 0:n].unsqueeze(1).to_broadcast([P, C, n])
            gmax, gsum, pg = rsm[:, 0:2], rsm[:, 2:4], rsm[:, 2:4]
            run(nc.vector.tensor_reduce(gmax, lg[:, :, 0:NG], AX.X, ALU.max))
            G4 = gtmp[:, :, 0:NG]
            nc.vector.tensor_tensor(G4, lg[:, :, 0:NG], b3(gmax, NG), ALU.subtract).then_inc(ge_in, 1)
            dve.wait_ge(ge_exp, 1)
            run(nc.vector.tensor_reduce(gsum, G4, AX.X, ALU.add))
            run(nc.vector.reciprocal(pg, gsum))

            def first_max(oh_out, values, vmax, n, tmp):
                run(nc.vector.tensor_tensor(tmp, values, b3(vmax, n), ALU.is_lt))
                run(nc.vector.scalar_tensor_tensor(tmp, tmp, 1000.0, io_c(n), ALU.mult, ALU.add))
                run(nc.vector.tensor_reduce(rsm[:, 6:8], tmp, AX.X, ALU.min))
                run(nc.vector.tensor_tensor(oh_out, io_c(n), b3(rsm[:, 6:8], n), ALU.is_equal))

            first_max(gtmp[:, :, NG:2 * NG], lg[:, :, 0:NG], gmax, NG, G4)
            run(nc.vector.tensor_scalar(gtmp[:, :, NG:2 * NG], gtmp[:, :, NG:2 * NG], -1.0, -FAR, ALU.add, ALU.mult))
            run(nc.vector.tensor_tensor(elm, lg[:, :, NG:NG + NE], rbias.unsqueeze(1).to_broadcast([P, C, NE]), ALU.add))
            for c in range(C):
                run(nc.vector.tensor_tensor(elm[:, c, :].rearrange("p (g e) -> p g e", e=EPG),
                                            elm[:, c, :].rearrange("p (g e) -> p g e", e=EPG),
                                            gtmp[:, c, NG:2 * NG].unsqueeze(2).to_broadcast([P, NG, EPG]), ALU.add))
            run(nc.vector.tensor_reduce(rsm[:, 8:10], elm, AX.X, ALU.max))
            first_max(oh[:, 0], elm, rsm[:, 8:10], NE, etmp)
            run(nc.vector.scalar_tensor_tensor(elm, oh[:, 0], 3 * FAR, elm, ALU.mult, ALU.add))
            run(nc.vector.tensor_reduce(rsm[:, 10:12], elm, AX.X, ALU.max))
            first_max(oh[:, 1], elm, rsm[:, 10:12], NE, etmp)
            nc.vector.tensor_tensor(msum, oh[:, 0], oh[:, 1], ALU.add).then_inc(picks, 1)
            nc.vector.tensor_tensor(rsm[:, 4:6], rsm[:, 10:12], rsm[:, 8:10], ALU.subtract).then_inc(two_in, 1)
            key = ("count", 0)
            wait_full(dve, key)
            run(nc.vector.tensor_tensor(cnt4, bank(key)[:, 64:96].unsqueeze(2).to_broadcast([P, NE, 3]),
                                        con("steps").unsqueeze(1).to_broadcast([P, NE, 3]), ALU.is_gt))
            run(nc.vector.tensor_reduce(icl[:, 0, :], cnt4, AX.X, ALU.add))
            run(nc.vector.tensor_tensor_scan(icl[:, 1, :], con("ones")[:, 0:NE], icl[:, 0, :], 0.0, ALU.mult, ALU.add))
            run(nc.vector.tensor_tensor(icl[:, 2, :], icl[:, 1, :], icl[:, 0, :], ALU.subtract))
            run(nc.vector.scalar_tensor_tensor(icl[:, 2, :], icl[:, 2, :], float(SLOT), con("extra_item"), ALU.mult,
                                               ALU.add))
            rank = bank(key)[:, 0:64].rearrange("p (c e) -> p c e", c=C)
            run(nc.vector.tensor_scalar(etmp, rank, float(SLOT), None, ALU.is_ge))
            run(nc.vector.tensor_tensor(etmp, etmp, icl[:, 2, :].unsqueeze(1).to_broadcast([P, C, NE]), ALU.mult))
            drains(nc.vector.tensor_tensor(dest, rank, con("first_item").unsqueeze(1).to_broadcast([P, C, NE]),
                                           ALU.add), key)
            wait_drained(dve, key)
            run(nc.vector.tensor_tensor(dest, dest, etmp, ALU.add))
            for j in range(2):
                run(nc.vector.tensor_tensor(etmp, oh[:, j], dest, ALU.mult))
                run(nc.vector.tensor_reduce(fidx[:, 2 * j:2 * j + 2], etmp, AX.X, ALU.add))
            nc.vector.tensor_copy(idx, fidx[:, 0:4]).then_inc(idx_ready, 1)
            step(nc.vector.tensor_copy(fidx[:, 4:36], io[:, 0:NE]))
            run(nc.vector.tensor_tensor(itm, icl[:, 1, :].unsqueeze(1).to_broadcast([P, 8, NE]),
                                        io[:, 0:8].unsqueeze(2).to_broadcast([P, 8, NE]), ALU.is_le))
            run(nc.vector.tensor_reduce(fidx[:, 36:44], itm, AX.X, ALU.add))
            step(nc.vector.tensor_scalar(fidx[:, 36:44], fidx[:, 36:44], float(NE - 1), None, ALU.min))
            run(nc.vector.tensor_tensor(itm[:, 0, 0:4], con("pairs"), icl[:, 1, NE - 1:NE].to_broadcast([P, 4]),
                                        ALU.is_lt))
            run(nc.vector.tensor_reduce(fidx[:, 44:45], itm[:, 0, 0:4], AX.X, ALU.add))
            run(nc.vector.tensor_scalar(fidx[:, 45:46], fidx[:, 44:45], float(NE // 2 - 1), None, ALU.add))
            run(nc.vector.tensor_scalar(fidx[:, 44:45], fidx[:, 44:45], float(NE // 2), None, ALU.add))
            nc.vector.tensor_copy(eid, fidx[:, 4:46]).then_inc(eid_ready, 1)
            dve.wait_ge(two_exp, 1)
            run(nc.vector.tensor_scalar(rsm[:, 12:14], rsm[:, 4:6], 1.0, None, ALU.add))
            run(nc.vector.reciprocal(rsm[:, 12:14], rsm[:, 12:14]))
            run(nc.vector.tensor_tensor(rsm[:, 12:14], rsm[:, 12:14], pg, ALU.mult))
            run(nc.vector.tensor_tensor(rsm[:, 14:16], rsm[:, 12:14], rsm[:, 4:6], ALU.mult))
            dve.wait_ge(eid_ready, 1)
            pairs = nc.vector.value_load(eid[0:1, MAX_ITEMS:MAX_ITEMS + 1], min_val=NE // 2, max_val=MAX_ITEMS // 2)
            with dve.Fori(0, pairs) as i:
                dve.wait_ge(tx_full, i + 1)
                for b in range(2):
                    nc.vector.tensor_tensor(xgT[:, 4 * b:4 * b + 4, :], banks[b].rearrange("p (k s) -> p k s", s=P),
                                            gm2[:, 4 * b:4 * b + 4].unsqueeze(2).to_broadcast([P, 4, P]),
                                            ALU.mult).then_inc(xg_half, 1)
                for b in range(2):
                    dve.wait_ge(xg_half, i * 2 + (b + 1))
                    nc.vector.tensor_tensor(xgT[:, 4 * b:4 * b + 4, :], xgT[:, 4 * b:4 * b + 4, :],
                                            col("sh2", 4 * b, 4).unsqueeze(2).to_broadcast([P, 4, P]),
                                            ALU.add).then_inc(xg_ready, 1)
                for u in range(2):
                    dve.wait_ge(expert_used, i * 6 + (3 * u + 2))
                    dve.wait_ge(sg_ready, i * 2 + (u + 1))
                    nc.vector.tensor_tensor(hd[:, u, :], banks[3][:, 0:256], sg[:, u, :],
                                            ALU.mult).then_inc(hd_ready, 1)
            dve.wait_ge(ld_gt2, 16)
            tail = fin_steps
            at = 0
            for c in range(C):
                dve.wait_ge(gathered, 32 * (c + 1))
                nc.vector.tensor_scalar(yk[:, c, :], yk[:, c, :], rsm[:, 12 + c:13 + c], None, ALU.mult).then_inc(tail, 1)
                dve.wait_ge(tail, 3 * c + 1)
                nc.vector.scalar_tensor_tensor(yk[:, c, :], yk[:, 2 + c, :], rsm[:, 14 + c:15 + c], yk[:, c, :], ALU.mult,
                                               ALU.add).then_inc(tail, 1)
                dve.wait_ge(tail, 3 * c + 2)
                nc.vector.tensor_tensor(yk[:, c, :], yk[:, c, :], gt2b, ALU.mult).then_inc(tail, 1)
                dve.wait_ge(tail, 3 * c + 3)
                nc.vector.tensor_tensor(X[:, c, :], X[:, c, :], yk[:, c, :], ALU.add).then_inc(fin_c, 1)

        @block.tensor
        def _(pe):
            def slot(t, n=512):
                return ring[t % RING].rearrange("p (k n) -> p k n", n=n)

            def norm(n):
                for c in range(C):
                    pe.wait_ge(xn_ready[c], n + 1)
                    for k in range(KD):
                        key = ("norm", n, k // 2)
                        if c == 0 and k % 2 == 0:
                            wait_free(pe, key)
                        at = (k % 2) * SEQ + c * P
                        mm = pe.transpose(bank(key)[:, at:at + P], xn[:, c, k * P:(k + 1) * P], ident)
                        if c == 1 and k % 2 == 1:
                            fills(mm, key)

            def h_ready(n):
                for b in range(4):
                    wait_drained(pe, ("norm", n, b))

            def cols_group(key, wt, m0, i=None, rhs=None):
                wait_free(pe, key, i)
                for b in range(2):
                    for k in range(KD):
                        mm = pe.matmul(bank(key)[:, b * SEQ:(b + 1) * SEQ], wt[:, k, (m0 + b) * P:(m0 + b + 1) * P],
                                       hT[:, k, :], start=(k == 0), stop=(k == KD - 1))
                fills(mm, key)

            def ada(q):
                key = ("ada", q)
                t = T["ada", q]
                wait_free(pe, key)
                if q == 0:
                    pe.wait_ge(silu_ready, 1)
                for k in range(KD):
                    if k % 2 == 0:
                        wait_tile(pe, t + k // 2)
                    s = slot(t + k // 2, 2048)
                    for j in range(4):
                        mm = pe.matmul(bank(key)[32 * j:32 * j + 1, :], sil[:, k:k + 1],
                                       s[:, k % 2, 512 * j:512 * j + 512], start=(k == 0), stop=(k == KD - 1))
                    if k % 2:
                        mm.then_inc(tile_used, 1)

            def ffn(l):
                with pe.Fori(0, 3) as i:
                    for u in range(2):
                        t = T["up", l] + 2 * u
                        wait_tile(pe, t, i)
                        for h in range(2):
                            cols_group(("gate", l, u, h), slot(t), 2 * h, i)
                            if h == 0:
                                wait_tile(pe, t + 1, i)
                            cols_group(("val", l, u, h), slot(t + 1), 2 * h, i)
                for n in range(2):
                    for kk in range(3):
                        t = T["down", l] + 3 * n + kk
                        wait_tile(pe, t)
                        for c in range(C):
                            key = ("down", l, n, c)
                            if kk == 0:
                                wait_free(pe, key)
                            for k in range(8):
                                kf = 8 * kk + k
                                if n == 0 and c == 0 and k % 2 == 0:
                                    pe.wait_ge(ff_ready, 12 * l + kf // 2 + 1)
                                mm = pe.matmul(bank(key)[:, :], ffT[:, kf, c * P:(c + 1) * P], slot(t)[:, k, :],
                                               start=(kf == 0), stop=(kf == KF - 1))
                            if kk == 2:
                                fills(mm, key)
                            elif c == 1:
                                mm.then_inc(tile_used, 1)

            def rows_to_cols(g, loads):
                pe.wait_ge(ld_rows[g], 16 * loads)
                key = ("rows", g)
                wait_free(pe, key)
                fills(pe.transpose(bank(key)[:, 0:P], rowbuf[:, g, :], ident), key)

            pe.wait_ge(ld_ident, 16)
            rows_to_cols(0, 6)
            norm(0)
            h_ready(0)
            for j in range(4):
                wait_tile(pe, T["av"] + j)
                for c in range(C):
                    key = ("av", j, c)
                    wait_free(pe, key)
                    for k in range(KD):
                        mm = pe.matmul(bank(key)[:, :], hT[:, k, c * P:(c + 1) * P], slot(T["av"] + j)[:, k, :],
                                       start=(k == 0), stop=(k == KD - 1))
                    fills(mm, key)
            for g, loads in ((1, 7), (2, 4), (3, 4), (4, 10)):
                rows_to_cols(g, loads)
            pe.wait_ge(ld_ws, 16)
            for q in range(2):
                key = ("ws", q)
                wait_free(pe, key)
                for g in range(4):
                    mm = pe.transpose(bank(key)[:, g * P:(g + 1) * P], ws_in[:, 4 * q + g, :], ident)
                fills(mm, key)
            for j in range(4):
                wait_tile(pe, T["au"] + j)
                for h in range(2):
                    cols_group(("au", j, h), slot(T["au"] + j), 2 * h)
            pe.wait_ge(ws_scaled, 2)
            for c in range(C):
                wait_drained(pe, ("av", 3, c))
            for m in range(16):
                key = ("sv", m // 2)
                if m % 2 == 0:
                    wait_free(pe, key)
                for c in range(C):
                    at = (m % 2) * SEQ + c * P
                    g = m // 2
                    mm = pe.matmul(bank(key)[:, at:at + P], V[:, c, m * P:(m + 1) * P], wsr[:, c, g * P:(g + 1) * P],
                                   start=True, stop=True)
                if m % 2:
                    fills(mm, key)
            for n in range(2):
                for kh in range(2):
                    t = T["ao"] + 2 * n + kh
                    wait_tile(pe, t)
                    for c in range(C):
                        key = ("ao", n, c)
                        if kh == 0:
                            wait_free(pe, key)
                        for k in range(8):
                            ku = 8 * kh + k
                            if n == 0 and c == 0 and k % 2 == 0:
                                pe.wait_ge(y_ready, ku // 2 + 1)
                            mm = pe.matmul(bank(key)[:, :], uT[:, ku, c * P:(c + 1) * P], slot(t)[:, k, :],
                                           start=(ku == 0), stop=(ku == 15))
                        if kh == 1:
                            fills(mm, key)
                        elif c == 1:
                            mm.then_inc(tile_used, 1)
            ada(0)
            norm(1)
            h_ready(1)
            ffn(0)
            ada(1)
            norm(2)
            h_ready(2)
            for q in range(6):
                t = T["bx"] + q // 2
                if q % 2 == 0:
                    wait_tile(pe, t)
                cols_group(("bx", q), slot(t), 2 * (q % 2))
            for j in range(2):
                wait_tile(pe, T["bgate"] + j)
            for h in range(B_H):
                wait_drained(pe, ("bx", h))
                for j, name in enumerate(("br", "bi")):
                    key = (name, h)
                    wt = ring[(T["bgate"] + j) % RING][:, 0:12 * 256].rearrange("p (k e) -> p k e", e=256)
                    wait_free(pe, key)
                    for b in range(2):
                        for k in range(2):
                            mm = pe.matmul(bank(key)[:, b * SEQ:(b + 1) * SEQ], wt[:, 2 * h + k, b * P:(b + 1) * P],
                                           xbT[:, 2 * h + k, :], start=(k == 0), stop=(k == 1))
                    fills(mm, key)
            for q in range(6):
                t = T["bg"] + q // 2
                if q % 2 == 0:
                    wait_tile(pe, t)
                cols_group(("bg", q), slot(t), 2 * (q % 2))
            for j in range(3):
                t = T["bo"] + j
                wait_tile(pe, t)
                for n in ((j,) if j < 2 else (0, 1)):
                    for c in range(C):
                        key = ("bo", n, c)
                        if j < 2:
                            wait_free(pe, key)
                        for k in range(8 if j < 2 else 4):
                            kb, at = (k, k) if j < 2 else (8 + k, 4 * n + k)
                            if (n, c) == (0, 0) and kb in (0, 6):
                                pe.wait_ge(b_y, 1 + kb // 6)
                            mm = pe.matmul(bank(key)[:, :], Rt[:, kb, c * P:(c + 1) * P], slot(t)[:, at, :],
                                           start=(kb == 0), stop=(kb == KB - 1))
                        if j == 2:
                            fills(mm, key)
                        elif c == 1:
                            mm.then_inc(tile_used, 1)
            ada(2)
            norm(3)
            h_ready(3)
            ffn(1)
            pe.wait_ge(ld_mod, 32)
            key = ("rows", 5)
            wait_free(pe, key)
            fills(pe.transpose(bank(key)[:, 0:32], rowbuf[0:32, 0, :], ident[0:32, 0:32]), key)
            norm(4)
            h_ready(4)
            t = T["lora"]
            wait_tile(pe, t)
            s = ring[t % RING][:, 0:8 * 328].rearrange("p (k n) -> p k n", n=328)

            def cols_block(dst, wt, n0, n1):
                for k in range(KD):
                    mm = pe.matmul(dst, wt[:, k, n0:n1], hT[:, k, :], start=(k == 0), stop=(k == KD - 1))
                return mm

            wait_free(pe, ("kw", 0))
            fills(cols_block(banks[5][0:40, 0:SEQ], s, 0, 40), ("kw", 0))
            wait_free(pe, ("lora", 0))
            cols_block(banks[6][:, 0:SEQ], s, 40, 168)
            fills(cols_block(banks[6][:, SEQ:2 * SEQ], s, 168, 296), ("lora", 0))
            wait_free(pe, ("lora", 1))
            fills(cols_block(banks[7][0:32, 0:SEQ], s, 296, 328), ("lora", 1))
            for name in "rkv":
                wait_tile(pe, T[name])
                for q in range(2):
                    cols_group((name, q), slot(T[name]), 2 * q)
            pe.wait_ge(ld_mx, 64)
            pe.wait_ge(lora_act, 3)
            for name, r in (("zw", slice(0, HD)), ("za", slice(HD, P))):
                for q in range(2):
                    key = (name, q)
                    wait_free(pe, key)
                    for b in range(2):
                        m = 2 * q + b
                        mm = pe.matmul(bank(key)[:, b * SEQ:(b + 1) * SEQ], wa2[r, m * P:(m + 1) * P], mix[r, 12, :],
                                       start=True, stop=True)
                    fills(mm, key)
            for c in range(C):
                key = ("gg", c)
                ts = slice(c * P, (c + 1) * P)
                wait_free(pe, key)
                pe.matmul(bank(key)[:, :], mix[:, 13, ts], g2[:, 0, :], start=True, stop=False)
                fills(pe.matmul(bank(key)[:, :], mix[0:32, 14, ts], g2[0:32, 1, :], start=False, stop=True), key)
            t = T["q"]
            wait_tile(pe, t)
            for c in range(C):
                key = ("q", c)
                wait_free(pe, key)
                for k in range(KD):
                    mm = pe.matmul(bank(key)[:, :], hT[:, k, c * P:(c + 1) * P], slot(t)[:, k, :], start=(k == 0),
                                   stop=(k == KD - 1))
                fills(mm, key)
            t = T["kv"]
            wait_tile(pe, t)
            wait_free(pe, ("kv", 0))
            for c in range(C):
                for k in range(KD):
                    mm = pe.matmul(banks[6][:, c * SEQ:(c + 1) * SEQ], hT[:, k, c * P:(c + 1) * P],
                                   slot(t)[:, k, 0:256], start=(k == 0), stop=(k == KD - 1))
            fills(mm, ("kv", 0))
            cols_group(("qi", 0), slot(t), 2)
            pe.wait_ge(kx2, 1)
            for q in range(2):
                key = ("kn", q)
                wait_free(pe, key)
                for b in range(2):
                    mm = pe.matmul(bank(key)[:, b * SEQ:(b + 1) * SEQ], con("head_ones"), sq[:, 2 * q + b, :],
                                   start=True, stop=True)
                fills(mm, key)

            def turn(key, b, src):
                return pe.transpose(bank(key)[:, b * P:(b + 1) * P], src, ident)

            def gates(j):
                wait_tile(pe, T["gate", j])
                for h in range(2):
                    cols_group(("ga", 2 * j + h), slot(T["gate", j]), 2 * h)

            gates(0)
            for c in range(C):
                wait_drained(pe, ("q", c))
            for q in range(2):
                key = ("qt", q)
                wait_free(pe, key)
                for b in range(2):
                    for c in range(C):
                        mm = turn(key, 2 * b + c, qn[:, c, (2 * q + b) * P:(2 * q + b + 1) * P])
                fills(mm, key)
            wait_drained(pe, ("kv", 0))
            key = ("kvt", 0)
            wait_free(pe, key)
            for b in range(2):
                for c in range(C):
                    mm = turn(key, 2 * b + c, kvn[:, c, b * P:(b + 1) * P])
            fills(mm, key)
            gates(1)
            t = T["kvup"]
            wait_tile(pe, t)
            wait_drained(pe, ("kvt", 0))
            s = ring[t % RING][:, 0:2 * D].rearrange("p (k n) -> p k n", n=D)
            for name, n0 in (("kr", 0), ("vr", 512)):
                for c in range(C):
                    key = (name, c)
                    wait_free(pe, key)
                    for k in range(2):
                        mm = pe.matmul(bank(key)[:, :], kvnT[:, k, c * P:(c + 1) * P], s[:, k, n0:n0 + 512],
                                       start=(k == 0), stop=(k == 1))
                    fills(mm, key)
            key = ("wi", 0)
            wait_free(pe, key)
            wait_drained(pe, ("kw", 0))
            for c in range(C):
                mm = pe.transpose(bank(key)[:, 8 * c:8 * c + 8], kw_sb[32:40, c * P:(c + 1) * P], ident[32:40, 32:40])
            fills(mm, key)
            pe.wait_ge(ld_rep, 64)
            wait_drained(pe, ("qi", 0))
            for c in range(C):
                S = (c + 1) * P
                for b in range(4):
                    key = ("dot", c, b)
                    wait_free(pe, key)
                    r = slice(32 * b, 32 * b + 32)
                    for j in range(2):
                        mm = pe.matmul(bank(key)[:, j * SEQ:j * SEQ + S], qiT[r, j, c * P:(c + 1) * P], kirep[r, 0:S],
                                       start=True, stop=True)
                    fills(mm, key)
            for c in range(C):
                wait_drained(pe, ("kr", c))
            for q in range(2):
                key = ("kt", q)
                wait_free(pe, key)
                for b in range(2):
                    for c in range(C):
                        mm = turn(key, 2 * b + c, qn[:, c, (2 * q + b) * P:(2 * q + b + 1) * P])
                fills(mm, key)
            gates(2)
            gates(3)
            for q in range(2):
                wait_drained(pe, ("kt", q))
                wait_drained(pe, ("qt", q))
                wait_drained(pe, ("vr", q))

            def logits(c, g):
                S = (c + 1) * P
                key = ("lg", c, g)
                wait_free(pe, key)
                for j in range(2):
                    h = head_of(g, j)
                    r = slice(HD * (h % 2), HD * (h % 2) + HD)
                    mm = pe.matmul(bank(key)[:, j * SEQ:j * SEQ + S], qT[r, h // 2, c * P:(c + 1) * P],
                                   kT[r, h // 2, 0:S], start=True, stop=True)
                fills(mm, key)

            def turn_p(c, g):
                key = ("pt", c, g)
                n = 4 * c + g
                wait_free(pe, key)
                pe.wait_ge(p_ready, 2 * n + 2)
                for j in range(2):
                    for st in range(c + 1):
                        mm = turn(key, j * (c + 1) + st, Pb[:, n % 2, j, st * P:(st + 1) * P])
                fills(mm, key)

            def values(c, g):
                key = ("o", c)
                n = 4 * c + g
                if g == 0:
                    wait_free(pe, key)
                wait_drained(pe, ("pt", c, g))
                for j in range(2):
                    h = head_of(g, j)
                    for st in range(c + 1):
                        mm = pe.matmul(bank(key)[:, h * HD:(h + 1) * HD], pT[:, n % 2, j * (c + 1) + st, :],
                                       Vt[:, st, h * HD:(h + 1) * HD], start=(st == 0), stop=(st == c))
                if g == 3:
                    fills(mm, key)
                else:
                    mm.then_inc(pv_used, 1)
            for c in range(C):
                for g in range(4):
                    logits(c, g)
                    if g > 0:
                        turn_p(c, g - 1)
                        values(c, g - 1)
                turn_p(c, 3)
                values(c, 3)
            for c in range(C):
                wait_drained(pe, ("o", c))
            for q in range(2):
                key = ("oat", q)
                wait_free(pe, key)
                for b in range(2):
                    for c in range(C):
                        mm = turn(key, 2 * b + c, otok[:, c, (2 * q + b) * P:(2 * q + b + 1) * P])
                fills(mm, key)
            for c in range(C):
                key = ("vt", c)
                wait_free(pe, key)
                for q in range(2):
                    wait_drained(pe, ("v", q))
                for m in range(4):
                    mm = turn(key, m, mix[:, 8 + m, c * P:(c + 1) * P])
                fills(mm, key)
            pe.wait_ge(qr_ready, 1)
            for key, src in ((("bt", 0), aS), (("ktt", 0), Kh)):
                wait_free(pe, key)
                for m in range(4):
                    mm = turn(key, m, src[:, m, 0:P])
                fills(mm, key)
            key = ("bonus", 0)
            wait_free(pe, key)
            for c in range(C):
                for m in range(4):
                    mm = pe.matmul(bank(key)[:, 8 * c + 2 * m:8 * c + 2 * m + 2], sq[:, m, c * P:(c + 1) * P],
                                   rkbd[:, m, :], start=True, stop=True)
            fills(mm, key)
            for c in range(C):
                ts = slice(c * P, (c + 1) * P)
                for h in range(8):
                    key = ("mt", c, h)
                    r = slice(HD * (h % 2), HD * (h % 2) + HD)
                    wait_free(pe, key)
                    qr = QR[r, 2 * (h // 2) + c, :, :]
                    pe.matmul(bank(key)[:, 0:256].rearrange("p (a t) -> p a t", a=2), aS[r, h // 2, ts], qr, start=True,
                              stop=True)
                    fills(pe.matmul(bank(key)[:, 256:512].rearrange("p (a t) -> p a t", a=2), Kh[r, h // 2, ts], qr,
                                    start=True, stop=True), key)
                for lv in range(1, 8):
                    for hf in range(2):
                        key = ("t1", c, lv, hf)
                        wait_free(pe, key)
                        pe.wait_ge(ct_ready, 14 * c + 2 * (lv - 1) + hf + 1)
                        if lv == 2:
                            wait_drained(pe, ("t1", c, 1, hf))
                            pe.wait_ge(x_first, 2 * c + hf + 1)
                        elif lv > 2:
                            wait_drained(pe, ("xa", c, lv - 1, hf))
                        for b in range(4):
                            h = 4 * hf + b
                            if lv == 1:
                                mm = turn(key, b, CT[:, h, :])
                            else:
                                mm = pe.matmul(bank(key)[:, b * P:(b + 1) * P], CT[:, h, :], Xm[:, h, :], start=True,
                                               stop=True)
                        fills(mm, key)
                    if lv == 1:
                        continue
                    for hf in range(2):
                        wait_drained(pe, ("t1", c, lv, hf))
                        if lv > 2:
                            wait_drained(pe, ("xb", c, lv - 1, hf))
                        for name in ("xa", "xb"):
                            if lv == 7 and name == "xa":
                                continue
                            key = (name, c, lv, hf)
                            wait_free(pe, key)
                            for b in range(4):
                                h = 4 * hf + b
                                left, right = T1[:, h, :], XT[:, c, h, :]
                                if name == "xa":
                                    left, right = right, left
                                mm = pe.matmul(bank(key)[:, b * P:(b + 1) * P], left, right, start=True, stop=True)
                            fills(mm, key)
                for par in range(2):
                    key = ("rh", c, par)
                    wait_free(pe, key)
                    r = slice(HD * par, HD * par + HD)
                    if c == 1:
                        wait_drained(pe, ("z", 0))
                    for a in range(4):
                        h = 2 * a + par
                        dst = bank(key)[:, a * HD:(a + 1) * HD]
                        if c == 1:
                            pe.matmul(dst, QR[r, 2 * a + c, 0, :], zst[r, a, :], start=True, stop=False)
                        mm = pe.matmul(dst, MT[:, h, 256:384], vtok[:, c, h * HD:(h + 1) * HD], start=(c == 0),
                                       stop=True)
                    fills(mm, key)
                for par in range(2):
                    wait_drained(pe, ("rh", c, par))
                for hf in range(2):
                    wait_drained(pe, ("xb", c, 7, hf))
                key = ("sa", c)
                wait_free(pe, key)
                for h in range(8):
                    mm = pe.matmul(bank(key)[:, h * HD:(h + 1) * HD], XT[:, c, h, :], rhtok[:, h * HD:(h + 1) * HD],
                                   start=True, stop=True)
                fills(mm, key)
                wait_drained(pe, key)
                for par in range(2):
                    key = ("y", c, par)
                    wait_free(pe, key)
                    r = slice(HD * par, HD * par + HD)
                    for a in range(4):
                        h = 2 * a + par
                        hs = slice(h * HD, (h + 1) * HD)
                        dst = bank(key)[:, a * HD:(a + 1) * HD]
                        if c == 1:
                            pe.matmul(dst, QR[r, 2 * a + c, 1, :], zst[r, a, :], start=True, stop=False)
                        pe.matmul(dst, MT[:, h, 128:256], satok[:, c, hs], start=(c == 0), stop=False)
                        mm = pe.matmul(dst, MT[:, h, 384:512], vtok[:, c, hs], start=False, stop=True)
                    fills(mm, key)
                if c == 0:
                    key = ("z", 0)
                    wait_free(pe, key)
                    wait_drained(pe, ("bt", 0))
                    wait_drained(pe, ("ktt", 0))
                    for h in range(8):
                        hs = slice(h * HD, (h + 1) * HD)
                        dst = banks[4][HD * (h % 2):HD * (h % 2) + HD, (h // 2) * HD:(h // 2 + 1) * HD]
                        pe.matmul(dst, btok[:, hs], satok[:, 0, hs], start=True, stop=False)
                        mm = pe.matmul(dst, ktok[:, hs], vtok[:, 0, hs], start=False, stop=True)
                    fills(mm, key)
            pe.wait_ge(or_rows, 2)
            for q in range(2):
                key = ("ort", q)
                wait_free(pe, key)
                for b in range(2):
                    for c in range(C):
                        mm = turn(key, 2 * b + c, ytok[:, c, (2 * q + b) * P:(2 * q + b + 1) * P])
                fills(mm, key)
            for b, (src, name) in enumerate(((oaT, "oat"), (orT, "ort"))):
                t = T["branch"] + b
                wait_tile(pe, t)
                for q in range(2):
                    wait_drained(pe, (name, q))
                s = ring[t % RING].rearrange("p (k n) -> p k n", n=D)
                for q in range(4):
                    key = ("br", b, q)
                    wait_free(pe, key)
                    for j in range(2):
                        m = 2 * q + j
                        for k in range(4):
                            mm = pe.matmul(bank(key)[:, j * SEQ:(j + 1) * SEQ], s[:, k, m * P:(m + 1) * P], src[:, k, :],
                                           start=(k == 0), stop=(k == 3))
                    fills(mm, key)
            for n in range(2):
                t = T["mo"] + n
                wait_tile(pe, t)
                for c in range(C):
                    key = ("mo", n, c)
                    wait_free(pe, key)
                    for k in range(KD):
                        if (n, c) == (0, 0) and k % 2 == 0:
                            pe.wait_ge(merg, k // 2 + 1)
                        mm = pe.matmul(bank(key)[:, :], mergT[:, k, c * P:(c + 1) * P], slot(t)[:, k, :],
                                       start=(k == 0), stop=(k == KD - 1))
                    fills(mm, key)
            norm(5)
            h_ready(5)
            pe.wait_ge(ld_route, 48)
            key = ("route", 0)
            wait_free(pe, key)
            for c in range(C):
                for k in range(KD):
                    mm = pe.matmul(bank(key)[:, 36 * c:36 * c + 36], hT[:, k, c * P:(c + 1) * P], rw[:, k, :],
                                   start=(k == 0), stop=(k == KD - 1))
            fills(mm, key)
            key = ("count", 0)
            wait_free(pe, key)
            pe.wait_ge(picks, 1)
            pe.matmul(bank(key)[:, 0:NE], con("before"), msum[:, 0, :], start=True, stop=True)
            pe.matmul(bank(key)[:, NE:2 * NE], con("ones"), msum[:, 0, :], start=True, stop=False)
            pe.matmul(bank(key)[:, NE:2 * NE], con("before"), msum[:, 1, :], start=False, stop=True)
            pe.matmul(bank(key)[:, 2 * NE:3 * NE], con("ones"), msum[:, 0, :], start=True, stop=False)
            fills(pe.matmul(bank(key)[:, 2 * NE:3 * NE], con("ones"), msum[:, 1, :], start=False, stop=True), key)
            wait_drained(pe, key)
            pe.wait_ge(eid_ready, 1)
            pairs = nc.tensor.value_load(eid[0:1, MAX_ITEMS:MAX_ITEMS + 1], min_val=NE // 2, max_val=MAX_ITEMS // 2)
            with pe.Fori(0, pairs) as i:
                pe.wait_ge(e_x, i * 16 + 16)
                for k in range(KD):
                    mm = pe.transpose(banks[k // 4][:, k % 4 * P:(k % 4 + 1) * P], xsl[:, k * P:(k + 1) * P], ident)
                mm.then_inc(tx_full, 1)
                pe.wait_ge(xg_ready, i * 2 + 2)
                for u in range(2):
                    for q in range(2):
                        pe.wait_ge(e_w[3 * u + q], i * 32 + 32)
                        s = slots[3 * u + q].rearrange("p (k n) -> p k n", n=512)
                        for k in range(KD):
                            for n in range(2):
                                mm = pe.matmul(banks[2 + q][n * SLOT:(n + 1) * SLOT, 0:256],
                                               xgT[:, k, u * SLOT:(u + 1) * SLOT], s[:, k, 256 * n:256 * n + 256],
                                               start=(k == 0), stop=(k == KD - 1))
                        mm.then_inc(expert_used, 1)
                    pe.wait_ge(hd_ready, i * 2 + (u + 1))
                    for b in range(2):
                        mm = pe.transpose(banks[4 + u][:, b * P:(b + 1) * P], hd[:, u, b * P:(b + 1) * P], ident)
                    mm.then_inc(ht_full, 1)
                    pe.wait_ge(ht_ready, i * 2 + (u + 1))
                    pe.wait_ge(e_w[3 * u + 2], i * 32 + 32)
                    s = slots[3 * u + 2].rearrange("p (k n) -> p k n", n=D)
                    for k in range(4):
                        half, b = divmod(k, 2)
                        for n in range(2):
                            mm = pe.matmul(banks[6 + u][n * SLOT:(n + 1) * SLOT, :],
                                           hTe[:, u, b * P + half * SLOT:b * P + (half + 1) * SLOT],
                                           s[:, k, 512 * n:512 * n + 512], start=(k == 0), stop=(k == 3))
                    mm.then_inc(expert_used, 1)


def kernel(**inputs):
    import numpy as _np
    import concourse.bacc as _bacc
    from concourse import mybir as _mybir
    from concourse.bass_utils import run_bass_kernel_spmd as _run

    nc = _bacc.Bacc("TRN2", target_bir_lowering=False, num_devices=1)
    arrays = {f"in_{name}": _np.ascontiguousarray(a) for name, a in inputs.items()}
    arrays["in_constants"] = _constants()
    aps = {}
    for name, a in arrays.items():
        aps[name[3:]] = nc.dram_tensor(name, a.shape, _mybir.dt.from_np(a.dtype), kind="ExternalInput").ap()
    out = nc.dram_tensor("out_0", (1, SEQ, D), F32, kind="ExternalOutput").ap()
    scratch = {name: nc.dram_tensor(name, shape, F32, kind="Internal").ap() for name, shape in SCRATCH.items()}
    x = aps.pop("x")
    build(nc, x, aps, out, scratch)
    r = _run(nc, [arrays], core_ids=[0])
    return r.results[0]["out_0"]
```

```python
from contextlib import ExitStack

import numpy as np

import concourse.bass as bass
from concourse import mybir

ALU = mybir.AluOpType
ACT = mybir.ActivationFunctionType
F32 = mybir.dt.float32
F32R = mybir.dt.float32r
I32 = mybir.dt.int32
U32 = mybir.dt.uint32
AX = mybir.AxisListType

P = 128
SEQ = 256
C = SEQ // P
D = 1024
KD = D // P
A_W = 2048
A_G = 8
B_W = 1536
KB = B_W // P
B_H = 6
FF = 3072
KF = FF // P
EPS = 1e-6
TILE = 8 * 512
RING = 4

AH = 8
HD = 64
IH = 8
IHD = 32
TOPK = 64
NG = 4
NE = 32
EPG = NE // NG
DE = 512
SLOT = 32
EXTRA = 16
MAX_ITEMS = NE + EXTRA
STEPS = SEQ // SLOT - 1
STRIPS = P // SLOT
KAPPA = float(np.exp(-0.5))
FAR = -1e30

ROWS = {}


def _rows():
    groups = [
        [("norm_mix", 16), ("norm_ffn", 16), ("a_gain", 16), ("cvec", 8), ("mix_g", 8), ("bcw", 48)],
        [("fcw0_0", 48), ("fcw0_1", 48), ("moe_g", 8), ("k_k", 4), ("k_a", 4), ("w0", 4), ("a0", 4)],
        [("fcw0_2", 48), ("fcb0", 48), ("lam", 12), ("bcb", 12)],
        [("fcw1_0", 48), ("fcw1_1", 48), ("bba", 12), ("bbx", 12)],
        [("fcw1_2", 48), ("fcb1", 48), ("mu", 14), ("mu_tail", 1), ("r_k", 4), ("kv_g", 2), ("q_g", 1), ("k_g", 1)],
        [("sh1", 8), ("sc1", 8), ("sh2", 8), ("sc2", 8)],
    ]
    for g, group in enumerate(groups):
        at = 0
        for name, n in group:
            ROWS[name] = (g, at, n)
            at += n
    return groups


ROW_GROUPS = _rows()
NCOLS = len(ROW_GROUPS) * P

CONSTS = {}


def _constants():
    s = np.arange(P)[:, None]
    t = np.arange(P)[None, :]
    parts = []

    def put(name, a):
        a = np.broadcast_to(np.asarray(a, np.float32), (P, np.asarray(a).shape[-1]))
        at = sum(x.shape[1] for x in parts)
        CONSTS[name] = (at, a.shape[1])
        parts.append(a)

    put("ident", s == t)
    put("ones", np.ones((1, P)))
    put("before", s < t)
    put("head_ones", s // HD == t // HD)
    put("keep", np.concatenate([s < t, s <= t, s < t, s <= t], 1))
    put("level", np.concatenate([(s >> i == t >> i) & ((t >> (i - 1)) % 2 == 1) & ((s >> (i - 1)) % 2 == 0)
                                 for i in range(1, 8)], 1))
    put("dist", np.concatenate([s + c * P - np.arange(SEQ)[None, :] for c in range(C)], 1))
    put("iota", np.arange(MAX_ITEMS)[None, :])
    put("steps", ((1 + np.arange(STEPS)) * SLOT)[None, :])
    put("pairs", (2 * np.arange(EXTRA // 2))[None, :])
    put("first_item", (SLOT * np.arange(NE))[None, :])
    put("extra_item", (SLOT * (NE - 1 - np.arange(NE)))[None, :])
    return np.ascontiguousarray(np.concatenate(parts, 1), np.float32)


class Plan:

    def __init__(self):
        self.groups, self.uses, self.fulls, self.tiles, self.body = {}, [0] * 8, [0] * 8, 0, None

    def group(self, key, bank, closes_tile=False):
        self.uses[bank] += 1
        if closes_tile:
            self.tiles += 1
            full = ("tile", self.tiles)
        else:
            self.fulls[bank] += 1
            full = ("bank", self.fulls[bank])
        self.groups[key] = [bank, self.uses[bank] - 1, full, 0, 0]
        if self.body is not None:
            self.body.append(key)

    def tile(self):
        self.tiles += 1

    def loop(self, times, body):
        uses, fulls, tiles = list(self.uses), list(self.fulls), self.tiles
        self.body = []
        body()
        for key in self.body:
            g = self.groups[key]
            g[3] = self.uses[g[0]] - uses[g[0]]
            g[4] = self.tiles - tiles if g[2][0] == "tile" else self.fulls[g[0]] - fulls[g[0]]
        self.body = None
        for b in range(8):
            self.uses[b] += (times - 1) * (self.uses[b] - uses[b])
            self.fulls[b] += (times - 1) * (self.fulls[b] - fulls[b])
        self.tiles += (times - 1) * (self.tiles - tiles)


def at_turn(value, stride, i):
    return value if i is None else i * stride + value


class Steps:

    def __init__(self, eng, sem):
        self.eng, self.sem, self.n, self.i, self.per = eng, sem, 0, None, 0

    def __call__(self, instruction):
        instruction.then_inc(self.sem, 1)
        self.n += 1

    def join(self):
        self.eng.wait_ge(self.sem, at_turn(self.n, self.per, self.i))

    def enter(self, i, per):
        self.i, self.per, self.start = i, per, self.n

    def leave(self, times):
        assert self.n - self.start == self.per, (self.n - self.start, self.per)
        self.n += (times - 1) * self.per
        self.i = None

SCRATCH = {"xs": (MAX_ITEMS * SLOT, D), "mod": (6 * D,)}


def make_plan():
    p = Plan()
    T = {}

    def norm(n):
        for b in range(4):
            p.group(("norm", n, b), b)

    def ada_first(q):
        T["ada", q] = [p.tiles, p.tiles + 1, p.tiles + 3, p.tiles + 4]
        p.tile()
        p.tile()

    def ada(q):
        p.tile()
        p.group(("ada", q), 7, closes_tile=True)

    def ffn(l):
        T["up", l] = p.tiles

        def body():
            for u in range(2):
                for j, name in enumerate(("gate", "val")):
                    for h in range(2):
                        p.group((name, l, u, h), 4 * (1 - u) + 2 * h + j, closes_tile=h == 1)
        p.loop(3, body)
        T["down", l] = [p.tiles + j + 2 * (j == 5 and l == 0) for j in range(6)]
        for n in range(2):
            p.tile()
            p.tile()
            if (l, n) == (0, 1):
                ada_first(1)
            p.group(("down", l, n, 0), 2 * n)
            p.group(("down", l, n, 1), 2 * n + 1, closes_tile=True)

    p.group(("rows", 0), 4)
    norm(0)
    T["av"] = p.tiles
    for j in range(4):
        for c in range(C):
            p.group(("av", j, c), 4 + (2 * j + c) % 4, closes_tile=c == 1)
    for g in range(1, 5):
        p.group(("rows", g), g - 1)
    for q in range(2):
        p.group(("ws", q), q)
    T["au"] = p.tiles
    for j in range(4):
        for h in range(2):
            p.group(("au", j, h), (2 * j + h + 2) % 4, closes_tile=h == 1)
    for m in range(8):
        p.group(("sv", m), 4 + m % 4)
    T["ao"] = [p.tiles + j + 2 * (j == 3) for j in range(4)]
    for n in range(2):
        p.tile()
        if n == 1:
            ada_first(0)
        p.group(("ao", n, 0), 2 * n)
        p.group(("ao", n, 1), 2 * n + 1, closes_tile=True)
    ada(0)
    norm(1)
    ffn(0)
    ada(1)
    norm(2)
    T["bx"] = p.tiles
    for q in range(6):
        p.group(("bx", q), (q + 4) % 8, closes_tile=q % 2 == 1)
    T["bgate"] = p.tiles
    for h in range(B_H):
        p.group(("br", h), (2 + 2 * h) % 8, closes_tile=h == B_H - 1)
        p.group(("bi", h), (3 + 2 * h) % 8, closes_tile=h == B_H - 1)
    T["bg"] = p.tiles
    for q in range(6):
        p.group(("bg", q), 2 + q, closes_tile=q % 2 == 1)
    T["bo"] = [p.tiles + j + 2 * (j == 2) for j in range(3)]
    p.tile()
    p.tile()
    ada_first(2)
    for n in range(2):
        p.group(("bo", n, 0), 2 * n)
        p.group(("bo", n, 1), 2 * n + 1, closes_tile=n == 1)
    ada(2)
    norm(3)
    ffn(1)
    def gates(j, *at):
        T["gate", j] = p.tiles
        for h in range(2):
            p.group(("ga", 2 * j + h), at[h], closes_tile=h == 1)

    p.group(("rows", 5), 4)
    norm(4)
    for name, q in (("lora", 0), ("lora", 1), ("r", 0), ("r", 1), ("k", 0), ("k", 1), ("v", 0), ("v", 1)):
        if (name, q) == ("lora", 0):
            T["lora"] = p.tiles
            p.group(("kw", 0), 5)
        if name in "rkv" and q == 0:
            T[name] = p.tiles
        p.group((name, q), {"lora": 6, "r": 0, "k": 2, "v": 4}[name] + q, closes_tile=q == 1)
    for q in range(2):
        p.group(("zw", q), 6 + q)
    for q in range(2):
        p.group(("za", q), q)
    for c in range(C):
        p.group(("gg", c), 2 + c)
    T["q"] = p.tiles
    for c in range(C):
        p.group(("q", c), 4 + c, closes_tile=c == 1)
    T["kv"] = p.tiles
    p.group(("kv", 0), 6)
    p.group(("qi", 0), 7, closes_tile=True)
    for q in range(2):
        p.group(("kn", q), q)
    gates(0, 7, 0)
    for q in range(2):
        p.group(("qt", q), 2 + q)
    p.group(("kvt", 0), 4)
    gates(1, 1, 2)
    T["kvup"] = p.tiles
    for c in range(C):
        p.group(("kr", c), 5 + c)
    for c in range(C):
        p.group(("vr", c), 7 if c == 0 else 0, closes_tile=c == 1)
    p.group(("wi", 0), 1)
    for c in range(C):
        for b in range(4):
            p.group(("dot", c, b), 2 + b if c == 0 else (6 + b) % 8)
    for q in range(2):
        p.group(("kt", q), 2 + q)
    gates(2, 0, 1)
    gates(3, 6, 7)
    for c in range(C):
        for g in range(4):
            p.group(("lg", c, g), 4 + (g % 2))
            if g > 0:
                p.group(("pt", c, g - 1), 6 + (g - 1) % 2)
        p.group(("pt", c, 3), 7)
    for c in range(C):
        p.group(("o", c), 2 + c)
    for q in range(2):
        p.group(("oat", q), 4 + q)
    for c in range(C):
        p.group(("vt", c), 6 + c)
    p.group(("bt", 0), 0)
    p.group(("ktt", 0), 1)
    p.group(("bonus", 0), 2)
    for c in range(C):
        for h in range(8):
            p.group(("mt", c, h), 4 + h % 4)
        for hf in range(2):
            p.group(("t1", c, 1, hf), hf)
        for lv in range(2, 8):
            for hf in range(2):
                p.group(("t1", c, lv, hf), hf)
            if c == 1 and lv < 4:
                if lv == 2:
                    T["branch"] = p.tiles
                p.group(("br", 0, lv - 2), 6 + lv % 2)
            for hf in range(2):
                if lv < 7:
                    p.group(("xa", c, lv, hf), 2 + hf)
                p.group(("xb", c, lv, hf), 4 + hf)
        for par in range(2):
            p.group(("rh", c, par), 6 + par)
        p.group(("sa", c), 0)
        for par in range(2):
            p.group(("y", c, par), 2 + par)
        if c == 0:
            p.group(("z", 0), 4)
    for q in (2, 3):
        p.group(("br", 0, q), 2 + q, closes_tile=q == 3)
    for q in range(2):
        p.group(("ort", q), 6 + q)
    for q in range(4):
        p.group(("br", 1, q), q, closes_tile=q == 3)
    T["mo"] = p.tiles
    for n in range(2):
        p.group(("mo", n, 0), 2 * n)
        p.group(("mo", n, 1), 2 * n + 1, closes_tile=True)
    norm(5)
    p.group(("route", 0), 4)
    p.group(("count", 0), 5)
    return p, T


def build(nc, x, w, out, scratch):
    plan, T = make_plan()
    _constants()
    ctx = ExitStack()
    with ctx:
        def sb(name, shape, dt=F32):
            return ctx.enter_context(nc.sbuf_tensor(name, shape, dt))

        def sem(name):
            return ctx.enter_context(nc.semaphore(name))

        NCONST = sum(n for _, n in CONSTS.values())
        ARENA = 26880
        at_big = -(-nc.sbuf_base // 32) * 32
        big = sb("big", [P, RING * TILE + ARENA])
        X = sb("X", [P, C, D])
        at_xn = -(-nc.sbuf_base // 32) * 32
        xn = sb("xn", [P, C, D])
        at_hT = -(-nc.sbuf_base // 32) * 32
        hT = sb("hT", [P, KD, SEQ])

        def parts(name, shape, offset):
            return nc.alloc_sbuf_tensor_at(name, shape, F32R, offset=offset)
        cols = sb("cols", [P, NCOLS])
        const = sb("const", [P, NCONST])
        small = sb("small", [P, 256])
        banks = [ctx.enter_context(nc.psum_tensor(f"bank{b}", [P, 512], F32)) for b in range(8)]

        def con(name, parts=P):
            at, n = CONSTS[name]
            return const[0:parts, at:at + n]

        def col(name, k=0, n=1):
            g, at, _ = ROWS[name]
            return cols[:, g * P + at + k:g * P + at + k + n]

        def col_at(name, k):
            g, at, _ = ROWS[name]
            return cols[:, bass.ds(k + (g * P + at), 1)]

        ident = con("ident")
        ring = [big[:, s * TILE:(s + 1) * TILE] for s in range(RING)]
        arena = big[:, RING * TILE:RING * TILE + ARENA]

        def area(at, *shape):
            n = int(np.prod(shape))
            assert at + n <= ARENA, (at, n)
            v = arena[:, at:at + n]
            if len(shape) == 2:
                v = v.rearrange("p (a b) -> p a b", b=shape[1])
            if len(shape) == 3:
                v = v.rearrange("p (a b c) -> p a b c", b=shape[1], c=shape[2])
            return v

        V = area(0, C, A_W)
        uT = area(4096, 16, SEQ)
        bsb = area(8192, A_G, P)
        ws_in = area(9216, A_G, P)
        wsT = area(10240, A_G * P)
        wsr = area(11264, C, A_G * P)
        sv_tmp = area(13312, 4, SEQ)
        v_junk = area(4096, A_W)
        rowbuf = area(14336, 5, P)
        adab = area(23552, 3, 512)
        at_arena = at_big + 4 * RING * TILE
        ff_hi = parts("ff_hi", [P, KF, SEQ], at_arena)
        ff_lo = parts("ff_lo", [P, KF, SEQ], at_arena + 4 * KF * SEQ)
        conv_g = area(12288, 2, 512)
        conv_v = area(13312, 2, 512)
        gelu_g = area(14336, 2, 512)
        b_hi = parts("b_hi", [P, KB, SEQ], at_arena + 4 * KB * SEQ)
        b_lo = parts("b_lo", [P, KB, SEQ], at_arena + 8 * KB * SEQ)
        y_hi = parts("y_hi", [P, 16, SEQ], at_arena + 4 * 4096)
        y_lo = parts("y_lo", [P, C, A_W], at_arena)
        w_hi = [parts(f"w_hi{j}", [P, TILE], at_arena + 4 * (15360 + j * TILE)) for j in range(2)]
        w_lo = [parts(f"w_lo{j}", [P, TILE], at_big + 4 * j * TILE) for j in range(RING)]
        h_hi = parts("h_hi", [P, KD, SEQ], at_hT)
        h_lo = parts("h_lo", [P, KD, SEQ], at_xn)
        mod_rows = area(25664, P)
        xbT = area(0, KB, SEQ)
        Rt = area(3072, KB, SEQ)
        It = area(6144, KB, SEQ)
        At = area(9216, KB, SEQ)
        Tt = area(12288, KB, SEQ)
        Gt = area(0, KB, SEQ)
        lamt = area(25088, 4, KB)
        ssq = small[:, 0:2]
        var = small[:, 2:4]
        std = small[:, 4:6]
        rstd = small[:, 6:8]
        vsq = small[:, 8:10]
        vvar = small[:, 10:12]
        vstd = small[:, 12:14]
        vrstd = small[:, 14:16]
        sil = small[:, 16:24]
        s8 = small[:, 24:36]

        ld_x, ld_ident, ld_const, ld_ws, ld_bs, ld_adab = sem("ld_x"), sem("ld_ident"), sem("ld_const"), sem("ld_ws"), sem("ld_bs"), sem("ld_adab")
        ld_rows = [sem(f"ld_rows{g}") for g in range(5)]
        rows_zero = sem("rows_zero")
        tile_loaded = [sem(f"tile_loaded{s}") for s in range(RING)]
        tile_used = sem("tile_used")
        bank_full = [sem(f"bank_full{b}") for b in range(8)]
        bank_free = [sem(f"bank_free{b}") for b in range(8)]
        act_steps, dve_steps, pool_steps = sem("act_steps"), sem("dve_steps"), sem("pool_steps")
        norm_sq, norm_var, norm_std, norm_rstd = sem("norm_sq"), sem("norm_var"), sem("norm_std"), sem("norm_rstd")
        xn_ready = [sem(f"xn_ready{c}") for c in range(C)]
        v_sq, v_var, v_std = sem("v_sq"), sem("v_var"), sem("v_std")
        ws_scaled, y_ready = sem("ws_scaled"), sem("y_ready")
        silu_ready = sem("silu_ready")
        conv_g0, conv_v0, gelu_done, ff_ready = sem("conv_g0"), sem("conv_v0"), sem("gelu_done"), sem("ff_ready")
        y_prod, y_hi_ready, b_prod, b_hi_ready = sem("y_prod"), sem("y_hi_ready"), sem("b_prod"), sem("b_hi_ready")
        w_hi_ready, w_lo_ready, h_hi_ready, ff_prod, ff_hi_ready = (sem("w_hi_ready"), sem("w_lo_ready"), sem("h_hi_ready"),
                                                                    sem("ff_prod"), sem("ff_hi_ready"))
        bx0, b_log, b_exp, b_gated, b_m2, b_mult, b_y = (sem("bx0"), sem("b_log"), sem("b_exp"), sem("b_gated"),
                                                          sem("b_m2"), sem("b_mult"), sem("b_y"))
        lam_exp = sem("lam_exp")
        st_mod, st_out = sem("st_mod"), sem("st_out")

        mix = area(0, 15, SEQ)
        sw = area(4096, 4, SEQ)
        cum = area(5120, 4, SEQ)
        em = area(6144, 4, SEQ)
        kx = area(7168, 4, SEQ)
        sq = area(8192, 4, SEQ)
        aS = area(9216, 4, SEQ)
        QR = area(10240, 8, 2, P)
        Kh = area(12288, 4, SEQ)
        vtok = area(13312, C, 512)
        btok = area(14336, 512)
        ktok = area(14848, 512)
        gtok = area(15360, C, 512)
        ytok = area(16384, C, 512)
        satok = area(17408, C, 512)
        rhtok = area(18432, 512)
        zst = area(18944, 4, HD)
        XT = area(19200, C, 8, P)
        Xm = area(21248, 8, P)
        T1 = area(22272, 8, P)
        CT = area(23296, 8, P)
        lnw = area(24320, 512)
        lnb = area(24832, 512)
        rw = area(25344, KD, 36)
        rbias = area(25632, NE)
        gt1b = area(25856, D)
        MT = area(0, 8, 512)
        gates = area(4096, 16, SEQ)
        mergT = area(0, 8, SEQ)
        orT = area(10240, 4, SEQ)
        gfb = area(23552, D)
        kw_sb = area(16384, SEQ)
        kirep = area(16640, SEQ)
        qiT = area(16896, 2, SEQ)
        qn = area(17408, C, 512)
        kvn = area(18432, C, SEQ)
        kvnT = area(18944, 2, SEQ)
        qT = area(19456, 4, SEQ)
        kT = area(20480, 4, SEQ)
        Vt = area(21504, C, 512)
        rel = area(22528, 2, 512)
        sc = area(23552, C, SEQ)
        Pb = area(13312, 2, 2, SEQ)
        pT = area(14336, 2, 4, P)
        wa2 = area(22784, 512)
        g2 = area(23296, 2, 512)
        oaT = xn[:, 0, :].rearrange("p (m t) -> p m t", t=SEQ)
        work = xn[:, 1, 0:512].rearrange("p (c s) -> p c s", c=C)
        neg = xn[:, 1, 512:1024].rearrange("p (c s) -> p c s", c=C)
        otok = qn
        gm1, gm2 = small[:, 36:44], small[:, 44:52]
        omu = small[:, 52:67]
        cmid, dmid, epc = small[:, 68:76], small[:, 76:84], small[:, 84:92]
        qst, kst, kvst = small[:, 92:108], small[:, 108:124], small[:, 124:126]
        gq8 = small[:, 126:127]
        wi = small[:, 128:144]
        m8 = small[:, 144:160]
        nmax, psum_, prec = small[:, 160:176], small[:, 176:192], small[:, 192:208]
        bonus = small[:, 208:224]
        gn_a, gn_b = small[:, 224:232], small[:, 232:240]
        rkbd = small[:, 240:248].rearrange("p (m h) -> p m h", h=2)
        slots = [big[:, s * TILE:(s + 1) * TILE] for s in range(6)]
        xsl = area(8192, D)
        xgT = area(10240, KD, 2 * SLOT)
        sg = area(11264, 2, P)
        hd = area(11776, 2, P)
        hTe = area(12288, 2, P)
        ysb = area(12800, 2, 256)
        gt2b = area(13824, D)
        yk = area(14848, 4, D)
        lg = area(19000, C, 36)
        gtmp = area(19080, C, 8)
        oh = area(19100, 2, C, NE)
        elm = area(19228, C, NE)
        etmp = area(19292, C, NE)
        dest = area(19356, C, NE)
        rsm = area(19420, 64)
        cnt4 = area(19500, NE, STEPS)
        icl = area(19724, 3, NE)
        itm = area(19820, EXTRA, NE)
        fidx = area(21004, 4 + MAX_ITEMS + 2)
        idx = area(21060, 4).bitcast(U32)
        eid = area(21064, MAX_ITEMS + 2).bitcast(I32)
        msum = area(21120, C, NE)

        ld_mod, ld_gfb, ld_mx, ld_ln, ld_gt1, ld_gt2, ld_rep = (sem("ld_mod"), sem("ld_gfb"), sem("ld_mx"), sem("ld_ln"),
                                                                sem("ld_gt1"), sem("ld_gt2"), sem("ld_rep"))
        ld_route = sem("ld_route")
        x_final, gm_ready, mix0, lora_act, cum_ready, exp_ready = (sem("x_final"), sem("gm_ready"), sem("mix0"),
                                                                   sem("lora_act"), sem("cum_ready"), sem("exp_ready"))
        kx2, qr_ready = sem("kx2"), sem("qr_ready")
        q_sq, q_var, q_root, k_sq, k_var, k_root = (sem("q_sq"), sem("q_var"), sem("q_root"), sem("k_sq"), sem("k_var"),
                                                    sem("k_root"))
        rel_used, score_sum, score_masked, neg_raw, neg_ready = (
            sem("rel_used"), sem("score_sum"), sem("score_masked"), sem("neg_raw"), sem("neg_ready"))
        lg_ready, p_ready = sem("lg_ready"), sem("p_ready")
        ct_ready, x_first, mt_clear = sem("ct_ready"), sem("x_first"), sem("mt_clear")
        gn_var, gn_root, or_rows, merg = sem("gn_var"), sem("gn_root"), sem("or_rows"), sem("merg")
        xs_zero, xs_cleared, ge_exp, ge_in, two_in, two_exp, picks, idx_ready, scattered = (
            sem("xs_zero"), sem("xs_cleared"), sem("ge_exp"), sem("ge_in"), sem("two_in"), sem("two_exp"), sem("picks"),
            sem("idx_ready"), sem("scattered"))
        e_w = [sem(f"expert_w{s}") for s in range(6)]
        e_x = sem("expert_x")
        st_y = [sem(f"st_y{u}") for u in range(2)]
        expert_used, tx_full, xg_ready, sg_ready, hd_ready, ht_full, ht_ready, y_copied = (
            sem("expert_used"), sem("tx_full"), sem("xg_ready"), sem("sg_ready"), sem("hd_ready"), sem("ht_full"),
            sem("ht_ready"), sem("y_copied"))
        gathered, fin_c, eid_ready = sem("gathered"), sem("fin_c"), sem("eid_ready")
        pv_used, y_sb, xg_half, fin_steps = sem("pv_used"), sem("y_sb"), sem("xg_half"), sem("fin_steps")

        def head_of(g, j):
            return 4 * (g // 2) + g % 2 + 2 * j

        def bank(key):
            return banks[plan.groups[key][0]]

        def wait_free(eng, key, i=None):
            b, use, _, du, _ = plan.groups[key]
            if use > 0:
                eng.wait_ge(bank_free[b], at_turn(use, du, i))

        def wait_full(eng, key, i=None):
            b, _, (kind, value), _, df = plan.groups[key]
            eng.wait_ge(tile_used if kind == "tile" else bank_full[b], at_turn(value, df, i))

        def wait_drained(eng, key, i=None):
            b, use, _, du, _ = plan.groups[key]
            eng.wait_ge(bank_free[b], at_turn(use + 1, du, i))

        def fills(matmul, key):
            b, _, (kind, _), _, _ = plan.groups[key]
            matmul.then_inc(tile_used if kind == "tile" else bank_full[b], 1)

        def drains(instruction, key):
            instruction.then_inc(bank_free[plan.groups[key][0]], 1)

        def wait_tile(eng, t, i=None):
            eng.wait_ge(tile_loaded[t % RING], at_turn(32 * (t // RING + 1), 32, i))

        b_tiles = [T["bx"] + j for j in range(3)] + [T["bg"] + j for j in range(3)] + T["bo"]
        ff_tiles = [[T["up", l] + j for j in range(12)] + T["down", l] for l in range(2)]
        split_tiles = [T["av"] + j for j in range(8)] + T["ao"] + ff_tiles[0] + b_tiles + ff_tiles[1]
        split_no = {t: n for n, t in enumerate(split_tiles)}

        def split_hi(t, i=None):
            n = split_no[t]
            wait_tile(nc.scalar, t, i)
            if n >= 2:
                nc.scalar.wait_ge(tile_used, at_turn(split_tiles[n - 2] + 1, 4, i))
            for hf in range(2):
                a = slice(hf * TILE // 2, (hf + 1) * TILE // 2)
                nc.scalar.copy(w_hi[n % 2][:, a], ring[t % RING][:, a]).then_inc(w_hi_ready, 1)

        def split_lo(t, i=None):
            n = split_no[t]
            wait_tile(nc.vector, t, i)
            for hf in range(2):
                a = slice(hf * TILE // 2, (hf + 1) * TILE // 2)
                nc.vector.wait_ge(w_hi_ready, at_turn(2 * n + hf + 1, 8, i))
                nc.vector.tensor_tensor(w_lo[t % RING][:, a], ring[t % RING][:, a], w_hi[n % 2][:, a].bitcast(F32),
                                        ALU.subtract).then_inc(w_lo_ready, 1)

        block = ctx.enter_context(nc.Block())

        @block.sync
        def _(sp):
            sp.dma_start(X[:, 0, :], x[0, 0:P, :]).then_inc(ld_x, 16)
            sp.dma_start(ident, w["constants"][:, 0:P]).then_inc(ld_ident, 16)
            sp.dma_start(X[:, 1, :], x[0, P:SEQ, :]).then_inc(ld_x, 16)

            def row_loads(g, names):
                for name, src in names:
                    _, at, n = ROWS[name]
                    sp.dma_start(rowbuf[at:at + n, g, :], src).then_inc(ld_rows[g], 16)

            def rows_of(v):
                return v.rearrange("(k p) -> k p", p=P)

            sp.wait_ge(rows_zero, 1)
            row_loads(0, [("norm_mix", w["norm_mix"].rearrange("l (k p) -> (l k) p", p=P)),
                          ("norm_ffn", w["norm_ffn"].rearrange("l (k p) -> (l k) p", p=P)),
                          ("a_gain", rows_of(w["a_v_gain"][0])),
                          ("cvec", w["c_2"].rearrange("a (k p) -> (a k) p", p=P)),
                          ("mix_g", rows_of(w["mix_norm_g_2"][0])),
                          ("bcw", w["b_conv_w"][0].rearrange("t (k p) -> (t k) p", p=P))])

            def small_loads():
                fcw, fcb = w["f_conv_w"], w["f_conv_b"]
                sp.dma_start(const[:, P:], w["constants"][:, P:]).then_inc(ld_const, 16)
                sp.dma_start(ws_in, w["a_w_s"][0].rearrange("g t s -> t g s")).then_inc(ld_ws, 16)
                sp.dma_start(bsb, w["a_b_s"][0].partition_broadcast(P)).then_inc(ld_bs, 16)
                row_loads(1, [("fcw0_0", rows_of(fcw[0, 0])), ("fcw0_1", rows_of(fcw[0, 1])),
                              ("moe_g", rows_of(w["moe_norm_g_2"][0])), ("k_k", rows_of(w["rwkv_k_k_2"][0])),
                              ("k_a", rows_of(w["rwkv_k_a_2"][0])), ("w0", rows_of(w["rwkv_w0_2"][0])),
                              ("a0", rows_of(w["rwkv_a0_2"][0]))])
                row_loads(2, [("fcw0_2", rows_of(fcw[0, 2])), ("fcb0", rows_of(fcb[0])),
                              ("lam", rows_of(w["b_lambda"][0])), ("bcb", rows_of(w["b_conv_b"][0]))])
                row_loads(3, [("fcw1_0", rows_of(fcw[1, 0])), ("fcw1_1", rows_of(fcw[1, 1])),
                              ("bba", w["b_b_a"][0].rearrange("h (k p) -> (h k) p", p=P)),
                              ("bbx", w["b_b_x"][0].rearrange("h (k p) -> (h k) p", p=P))])
                mu = w["rwkv_mu_2"][0]
                row_loads(4, [("fcw1_2", rows_of(fcw[1, 2])), ("fcb1", rows_of(fcb[1])),
                              ("mu", rows_of(mu[0:14 * P])),
                              ("r_k", w["rwkv_r_k_2"][0].rearrange("(m h) n -> m (h n)", h=2)),
                              ("kv_g", rows_of(w["kv_norm_g_2"][0]))])
                at = ROWS["mu_tail"][1]
                sp.dma_start(rowbuf[at:at + 1, 4, 0:32], mu[14 * P:14 * P + 32].unsqueeze(0)).then_inc(ld_rows[4], 16)
                for name, src in (("q_g", w["q_norm_g_2"]), ("k_g", w["k_norm_g_2"])):
                    at = ROWS[name][1]
                    for h in range(2):
                        sp.dma_start(rowbuf[at:at + 1, 4, h * HD:(h + 1) * HD], src).then_inc(ld_rows[4], 16)
                for j in range(4):
                    sp.dma_start(adab[32 * j:32 * j + 1, :, :],
                                 w["ada_b_2"].rearrange("a (q j n) -> a j q n", j=4, n=512)[:, j]).then_inc(ld_adab, 16)

            def load(t, first, second, i=None):
                if t >= RING:
                    sp.wait_ge(tile_used, at_turn(t - RING + 1, RING, i))
                for dst, src in (first, second):
                    sp.dma_start(dst, src).then_inc(tile_loaded[t % RING], 16)

            def block_of(wt, k0, n0):
                v = wt.rearrange("(k p) n -> p k n", p=P)
                n = bass.ds(n0, 512)
                return v[:, k0:k0 + 4, n], v[:, k0 + 4:k0 + 8, n]

            def load_block(t, wt, k0, n0, i=None):
                s = ring[t % RING].rearrange("p (k n) -> p k n", n=512)
                a, b = block_of(wt, k0, n0)
                load(t, (s[:, 0:4, :], a), (s[:, 4:8, :], b), i)

            def load_ada(q, js):
                v = w["ada_w_2"][0].rearrange("(k p) n -> p k n", p=P)[:, :, 2048 * q:2048 * q + 2048]
                for j in js:
                    t = T["ada", q][j]
                    s = ring[t % RING].rearrange("p (k n) -> p k n", n=2048)
                    load(t, (s[:, 0, :], v[:, 2 * j, :]), (s[:, 1, :], v[:, 2 * j + 1, :]))

            def load_ffn(l):
                with sp.Fori(0, 3) as i:
                    for u in range(2):
                        for v in range(2):
                            load_block(T["up", l] + 2 * u + v, w["f_w_up"][l], 0,
                                       i * 1024 + (u * 512 + v * FF), i)
                for n in range(2):
                    for kk in range(3):
                        if (l, n, kk) == (0, 1, 2):
                            load_ada(1, (0, 1))
                        load_block(T["down", l][3 * n + kk], w["f_w_down"][l], 8 * kk, 512 * n)

            for j in range(4):
                load_block(T["av"] + j, w["a_w_in"][0], 0, A_W + 512 * j)
                if j == 1:
                    small_loads()
            for j in range(4):
                load_block(T["au"] + j, w["a_w_in"][0], 0, 512 * j)
            for n in range(2):
                for kh in range(2):
                    if (n, kh) == (1, 1):
                        load_ada(0, (0, 1))
                    load_block(T["ao"][2 * n + kh], w["a_w_out"][0], 8 * kh, 512 * n)
            load_ada(0, (2, 3))
            load_ffn(0)
            load_ada(1, (2, 3))
            for j in range(3):
                load_block(T["bx"] + j, w["b_w_in"][0], 0, B_W + 512 * j)
            for j, wt in enumerate((w["b_w_a"][0], w["b_w_x"][0])):
                s = ring[(T["bgate"] + j) % RING][:, 0:12 * 256].rearrange("p (k e) -> p k e", e=256)
                v = wt.rearrange("h (k p) e -> p (h k) e", p=P)
                load(T["bgate"] + j, (s[:, 0:6, :], v[:, 0:6, :]), (s[:, 6:12, :], v[:, 6:12, :]))
            for j in range(3):
                load_block(T["bg"] + j, w["b_w_in"][0], 0, 512 * j)
            for n in range(2):
                load_block(T["bo"][n], w["b_w_out"][0], 0, 512 * n)
            load_ada(2, (0, 1))
            s = ring[T["bo"][2] % RING].rearrange("p (k n) -> p k n", n=512)
            v = w["b_w_out"][0].rearrange("(k p) n -> p k n", p=P)
            load(T["bo"][2], (s[:, 0:4, :], v[:, 8:12, 0:512]), (s[:, 4:8, :], v[:, 8:12, 512:1024]))
            load_ada(2, (2, 3))
            load_ffn(1)
            wi2 = w["w_in_2"][0].rearrange("(k p) n -> p k n", p=P)
            at = {"q": 0, "kv": 512, "kw": 1024, "r": 1064, "lora": 1064 + 1536, "gate": 1064 + 1824}
            s = ring[T["lora"] % RING][:, 0:8 * 328].rearrange("p (k n) -> p k n", n=328)
            load(T["lora"], (s[:, :, 0:40], wi2[:, :, at["kw"]:at["kw"] + 40]),
                 (s[:, :, 40:328], wi2[:, :, at["lora"]:at["lora"] + 288]))
            for j, name in enumerate("rkv"):
                load_block(T[name], w["w_in_2"][0], 0, at["r"] + 512 * j)
            load_block(T["q"], w["w_in_2"][0], 0, at["q"])
            load_block(T["kv"], w["w_in_2"][0], 0, at["kv"])

            def load_wide(t, wt, K):
                s = ring[t % RING][:, 0:K * D].rearrange("p (k n) -> p k n", n=D)
                v = wt.rearrange("(k p) n -> p k n", p=P)
                load(t, (s[:, 0:K // 2, :], v[:, 0:K // 2, :]), (s[:, K // 2:K, :], v[:, K // 2:K, :]))

            for j in range(2):
                load_block(T["gate", j], w["w_in_2"][0], 0, at["gate"] + 512 * j)
            load_wide(T["kvup"], w["w_kv_up_2"][0], 2)
            for j in range(2, 4):
                load_block(T["gate", j], w["w_in_2"][0], 0, at["gate"] + 512 * j)
            load_wide(T["branch"], w["w_branch_attn_2"][0], 4)
            load_wide(T["branch"] + 1, w["w_branch_rwkv_2"][0], 4)
            for n in range(2):
                load_block(T["mo"] + n, w["w_out_2"][0], 0, 512 * n)
            eg = w["expert_w_gate_2"][0].rearrange("e (k p) n -> e p k n", p=P)
            eu = w["expert_w_up_2"][0].rearrange("e (k p) n -> e p k n", p=P)
            ed = w["expert_w_down_2"][0].rearrange("e (k p) n -> e p k n", p=P)
            xs = scratch["xs"].rearrange("(i s) n -> i s n", s=2 * SLOT)

            def load_expert(s, e):
                q = s % 3
                v = (eg, eu, ed)[q][e].rearrange("e p k n -> p (e k) n")
                dst = slots[s].rearrange("p (k n) -> p k n", n=512 if q < 2 else D)
                h = 4 if q < 2 else 2
                for part in (slice(0, h), slice(h, 2 * h)):
                    sp.dma_start(dst[:, part, :], v[:, part, :]).then_inc(e_w[s], 16)

            last_tile = T["mo"] + 1
            for s in sorted(range(6), key=lambda s: last_tile if s >= RING else last_tile - (last_tile - s) % RING):
                sp.wait_ge(tile_used, last_tile + 1 if s >= RING else last_tile + 1 - (last_tile - s) % RING)
                load_expert(s, bass.ds(s // 3, 1))
            sp.wait_ge(scattered, 64)
            sp.dma_start(xsl[0:2 * SLOT], xs[0:1].rearrange("i s n -> (i s) n")).then_inc(e_x, 16)
            sp.wait_ge(eid_ready, 1)
            more = nc.sync.value_load(eid[0:1, MAX_ITEMS + 1:MAX_ITEMS + 2], min_val=NE // 2 - 1,
                                      max_val=MAX_ITEMS // 2 - 1)
            with sp.Fori(0, more) as i:
                for u in range(2):
                    e = nc.sync.value_load(eid[0:1, bass.ds(i * 2 + (u + 2), 1)], min_val=0, max_val=NE - 1)
                    for q in range(3):
                        sp.wait_ge(expert_used, i * 6 + (3 * u + q + 1))
                        load_expert(3 * u + q, bass.ds(e, 1))
                        if (u, q) == (0, 0):
                            sp.dma_start(xsl[0:2 * SLOT], xs[bass.ds(i + 1, 1)].rearrange("i s n -> (i s) n")).then_inc(e_x, 16)
            for c in range(C):
                sp.wait_ge(fin_c, c + 1)
                sp.dma_start(out[0, c * P:(c + 1) * P, :], X[:, c, :]).then_inc(st_out, 16)
            sp.wait_ge(st_out, 32)

        @block.gpsimd
        def _(pool):
            step = Steps(pool, pool_steps)
            nc.gpsimd.memset(rowbuf, 0.0).then_inc(rows_zero, 1)
            def ffn(l):
                with pool.Fori(0, 3) as i:
                    for q in range(4):
                        ms = bass.ds(i * 8 + 2 * q, 2)
                        src = gelu_g[:, q % 2, :].rearrange("p (a t) -> p a t", a=2)
                        pool.wait_ge(ff_prod, at_turn(12 * l + q + 1, 4, i))
                        nc.gpsimd.tensor_copy(ff_hi[:, ms, :], src).then_inc(ff_hi_ready, 1)
                        pool.wait_ge(ff_hi_ready, at_turn(12 * l + q + 1, 4, i))
                        nc.gpsimd.tensor_tensor(ff_lo[:, ms, :], src, ff_hi[:, ms, :].bitcast(F32),
                                                ALU.subtract).then_inc(ff_ready, 1)

            for m in range(8):
                pair = sv_tmp[:, 2 * (m % 2):2 * (m % 2) + 2, :]
                pool.wait_ge(y_prod, m + 1)
                nc.gpsimd.tensor_copy(y_hi[:, 2 * m:2 * m + 2, :], pair).then_inc(y_hi_ready, 1)
                pool.wait_ge(y_hi_ready, m + 1)
                wait_full(pool, ("sv", m))
                nc.gpsimd.tensor_tensor(
                    y_lo[:, :, 2 * m * P:(2 * m + 2) * P].rearrange("p c (m t) -> p m c t", m=2),
                    pair.rearrange("p m (c t) -> p m c t", c=C),
                    y_hi[:, 2 * m:2 * m + 2, :].bitcast(F32).rearrange("p m (c t) -> p m c t", c=C),
                    ALU.subtract).then_inc(y_ready, 1)
            nc.gpsimd.sem_inc(ff_ready, 2)
            ffn(0)
            for hf in range(2):
                for h in range(3 * hf, 3 * hf + 3):
                    wait_drained(pool, ("bi", h))
                    wait_drained(pool, ("bx", h))
                ms = slice(6 * hf, 6 * hf + 6)
                nc.gpsimd.tensor_tensor(It[:, ms, :], It[:, ms, :], xbT[:, ms, :], ALU.mult).then_inc(b_gated, 1)
            wait_drained(pool, ("bi", 0))
            nc.gpsimd.memset(gt1b, 0.0).then_inc(xs_zero, 1)
            pool.wait_ge(xs_zero, 1)
            for j in range(MAX_ITEMS * SLOT // P):
                pool.dma_start(scratch["xs"][j * P:(j + 1) * P, :], gt1b).then_inc(xs_cleared, 16)
            wait_drained(pool, ("ada", 2))
            mod = scratch["mod"]
            for j in range(4):
                pool.dma_start(mod.rearrange("(a q j n) -> a j q n", a=1, j=4, n=512)[:, j],
                               adab[32 * j:32 * j + 1, :, :]).then_inc(st_mod, 16)
            pool.wait_ge(st_mod, 64)
            pool.dma_start(gfb, w["norm_final"].partition_broadcast(P)).then_inc(ld_gfb, 16)
            pool.dma_start(mod_rows[0:16], mod[0:2 * D].rearrange("(k p) -> k p", p=P)).then_inc(ld_mod, 16)
            pool.dma_start(mod_rows[16:32], mod[3 * D:5 * D].rearrange("(k p) -> k p", p=P)).then_inc(ld_mod, 16)
            ffn(1)
            pool.wait_ge(xs_cleared, 16 * (MAX_ITEMS * SLOT // P))
            pool.dma_start(gt1b, mod[2 * D:3 * D].partition_broadcast(P)).then_inc(ld_gt1, 16)
            pool.wait_ge(x_final, 2)
            pool.wait_ge(tile_used, T["down", 1][5] + 1)
            pool.dma_start(wa2[0:HD, :], w["rwkv_w2_2"][0]).then_inc(ld_mx, 16)
            pool.dma_start(wa2[HD:P, :], w["rwkv_a2_2"][0]).then_inc(ld_mx, 16)
            pool.dma_start(g2[:, 0, :], w["rwkv_g2_2"][0, 0:P, :]).then_inc(ld_mx, 16)
            pool.dma_start(g2[0:32, 1, :], w["rwkv_g2_2"][0, P:P + 32, :]).then_inc(ld_mx, 16)
            pool.dma_start(lnw, w["rwkv_ln_w_2"][0].partition_broadcast(P)).then_inc(ld_ln, 16)
            pool.dma_start(lnb, w["rwkv_ln_b_2"][0].partition_broadcast(P)).then_inc(ld_ln, 16)
            pool.dma_start(rw[:, :, 0:NG],
                           w["router_group_w_2"][0].rearrange("(k p) n -> p k n", p=P)).then_inc(ld_route, 16)
            pool.dma_start(rw[:, :, NG:NG + NE],
                           w["router_expert_w_2"][0].rearrange("(k p) n -> p k n", p=P)).then_inc(ld_route, 16)
            pool.dma_start(rbias, w["router_expert_bias_2"][0].partition_broadcast(P)).then_inc(ld_route, 16)
            wait_drained(pool, ("kw", 0))
            for b in range(4):
                pool.dma_start(kirep[32 * b:32 * b + 32, :], kw_sb[0:32, :]).then_inc(ld_rep, 16)
            for c in range(C):
                S = (c + 1) * P
                pool.wait_ge(score_sum, c + 1)
                nc.gpsimd.affine_select(sc[:, c, 0:S], sc[:, c, 0:S], [[-1, S]], ALU.is_ge, -3e38, base=c * P,
                                        channel_multiplier=1).then_inc(score_masked, 1)
            for c in range(C):
                S = (c + 1) * P
                pool.wait_ge(neg_raw, c + 1)
                nc.gpsimd.affine_select(neg[:, c, 0:S], neg[:, c, 0:S], [[-1, S]], ALU.is_ge, FAR, base=c * P,
                                        channel_multiplier=1).then_inc(neg_ready, 1)
            for c in range(C):
                wait_drained(pool, ("vt", c))
            wait_full(pool, ("bonus", 0))
            pool.wait_ge(qr_ready, 1)
            nc.gpsimd.memset(MT, 0.0).then_inc(mt_clear, 1)
            for c in range(C):
                for lv in range(1, 8):
                    for hf in range(2):
                        hs = slice(4 * hf, 4 * hf + 4)
                        if lv == 1:
                            wait_drained(pool, ("mt", c, 4 * hf + 3))
                        if lv > 1 or c > 0:
                            wait_full(pool, ("t1", c, lv - 1, hf) if lv > 1 else ("t1", c - 1, 7, hf))
                        if lv == 2:
                            wait_drained(pool, ("t1", c, 1, hf))
                            pool.wait_ge(x_first, 2 * c + hf + 1)
                        mask = con("level")[:, (lv - 1) * P:lv * P].unsqueeze(1).to_broadcast([P, 4, P])
                        nc.gpsimd.tensor_tensor(CT[:, hs, :], MT[:, hs, 0:P], mask, ALU.mult).then_inc(ct_ready, 1)
            pool.wait_ge(merg, 4)
            pool.dma_start(gt2b, mod[5 * D:6 * D].partition_broadcast(P)).then_inc(ld_gt2, 16)
            pool.wait_ge(idx_ready, 1)
            for c in range(C):
                pool.wait_ge(xn_ready[c], 6)
            pool.wait_ge(xs_cleared, 16 * (MAX_ITEMS * SLOT // P))
            for j in range(2):
                for c in range(C):
                    nc.gpsimd.indirect_dma_start(
                        scratch["xs"], bass.IndirectOffsetOnAxis(ap=idx[:, 2 * j + c:2 * j + c + 1], axis=0),
                        xn[:, c, :], None).then_inc(scattered, 16)
            pool.wait_ge(y_copied, 1)
            for c in range(C):
                for j in range(2):
                    nc.gpsimd.indirect_dma_start(
                        yk[:, 2 * j + c, :], None, scratch["xs"],
                        bass.IndirectOffsetOnAxis(ap=idx[:, 2 * j + c:2 * j + c + 1], axis=0)).then_inc(gathered, 16)
                pool.wait_ge(gathered, 32 * (c + 1))

        @block.scalar
        def _(act):
            step = Steps(act, act_steps)
            def norm(n, ready, gain, bias=None, s=None, before_out=None, split=None, first_tile=None):
                s = n if s is None else s
                ready(act)
                nc.scalar.activation(xn[:, 0, :], X[:, 0, :], ACT.Square, accum_out=ssq[:, 0:1]).then_inc(norm_sq, 1)
                act.wait_ge(norm_var, s + 1)
                nc.scalar.activation(std, var, ACT.Sqrt).then_inc(norm_std, 1)
                act.wait_ge(norm_rstd, s + 1)
                nc.scalar.activation(xn[:, 0, :], X[:, 0, :], ACT.Identity,
                                     scale=rstd[:, 0:1]).then_inc(xn_ready[0], 1)
                if first_tile is not None:
                    split_hi(first_tile)
                if before_out:
                    before_out()
                for b in (1, 3):
                    key = ("norm", n, b)
                    wait_full(act, key)
                    for kk in range(2):
                        last = nc.scalar.activation((hT if split is None else h_hi)[:, 2 * b + kk, :],
                                                    bank(key)[:, kk * SEQ:(kk + 1) * SEQ],
                                                    ACT.Identity, scale=gain(2 * b + kk),
                                                    bias=bias(2 * b + kk) if bias else 0.0)
                    if split is None:
                        drains(last, key)
                    else:
                        last.then_inc(h_hi_ready, 1)

            def after(*keys):
                return lambda eng: [wait_drained(eng, k) for k in keys]

            def ffn(l):
                def first_tap(name, u, h, i):
                    key, q = (name, l, u, h), 2 * u + h
                    y, signal, base = (conv_g, conv_g0, 0) if name == "gate" else (conv_v, conv_v0, KF)
                    for b in range(2):
                        m = i * 8 + (base + 2 * q + b)
                        last = nc.scalar.activation(
                            y[:, h, b * SEQ:(b + 1) * SEQ], bank(key)[:, b * SEQ:(b + 1) * SEQ],
                            ACT.Identity, scale=col_at(f"fcw{l}_2", m), bias=col_at(f"fcb{l}", m))
                    last.then_inc(signal, 1)

                up = T["up", l]
                split_hi(up + 1)
                with act.Fori(0, 3) as i:
                    for u in range(2):
                        for name in ("gate", "val"):
                            for h in range(2):
                                q = 2 * u + h
                                if name == "gate":
                                    act.wait_ge(ff_ready, at_turn(12 * l + q + 1, 4, i))
                                wait_full(act, (name, l, u, h), i)
                                if h == 1:
                                    split_hi(up + 2 * u + 2 + (name == "val"), i)
                                first_tap(name, u, h, i)
                                if name == "val":
                                    wait_drained(act, ("gate", l, u, h), i)
                                    nc.scalar.activation(gelu_g[:, h, :], conv_g[:, h, :],
                                                         ACT.Gelu_apprx_tanh).then_inc(gelu_done, 1)
                for t in T["down", l][2:]:
                    split_hi(t)

            wait_drained(act, ("rows", 0))
            norm(0, lambda eng: eng.wait_ge(ld_x, 32), lambda k: col("norm_mix", k), split=0, first_tile=T["av"])
            split_hi(T["av"] + 1)
            for j in range(4):
                for c in range(C):
                    key = ("av", j, c)
                    wait_full(act, key)
                    if c:
                        split_hi(split_tiles[j + 2])
                    drains(nc.scalar.activation(V[:, c, 512 * j:512 * j + 512], bank(key)[:, :],
                                                ACT.Gelu_apprx_tanh), key)
            for c in range(C):
                wait_drained(act, ("av", 3, c))
                if c:
                    act.wait_ge(v_sq, c)
                nc.scalar.activation(v_junk, V[:, c, :], ACT.Square, accum_out=vsq[:, c:c + 1]).then_inc(v_sq, 1)
            act.wait_ge(v_var, 1)
            nc.scalar.activation(vstd, vvar, ACT.Sqrt).then_inc(v_std, 1)
            nc.scalar.activation(sil, col("cvec", 0, 8), ACT.Silu).then_inc(silu_ready, 1)
            for j in range(4):
                for h in range(2):
                    key = ("au", j, h)
                    wait_full(act, key)
                    if h:
                        split_hi(split_tiles[4 + j + 2])
                    drains(nc.scalar.activation(uT[:, 4 * j + 2 * h:4 * j + 2 * h + 2, :],
                                                bank(key).rearrange("p (a t) -> p a t", a=2),
                                                ACT.Gelu_apprx_tanh), key)
            for j in (2, 3):
                split_hi(T["ao"][j])
            norm(1, after(("ao", 0, 0), ("ao", 1, 0)), lambda k: col("norm_ffn", k), split=1, first_tile=T["up", 0])
            ffn(0)
            norm(2, after(("down", 0, 0, 0), ("down", 0, 1, 0)), lambda k: col("norm_mix", 8 + k), split=2, first_tile=T["bx"])
            act.wait_ge(lam_exp, 1)
            nc.scalar.activation(lamt[:, 1, :], lamt[:, 0, :], ACT.Exp).then_inc(lam_exp, 1)
            split_hi(T["bx"] + 1)
            for q in range(6):
                key = ("bx", q)
                wait_full(act, key)
                if q in (1, 3):
                    split_hi(b_tiles[(q + 1) // 2 + 1])
                for b in range(2):
                    m = 2 * q + b
                    last = nc.scalar.activation(xbT[:, m, :], bank(key)[:, b * SEQ:(b + 1) * SEQ], ACT.Identity,
                                                scale=col("bcw", 36 + m), bias=col("bcb", m))
                last.then_inc(bx0, 1)
            for h in range(B_H):
                for name, dst, bias in (("br", Rt, "bba"), ("bi", It, "bbx")):
                    key = (name, h)
                    wait_full(act, key)
                    for b in range(2):
                        last = nc.scalar.activation(dst[:, 2 * h + b, :], bank(key)[:, b * SEQ:(b + 1) * SEQ],
                                                    ACT.Sigmoid, bias=col(bias, 2 * h + b))
                    drains(last, key)
            split_hi(T["bg"] + 1)
            for hf in range(2):
                ms = slice(6 * hf, 6 * hf + 6)
                act.wait_ge(b_log, hf + 1)
                nc.scalar.activation(At[:, ms, :], Rt[:, ms, :], ACT.Exp)
                nc.scalar.activation(Tt[:, ms, :], Rt[:, ms, :], ACT.Tanh, scale=-1.0).then_inc(b_exp, 1)
            for hf in range(2):
                ms = slice(6 * hf, 6 * hf + 6)
                act.wait_ge(b_m2, hf + 1)
                nc.scalar.activation(Tt[:, ms, :], Tt[:, ms, :], ACT.Sqrt).then_inc(b_mult, 1)
            for q in range(6):
                key = ("bg", q)
                wait_full(act, key)
                if q in (1, 3):
                    split_hi(b_tiles[5 + q // 2])
                if q == 0:
                    act.wait_ge(b_gated, 2)
                drains(nc.scalar.activation(Gt[:, 2 * q:2 * q + 2, :], bank(key).rearrange("p (a t) -> p a t", a=2),
                                            ACT.Gelu_apprx_tanh), key)
            for hf in range(2):
                ms = slice(6 * hf, 6 * hf + 6)
                act.wait_ge(b_prod, hf + 1)
                nc.scalar.copy(b_hi[:, ms, :], Gt[:, ms, :]).then_inc(b_hi_ready, 1)
                split_hi(T["bo"][1 + hf])
            norm(3, after(("bo", 0, 0), ("bo", 1, 0)), lambda k: col("norm_ffn", 8 + k), split=3, first_tile=T["up", 1])
            ffn(1)
            for n in range(2):
                wait_drained(act, ("down", 1, n, 0))
            nc.scalar.activation(xn[:, 0, :], X[:, 0, :], ACT.Square, accum_out=ssq[:, 0:1]).then_inc(norm_sq, 1)
            act.wait_ge(norm_var, 5)
            nc.scalar.activation(std, var, ACT.Sqrt).then_inc(norm_std, 1)
            norm(4, lambda eng: (eng.wait_ge(x_final, 1), eng.wait_ge(norm_sq, 5)), lambda k: gm1[:, k:k + 1], lambda k: col("sh1", k), s=5,
                 before_out=lambda: act.wait_ge(gm_ready, 3))
            wait_full(act, ("kw", 0))
            drains(nc.scalar.copy(kw_sb[0:40, :], banks[5][0:40, 0:SEQ]), ("kw", 0))
            for key, ms in ((("lora", 0), (12, 13)), (("lora", 1), (14,)), (("r", 0), (0, 1)), (("r", 1), (2, 3)),
                            (("k", 0), (4, 5)), (("k", 1), (6, 7)), (("v", 0), (8, 9)), (("v", 1), (10, 11))):
                wait_full(act, key)
                for b, m in enumerate(ms):
                    r = slice(0, 32 if m == 14 else P)
                    last = nc.scalar.activation(mix[r, m, :], bank(key)[r, b * SEQ:(b + 1) * SEQ], ACT.Identity,
                                                scale=omu[r, m:m + 1])
                last.then_inc(mix0, 1)
            for q in range(2):
                wait_drained(act, ("lora", q))
            nc.scalar.activation(mix[0:HD, 12, :], mix[0:HD, 12, :], ACT.Tanh).then_inc(lora_act, 1)
            nc.scalar.activation(mix[:, 13, :], mix[:, 13, :], ACT.Sigmoid).then_inc(lora_act, 1)
            nc.scalar.activation(mix[0:32, 14, :], mix[0:32, 14, :], ACT.Sigmoid).then_inc(lora_act, 1)
            for name, dst, bias in (("zw", sw, "w0"), ("za", aS, "a0")):
                for q in range(2):
                    key = (name, q)
                    wait_full(act, key)
                    for b in range(2):
                        m = 2 * q + b
                        last = nc.scalar.activation(dst[:, m, :], bank(key)[:, b * SEQ:(b + 1) * SEQ], ACT.Sigmoid,
                                                    bias=col(bias, m))
                    drains(last, key)
            for c in range(C):
                key = ("gg", c)
                wait_full(act, key)
                drains(nc.scalar.copy(gtok[:, c, :], bank(key)[:, :]), key)
            for c in range(C):
                wait_full(act, ("q", c))
                nc.scalar.activation(qn[:, c, :], bank(("q", c))[:, :], ACT.Square).then_inc(q_sq, 1)
            wait_full(act, ("kv", 0))
            for c in range(C):
                nc.scalar.activation(kvn[:, c, :], banks[6][:, c * SEQ:(c + 1) * SEQ], ACT.Square,
                                     accum_out=kvst[:, c:c + 1]).then_inc(q_sq, 1)
            wait_full(act, ("qi", 0))
            drains(nc.scalar.copy(qiT, banks[7].rearrange("p (a t) -> p a t", a=2)), ("qi", 0))
            act.wait_ge(cum_ready, 1)
            nc.scalar.activation(em, cum, ACT.Exp, scale=KAPPA).then_inc(exp_ready, 1)
            nc.scalar.activation(sw, sw, ACT.Exp, scale=-KAPPA).then_inc(exp_ready, 1)
            act.wait_ge(exp_ready, 1)
            nc.scalar.activation(cum, cum, ACT.Exp, scale=-KAPPA).then_inc(exp_ready, 1)
            nc.scalar.activation(dmid, cmid, ACT.Exp, scale=-KAPPA).then_inc(exp_ready, 1)
            act.wait_ge(q_var, 1)
            nc.scalar.activation(qst, qst, ACT.Sqrt).then_inc(q_root, 1)
            nc.scalar.activation(kvst, kvst, ACT.Sqrt).then_inc(q_root, 1)
            act.wait_ge(kx2, 1)
            for q in range(2):
                key = ("kn", q)
                wait_full(act, key)
                drains(nc.scalar.activation(sq[:, 2 * q:2 * q + 2, :], bank(key).rearrange("p (a t) -> p a t", a=2),
                                            ACT.Sqrt), key)
            def open_gates(j):
                for q in (2 * j, 2 * j + 1):
                    key = ("ga", q)
                    wait_full(act, key)
                    drains(nc.scalar.activation(gates[:, 2 * q:2 * q + 2, :],
                                                bank(key).rearrange("p (a t) -> p a t", a=2), ACT.Sigmoid), key)

            act.wait_ge(qr_ready, 1)
            open_gates(0)
            open_gates(1)
            wait_drained(act, ("qt", 0))
            wait_drained(act, ("qt", 1))
            for c in range(C):
                wait_full(act, ("kr", c))
                nc.scalar.activation(qn[:, c, :], bank(("kr", c))[:, :], ACT.Square).then_inc(k_sq, 1)
            for c in range(C):
                key = ("vr", c)
                wait_full(act, key)
                drains(nc.scalar.copy(Vt[:, c, :], bank(key)[:, :]), key)
            act.wait_ge(k_var, 1)
            nc.scalar.activation(kst, kst, ACT.Sqrt).then_inc(k_root, 1)
            for c in range(C):
                S = (c + 1) * P
                for b in range(4):
                    key = ("dot", c, b)
                    n = 4 * c + b
                    wait_full(act, key)
                    if n in (4, 5):
                        act.wait_ge(score_sum, 1) if n == 5 else act.wait_ge(rel_used, 3)
                    elif n >= 2:
                        act.wait_ge(rel_used, 3 * ((n - 2) // 4) + (n - 2) % 4 + 1)
                    drains(nc.scalar.activation(rel[:, n % 2, :].rearrange("p (a s) -> p a s", a=2)[:, :, 0:S],
                                         bank(key).rearrange("p (a s) -> p a s", a=2)[:, :, 0:S], ACT.Relu,
                                         scale=float(IHD ** -0.5 * IH ** -0.5)), key)
            open_gates(2)
            open_gates(3)
            for c in range(C):
                S = (c + 1) * P
                for g in range(4):
                    n = 4 * c + g
                    act.wait_ge(lg_ready, n + 1)
                    for j in range(2):
                        h = head_of(g, j)
                        last = nc.scalar.activation(Pb[:, n % 2, j, 0:S], Pb[:, n % 2, j, 0:S], ACT.Exp,
                                                    bias=nmax[:, 8 * c + h:8 * c + h + 1],
                                                    accum_out=psum_[:, 8 * c + h:8 * c + h + 1])
                        last.then_inc(p_ready, 1)
                    key = ("pt", c, g)
                    wait_full(act, key)
                    if n >= 2:
                        act.wait_ge(pv_used, n - 1)
                    w_ = 2 * (c + 1) * P
                    drains(nc.scalar.copy(pT[:, n % 2, 0:2 * (c + 1), :],
                                          bank(key)[:, 0:w_].rearrange("p (a t) -> p a t", t=P)), key)
            for q in range(2):
                key = ("oat", q)
                wait_full(act, key)
                drains(nc.scalar.copy(oaT[:, 2 * q:2 * q + 2, :], bank(key).rearrange("p (a t) -> p a t", a=2)), key)
            for c in range(C):
                key = ("vt", c)
                wait_full(act, key)
                drains(nc.scalar.copy(vtok[:, c, :], bank(key)[:, :]), key)
            for key, dst in ((("bt", 0), btok), (("ktt", 0), ktok)):
                wait_full(act, key)
                drains(nc.scalar.copy(dst, bank(key)[:, :]), key)
            wait_full(act, ("bonus", 0))
            drains(nc.scalar.copy(bonus, banks[2][:, 0:16]), ("bonus", 0))
            for c in range(C):
                for lv in range(2, 8):
                    for hf in range(2):
                        key = ("t1", c, lv, hf)
                        wait_full(act, key)
                        if lv > 2:
                            wait_full(act, ("xb", c, lv - 1, hf))
                        elif c > 0:
                            wait_full(act, ("xb", c - 1, 7, hf))
                        drains(nc.scalar.copy(T1[:, 4 * hf:4 * hf + 4, :],
                                              bank(key).rearrange("p (a t) -> p a t", a=4)), key)
                wait_full(act, ("sa", c))
                drains(nc.scalar.copy(satok[:, c, :], banks[0][:, :]), ("sa", c))
                for par in range(2):
                    key = ("y", c, par)
                    wait_full(act, key)
                    drains(nc.scalar.copy(ytok[:, c, :].rearrange("p (a h n) -> p h a n", h=2, n=HD)[:, par],
                                          bank(key)[:, 0:256].rearrange("p (a n) -> p a n", a=4)), key)
                act.wait_ge(gn_var, c + 1)
                nc.scalar.activation(gn_b, gn_b, ACT.Sqrt).then_inc(gn_root, 1)
            for q in range(2):
                key = ("ort", q)
                wait_full(act, key)
                drains(nc.scalar.copy(orT[:, 2 * q:2 * q + 2, :], bank(key).rearrange("p (a t) -> p a t", a=2)), key)
            norm(5, after(("mo", 0, 0), ("mo", 1, 0)), lambda k: gm2[:, k:k + 1], lambda k: col("sh2", k), s=6)
            act.wait_ge(ge_in, 1)
            nc.scalar.activation(gtmp[:, :, 0:NG], gtmp[:, :, 0:NG], ACT.Exp).then_inc(ge_exp, 1)
            act.wait_ge(two_in, 1)
            nc.scalar.activation(rsm[:, 4:6], rsm[:, 4:6], ACT.Exp).then_inc(two_exp, 1)
            for u in range(2):
                nc.scalar.sem_inc(st_y[u], 16 * STRIPS)
            act.wait_ge(eid_ready, 1)
            pairs = nc.scalar.value_load(eid[0:1, MAX_ITEMS:MAX_ITEMS + 1], min_val=NE // 2, max_val=MAX_ITEMS // 2)
            ys = scratch["xs"].rearrange("(i s) n -> i s n", s=SLOT)
            with act.Fori(0, pairs) as i:
                for u in range(2):
                    act.wait_ge(expert_used, i * 6 + (3 * u + 1))
                    nc.scalar.activation(sg[:, u, :], banks[2][:, 0:P], ACT.Silu).then_inc(sg_ready, 1)
                    act.wait_ge(ht_full, i * 2 + (u + 1))
                    nc.scalar.copy(hTe[:, u, :], banks[4 + u][:, 0:P]).then_inc(ht_ready, 1)
                    act.wait_ge(expert_used, i * 6 + (3 * u + 3))
                    act.wait_ge(st_y[u], i * (16 * STRIPS) + 16 * STRIPS)
                    nc.scalar.copy(ysb[:, u, :], banks[6 + u][:, 0:256]).then_inc(y_sb, 1)
                    act.wait_ge(y_sb, i * 2 + (u + 1))
                    for n in range(STRIPS):
                        act.dma_start(ys[bass.ds(i * 2 + u, 1), :, 256 * n:256 * n + 256].rearrange("i s n -> (i s) n"),
                                      ysb[n * SLOT:(n + 1) * SLOT, u, :]).then_inc(st_y[u], 16)
            for u in range(2):
                act.wait_ge(st_y[u], pairs * (16 * STRIPS) + 16 * STRIPS)
            nc.scalar.sem_inc(y_copied, 1)

        @block.vector
        def _(dve):
            step = Steps(dve, dve_steps)

            def norm(n, ready, gain, bias=None, s=None, before_out=None, split=None, first_tile=None):
                s = n if s is None else s
                ready(dve)
                step(nc.vector.tensor_tensor_reduce(xn[:, 1, :], X[:, 1, :], X[:, 1, :], 1.0, 0.0, ALU.mult, ALU.add,
                                                    ssq[:, 1:2]))
                step.join()
                dve.wait_ge(norm_sq, s + 1)
                nc.vector.tensor_scalar(var, ssq, 1.0 / D, EPS, ALU.mult, ALU.add).then_inc(norm_var, 1)
                dve.wait_ge(norm_std, s + 1)
                nc.vector.reciprocal(rstd, std).then_inc(norm_rstd, 1)
                dve.wait_ge(norm_rstd, s + 1)
                nc.vector.tensor_scalar(xn[:, 1, :], X[:, 1, :], rstd[:, 1:2], None, ALU.mult).then_inc(xn_ready[1], 1)
                if before_out:
                    before_out()
                for b in (0, 2):
                    key = ("norm", n, b)
                    wait_full(dve, key)
                    for kk in range(2):
                        dst, src = hT[:, 2 * b + kk, :], bank(key)[:, kk * SEQ:(kk + 1) * SEQ]
                        k = 2 * b + kk
                        if bias:
                            last = nc.vector.tensor_scalar(dst, src, gain(k), bias(k), ALU.mult, ALU.add)
                        elif split is not None:
                            last = nc.vector.tensor_scalar(h_hi[:, k, :], src, gain(k), None, ALU.mult)
                        else:
                            last = nc.vector.tensor_scalar(dst, src, gain(k), None, ALU.mult)
                    if split is None:
                        drains(last, key)
                    else:
                        last.then_inc(h_hi_ready, 1)
                if split is None:
                    return
                split_lo(first_tile)
                for b in range(4):
                    wait_full(dve, ("norm", n, b))
                dve.wait_ge(h_hi_ready, 4 * split + 4)
                for b in range(4):
                    key = ("norm", n, b)
                    for k in (2 * b, 2 * b + 1):
                        last = nc.vector.scalar_tensor_tensor(h_lo[:, k, :], bank(key)[:, (k % 2) * SEQ:(k % 2 + 1) * SEQ],
                                                              gain(k), h_hi[:, k, :].bitcast(F32), ALU.mult,
                                                              ALU.subtract)
                    drains(last, key)

            def after(*keys):
                return lambda eng: [wait_drained(eng, k) for k in keys]

            def add_to_x(keys):
                for (n, c), key in keys:
                    wait_full(dve, key)
                    xs = X[:, c, 512 * n:512 * n + 512]
                    drains(nc.vector.tensor_tensor(xs, bank(key)[:, :], xs, ALU.add), key)

            def ada(q):
                key = ("ada", q)
                wait_full(dve, key)
                if q == 0:
                    dve.wait_ge(ld_adab, 64)
                for j in range(4):
                    r = slice(32 * j, 32 * j + 1)
                    last = nc.vector.tensor_tensor(adab[r, q, :], bank(key)[r, :], adab[r, q, :], ALU.add)
                drains(last, key)

            def ffn(l):
                def other_taps(name, u, h, i):
                    key, q = (name, l, u, h), 2 * u + h
                    y, signal, base = (conv_g, conv_g0, 0) if name == "gate" else (conv_v, conv_v0, KF)
                    dve.wait_ge(signal, at_turn(12 * l + q + 1, 4, i))
                    for tap in (1, 0):
                        sh = 2 - tap
                        for b in range(2):
                            m = i * 8 + (base + 2 * q + b)
                            to = y[:, h, b * SEQ + sh:(b + 1) * SEQ]
                            last = nc.vector.scalar_tensor_tensor(
                                to, bank(key)[:, b * SEQ:(b + 1) * SEQ - sh], col_at(f"fcw{l}_{tap}", m), to,
                                ALU.mult, ALU.add)
                            if (tap, b) == (0, 1):
                                drains(last, key)
                            else:
                                step(last)
                        if tap == 1:
                            step.join()

                up = T["up", l]
                split_lo(up + 1)
                with dve.Fori(0, 3) as i:
                    step.enter(i, 24)
                    for u in range(2):
                        for name in ("gate", "val"):
                            for h in range(2):
                                q = 2 * u + h
                                if h == 1:
                                    split_lo(up + 2 * u + 2 + (name == "val"), i)
                                other_taps(name, u, h, i)
                                if name == "val":
                                    dve.wait_ge(gelu_done, at_turn(12 * l + q + 1, 4, i))
                                    wait_drained(dve, ("val", l, u, h), i)
                                    nc.vector.tensor_tensor(gelu_g[:, h, :], gelu_g[:, h, :], conv_v[:, h, :],
                                                            ALU.mult).then_inc(ff_prod, 1)
                    step.leave(3)
                for t in T["down", l][2:]:
                    split_lo(t)
                add_to_x([((n, c), ("down", l, n, c)) for n in range(2) for c in range(C)])

            def rows_to_cols(g):
                key = ("rows", g)
                wait_full(dve, key)
                drains(nc.vector.tensor_copy(cols[:, g * P:(g + 1) * P], bank(key)[:, 0:P]), key)

            rows_to_cols(0)
            wait_drained(dve, ("rows", 0))
            norm(0, lambda eng: eng.wait_ge(ld_x, 32), lambda k: col("norm_mix", k), split=0, first_tile=T["av"])
            for j in range(1, 4):
                split_lo(T["av"] + j)
            split_lo(T["au"])
            for g in range(1, 5):
                rows_to_cols(g)
            split_lo(T["au"] + 1)
            dve.wait_ge(v_sq, 2)
            nc.vector.tensor_scalar(vvar, vsq, 1.0 / A_W, EPS, ALU.mult, ALU.add).then_inc(v_var, 1)
            dve.wait_ge(v_std, 1)
            step(nc.vector.reciprocal(vrstd, vstd))
            dve.wait_ge(ld_const, 16)
            keep = con("keep")[:, P:2 * P].unsqueeze(1).to_broadcast([P, 4, P])
            for q in range(2):
                key = ("ws", q)
                wait_full(dve, key)
                drains(nc.vector.tensor_tensor(wsT[:, q * 512:(q + 1) * 512].rearrange("p (g t) -> p g t", g=4),
                                               bank(key).rearrange("p (g t) -> p g t", g=4), keep, ALU.mult), key)
            step.join()
            for q in range(2):
                wait_drained(dve, ("ws", q))
            for c in range(C):
                nc.vector.tensor_scalar(wsr[:, c, :], wsT, vrstd[:, c:c + 1], None, ALU.mult).then_inc(ws_scaled, 1)
            for j in (2, 3):
                split_lo(T["au"] + j)
            split_lo(T["ao"][0])
            dve.wait_ge(ld_bs, 16)
            for m in range(16):
                key = ("sv", m // 2)
                if m % 2 == 0:
                    wait_full(dve, key)
                    if m >= 4:
                        dve.wait_ge(y_ready, m // 2 - 1)
                ins = nc.vector.scalar_tensor_tensor(
                    sv_tmp[:, m % 4, :].rearrange("p (c t) -> p c t", c=C),
                    bank(key)[:, (m % 2) * SEQ:(m % 2 + 1) * SEQ].rearrange("p (c t) -> p c t", c=C),
                    col("a_gain", m), bsb[:, m // 2, :].unsqueeze(1).to_broadcast([P, C, P]), ALU.mult, ALU.add)
                if m % 2:
                    drains(ins, key)
                else:
                    step(ins)
                if m % 2:
                    step.join()
                    wait_drained(dve, key)
                    if m % 4 == 1:
                        wait_drained(dve, ("au", m // 4, 0))
                    else:
                        wait_drained(dve, ("au", m // 4, 1))
                    if m == 7:
                        split_lo(T["ao"][1])
                    pair = sv_tmp[:, m % 4 - 1:m % 4 + 1, :]
                    nc.vector.tensor_tensor(pair, pair, uT[:, m - 1:m + 1, :], ALU.mult).then_inc(y_prod, 1)
            for j in (2, 3):
                split_lo(T["ao"][j])
            add_to_x([((n, c), ("ao", n, c)) for n in range(2) for c in range(C)])
            norm(1, after(("ao", 0, 1), ("ao", 1, 1)), lambda k: col("norm_ffn", k), before_out=lambda: ada(0), split=1, first_tile=T["up", 0])
            ffn(0)
            norm(2, after(("down", 0, 0, 1), ("down", 0, 1, 1)), lambda k: col("norm_mix", 8 + k), before_out=lambda: ada(1), split=2,
                 first_tile=T["bx"])
            lam = col("lam", 0, KB)
            step(nc.vector.tensor_scalar(lamt[:, 0, :], lam, -1.0, None, ALU.mult))
            step.join()
            nc.vector.tensor_tensor(lamt[:, 0, :], lamt[:, 0, :], lam, ALU.min).then_inc(lam_exp, 1)
            dve.wait_ge(lam_exp, 2)
            step(nc.vector.tensor_scalar(lamt[:, 2, :], lamt[:, 1, :], 2.0, None, ALU.add))
            step.join()
            step(nc.vector.reciprocal(lamt[:, 2, :], lamt[:, 2, :]))
            step.join()
            step(nc.vector.tensor_tensor(lamt[:, 1, :], lamt[:, 1, :], lamt[:, 2, :], ALU.mult))
            step.join()
            step(nc.vector.tensor_tensor(lamt[:, 2, :], lamt[:, 1, :], lamt[:, 1, :], ALU.mult))
            step(nc.vector.memset(lamt[:, 3, :], 1.0 / 17))
            for j in range(7, -1, -1):
                step.join()
                step(nc.vector.tensor_tensor(lamt[:, 3, :], lamt[:, 3, :], lamt[:, 2, :], ALU.mult))
                step.join()
                step(nc.vector.tensor_scalar(lamt[:, 3, :], lamt[:, 3, :], 1.0 / (2 * j + 1), None, ALU.add))
            step(nc.vector.tensor_scalar(lamt[:, 0, :], lam, 0.0, 8.0, ALU.min, ALU.mult))
            step.join()
            step(nc.vector.tensor_tensor(lamt[:, 3, :], lamt[:, 3, :], lamt[:, 1, :], ALU.mult))
            step.join()
            step(nc.vector.scalar_tensor_tensor(s8, lamt[:, 3, :], -16.0, lamt[:, 0, :], ALU.mult, ALU.add))
            step.join()
            split_lo(T["bx"] + 1)
            for q in range(6):
                key = ("bx", q)
                if q in (1, 3):
                    split_lo(b_tiles[(q + 1) // 2 + 1])
                dve.wait_ge(bx0, q + 1)
                for tap in (2, 1, 0):
                    sh = 3 - tap
                    for b in range(2):
                        m = 2 * q + b
                        to = xbT[:, m, sh:SEQ]
                        last = nc.vector.scalar_tensor_tensor(to, bank(key)[:, b * SEQ:(b + 1) * SEQ - sh],
                                                              col("bcw", 12 * tap + m), to, ALU.mult, ALU.add)
                        if (tap, b) == (0, 1):
                            drains(last, key)
                        else:
                            step(last)
                    if tap:
                        step.join()
            for h in range(B_H):
                wait_drained(dve, ("br", h))
                for b in range(2):
                    m = 2 * h + b
                    last = nc.vector.tensor_scalar(Rt[:, m, :], Rt[:, m, :], s8[:, m:m + 1], None, ALU.mult)
                if h % 3 == 2:
                    last.then_inc(b_log, 1)
            split_lo(T["bg"] + 1)
            for hf in range(2):
                ms = slice(6 * hf, 6 * hf + 6)
                dve.wait_ge(b_exp, hf + 1)
                dve.wait_ge(b_gated, hf + 1)
                step(nc.vector.tensor_tensor(Gt[:, ms, :], At[:, ms, :], At[:, ms, :], ALU.mult))
                step.join()
                nc.vector.scalar_tensor_tensor(Tt[:, ms, :], Gt[:, ms, :], 1.0, Tt[:, ms, :], ALU.add,
                                               ALU.mult).then_inc(b_m2, 1)

            def b_low_part(hf):
                ms = slice(6 * hf, 6 * hf + 6)
                dve.wait_ge(b_hi_ready, hf + 1)
                nc.vector.tensor_tensor(b_lo[:, ms, :], Gt[:, ms, :], b_hi[:, ms, :].bitcast(F32),
                                        ALU.subtract).then_inc(b_y, 1)

            for hf in range(2):
                ms = slice(6 * hf, 6 * hf + 6)
                dve.wait_ge(b_mult, hf + 1)
                dve.wait_ge(b_gated, hf + 1)
                step(nc.vector.tensor_tensor(It[:, ms, :], It[:, ms, :], Tt[:, ms, :], ALU.mult))
                step.join()
                for m in range(6 * hf, 6 * hf + 6):
                    step(nc.vector.tensor_tensor_scan(Rt[:, m, :], At[:, m, :], It[:, m, :], 0.0, ALU.mult, ALU.add))
                step.join()
                split_lo(b_tiles[5 + hf])
                if hf == 1:
                    b_low_part(0)
                for q in range(3 * hf, 3 * hf + 3):
                    wait_drained(dve, ("bg", q))
                nc.vector.tensor_tensor(Gt[:, ms, :], Rt[:, ms, :], Gt[:, ms, :], ALU.mult).then_inc(b_prod, 1)
            b_low_part(1)
            for j in (1, 2):
                split_lo(T["bo"][j])
            add_to_x([((n, c), ("bo", n, c)) for n in range(2) for c in range(C)])
            norm(3, after(("bo", 0, 1), ("bo", 1, 1)), lambda k: col("norm_ffn", 8 + k), before_out=lambda: ada(2),
                 split=3, first_tile=T["up", 1])
            ffn(1)
            key = ("rows", 5)
            for n in range(2):
                wait_drained(dve, ("down", 1, n, 1))
            step(nc.vector.tensor_tensor_reduce(xn[:, 1, :], X[:, 1, :], X[:, 1, :], 1.0, 0.0, ALU.mult, ALU.add,
                                                ssq[:, 1:2]))
            step.join()
            dve.wait_ge(norm_sq, 5)
            nc.vector.tensor_scalar(var, ssq, 1.0 / D, EPS, ALU.mult, ALU.add).then_inc(norm_var, 1)
            dve.wait_ge(norm_std, 5)
            nc.vector.reciprocal(rstd, std).then_inc(norm_rstd, 1)
            dve.wait_ge(norm_rstd, 5)
            dve.wait_ge(ld_gfb, 16)
            for c in range(C):
                for n in range(2):
                    wait_drained(dve, ("down", 1, n, c))
                nc.vector.scalar_tensor_tensor(X[:, c, :], X[:, c, :], rstd[:, c:c + 1], gfb, ALU.mult,
                                               ALU.mult).then_inc(x_final, 1)
            wait_full(dve, key)
            drains(nc.vector.tensor_copy(cols[:, 5 * P:5 * P + 32], bank(key)[:, 0:32]), key)
            wait_drained(dve, key)
            nc.vector.scalar_tensor_tensor(gm1, col("sc1", 0, 8), 1.0, col("mix_g", 0, 8), ALU.add,
                                           ALU.mult).then_inc(gm_ready, 1)
            nc.vector.scalar_tensor_tensor(gm2, col("sc2", 0, 8), 1.0, col("moe_g", 0, 8), ALU.add,
                                           ALU.mult).then_inc(gm_ready, 1)
            nc.vector.tensor_scalar(omu, col("mu", 0, 15), -1.0, 1.0, ALU.mult, ALU.add).then_inc(gm_ready, 1)
            dve.wait_ge(gm_ready, 3)
            norm(4, lambda eng: eng.wait_ge(x_final, 2), lambda k: gm1[:, k:k + 1], lambda k: col("sh1", k), s=5)
            for n, (key, ms) in enumerate(((("lora", 0), (12, 13)), (("lora", 1), (14,)), (("r", 0), (0, 1)),
                                           (("r", 1), (2, 3)), (("k", 0), (4, 5)), (("k", 1), (6, 7)),
                                           (("v", 0), (8, 9)), (("v", 1), (10, 11)))):
                dve.wait_ge(mix0, n + 1)
                for b, m in enumerate(ms):
                    r = slice(0, 32 if m == 14 else P)
                    last = nc.vector.scalar_tensor_tensor(mix[r, m, 1:SEQ], bank(key)[r, b * SEQ:(b + 1) * SEQ - 1],
                                                          col("mu", m)[r], mix[r, m, 1:SEQ], ALU.mult, ALU.add)
                drains(last, key)
            step(nc.vector.memset(rkbd, 0.0))
            step(nc.vector.tensor_scalar(gq8, col("q_g"), HD ** -0.5, None, ALU.mult))
            step.join()
            for h in range(2):
                step(nc.vector.tensor_copy(rkbd[h * HD:(h + 1) * HD, :, h], col("r_k", 0, 4)[h * HD:(h + 1) * HD]))
            for q in range(2):
                wait_drained(dve, ("k", q))
            for m in range(4):
                step(nc.vector.tensor_scalar(kx[:, m, :], mix[:, 4 + m, :], col("k_k", m), None, ALU.mult))
            step.join()
            nc.vector.tensor_tensor(sq, kx, kx, ALU.mult).then_inc(kx2, 1)
            for q in range(2):
                wait_drained(dve, ("zw", q))
            for m in range(4):
                for c in range(C):
                    t = slice(c * P, (c + 1) * P)
                    step(nc.vector.tensor_tensor_scan(cum[:, m, t], con("ones"), sw[:, m, t], 0.0, ALU.mult, ALU.add))
            step.join()
            cum8 = cum.rearrange("p m (c t) -> p (m c) t", c=C)
            step(nc.vector.tensor_copy(cmid, cum8[:, :, P // 2 - 1]))
            step.join()
            step(nc.vector.tensor_tensor(cum8, cum8, cmid.unsqueeze(2).to_broadcast([P, 8, P]), ALU.subtract))
            step.join()
            nc.vector.tensor_tensor(sw, cum, sw, ALU.subtract).then_inc(cum_ready, 1)
            for q in range(2):
                wait_drained(dve, ("za", q))
            for m in range(4):
                step(nc.vector.tensor_scalar(Kh[:, m, :], aS[:, m, :], -1.0, col("k_a", m), ALU.add, ALU.mult))
            step.join()
            step(nc.vector.scalar_tensor_tensor(mix[:, 4:8, :], Kh, 1.0, mix[:, 4:8, :], ALU.add, ALU.mult))
            dve.wait_ge(q_sq, 4)
            step(nc.vector.tensor_reduce(qst, qn.rearrange("p c (h n) -> p (c h) n", n=HD), AX.X, ALU.add))
            step(nc.vector.tensor_scalar(kvst, kvst, 1.0 / 256, EPS, ALU.mult, ALU.add))
            step.join()
            nc.vector.tensor_scalar(qst, qst, 1.0 / HD, EPS, ALU.mult, ALU.add).then_inc(q_var, 1)
            dve.wait_ge(q_root, 2)
            step(nc.vector.reciprocal(qst, qst))
            step(nc.vector.reciprocal(kvst, kvst))
            step.join()
            for c in range(C):
                key = ("q", c)
                drains(nc.vector.tensor_tensor(qn[:, c, :].rearrange("p (h n) -> p h n", n=HD),
                                               bank(key).rearrange("p (h n) -> p h n", n=HD),
                                               qst[:, 8 * c:8 * c + 8].unsqueeze(2).to_broadcast([P, 8, HD]), ALU.mult), key)
            for c in range(C):
                ins = nc.vector.tensor_scalar(kvn[:, c, :], banks[6][:, c * SEQ:(c + 1) * SEQ], kvst[:, c:c + 1], None,
                                              ALU.mult)
                if c:
                    drains(ins, ("kv", 0))
            for q in range(2):
                wait_drained(dve, ("kn", q))
            step(nc.vector.tensor_scalar(sq, sq, 1e-12, None, ALU.max))
            step.join()
            step(nc.vector.reciprocal(sq, sq))
            step.join()
            step(nc.vector.tensor_tensor(kx, kx, sq, ALU.mult))
            step.join()
            step(nc.vector.tensor_tensor(aS, aS, kx, ALU.mult))
            dve.wait_ge(exp_ready, 4)
            QRv = QR.rearrange("p (m c) a t -> p a m c t", c=C)
            v3 = lambda a: a.rearrange("p m (c t) -> p m c t", c=C)
            q8 = lambda a: a.rearrange("p m (c t) -> p (m c) t", c=C)
            step(nc.vector.tensor_copy(epc, q8(cum)[:, :, P - 1]))
            step(nc.vector.tensor_tensor(QR[:, :, 0, :], q8(kx), q8(sw), ALU.mult))
            step(nc.vector.tensor_tensor(QR[:, :, 1, :], q8(mix[:, 0:4, :]), q8(cum), ALU.mult))
            step.join()
            step(nc.vector.tensor_tensor(aS, aS, em, ALU.mult))
            step(nc.vector.tensor_tensor(Kh, mix[:, 4:8, :], em, ALU.mult))
            nc.vector.tensor_tensor(sq, mix[:, 0:4, :], mix[:, 4:8, :], ALU.mult).then_inc(qr_ready, 1)
            for q in range(2):
                key = ("qt", q)
                wait_full(dve, key)
                drains(nc.vector.tensor_scalar(qT[:, 2 * q:2 * q + 2, :], bank(key).rearrange("p (a t) -> p a t", a=2),
                                               gq8, None, ALU.mult), key)
            key = ("kvt", 0)
            wait_full(dve, key)
            for k in range(2):
                last = nc.vector.tensor_scalar(kvnT[:, k, :], bank(key)[:, k * SEQ:(k + 1) * SEQ], col("kv_g", k), None,
                                               ALU.mult)
            drains(last, key)
            dve.wait_ge(k_sq, 2)
            step(nc.vector.tensor_reduce(kst, qn.rearrange("p c (h n) -> p (c h) n", n=HD), AX.X, ALU.add))
            step.join()
            nc.vector.tensor_scalar(kst, kst, 1.0 / HD, EPS, ALU.mult, ALU.add).then_inc(k_var, 1)
            dve.wait_ge(k_root, 1)
            step(nc.vector.reciprocal(kst, kst))
            step.join()
            for c in range(C):
                key = ("kr", c)
                drains(nc.vector.tensor_tensor(qn[:, c, :].rearrange("p (h n) -> p h n", n=HD),
                                               bank(key).rearrange("p (h n) -> p h n", n=HD),
                                               kst[:, 8 * c:8 * c + 8].unsqueeze(2).to_broadcast([P, 8, HD]), ALU.mult), key)
            key = ("wi", 0)
            wait_full(dve, key)
            drains(nc.vector.tensor_copy(wi, bank(key)[:, 0:16]), key)
            wait_drained(dve, key)
            for c in range(C):
                S = (c + 1) * P
                for b in range(4):
                    n = 4 * c + b
                    wait_drained(dve, ("dot", c, b))
                    for j in range(2):
                        h = b + 4 * j
                        src = rel[:, n % 2, j * SEQ:j * SEQ + S]
                        wih = wi[:, 8 * c + h:8 * c + h + 1]
                        if (b, j) == (0, 0):
                            ins = nc.vector.tensor_scalar(sc[:, c, 0:S], src, wih, None, ALU.mult)
                        else:
                            ins = nc.vector.scalar_tensor_tensor(sc[:, c, 0:S], src, wih, sc[:, c, 0:S], ALU.mult,
                                                                 ALU.add)
                        if (b, j) == (3, 1):
                            ins.then_inc(score_sum, 1)
                            dve.wait_ge(score_sum, c + 1)
                        elif j == 0:
                            step(ins)
                            step.join()
                        else:
                            ins.then_inc(rel_used, 1)
                            dve.wait_ge(rel_used, 3 * c + b + 1)
            for q in range(2):
                key = ("kt", q)
                wait_full(dve, key)
                drains(nc.vector.tensor_scalar(kT[:, 2 * q:2 * q + 2, :], bank(key).rearrange("p (a t) -> p a t", a=2),
                                               col("k_g"), None, ALU.mult), key)
            for c in range(C):
                S = (c + 1) * P
                dve.wait_ge(score_masked, c + 1)
                for r in range(TOPK // 8):
                    src = (sc if r == 0 else work)[:, c, 0:S]
                    step(nc.vector.max(m8[:, 0:8], src))
                    step.join()
                    step(nc.vector.match_replace(work[:, c, 0:S], m8[:, 0:8], src, -3.4e38))
                    step.join()
                step(nc.vector.tensor_scalar(neg[:, c, 0:S], work[:, c, 0:S], -3.2e38, None, ALU.is_lt))
                step.join()
                nc.vector.tensor_scalar(neg[:, c, 0:S], neg[:, c, 0:S], -1.0, -FAR, ALU.add,
                                        ALU.mult).then_inc(neg_raw, 1)
            for c in range(C):
                S = (c + 1) * P
                dve.wait_ge(neg_ready, c + 1)
                for g in range(4):
                    n = 4 * c + g
                    key = ("lg", c, g)
                    wait_full(dve, key)
                    if n >= 2:
                        wait_full(dve, ("pt", (n - 2) // 4, (n - 2) % 4))
                    for j in range(2):
                        h = head_of(g, j)
                        slope = 2.0 ** (-8.0 * (h + 1) / AH)
                        ins = nc.vector.scalar_tensor_tensor(Pb[:, n % 2, j, 0:S], con("dist")[:, c * SEQ:c * SEQ + S],
                                                             -slope, bank(key)[:, j * SEQ:j * SEQ + S], ALU.mult,
                                                             ALU.add)
                        if j:
                            drains(ins, key)
                        else:
                            step(ins)
                    step.join()
                    wait_drained(dve, key)
                    for j in range(2):
                        h = head_of(g, j)
                        at = 8 * c + h
                        step(nc.vector.tensor_tensor_reduce(Pb[:, n % 2, j, 0:S], Pb[:, n % 2, j, 0:S], neg[:, c, 0:S],
                                                            1.0, -3.3e38, ALU.add, ALU.max, nmax[:, at:at + 1]))
                    step.join()
                    for j in range(2):
                        at = 8 * c + head_of(g, j)
                        ins = nc.vector.tensor_scalar(nmax[:, at:at + 1], nmax[:, at:at + 1], -1.0, None, ALU.mult)
                        if j:
                            ins.then_inc(lg_ready, 1)
                        else:
                            step(ins)
            dve.wait_ge(p_ready, 16)
            step(nc.vector.reciprocal(prec, psum_))
            step.join()
            for c in range(C):
                key = ("o", c)
                wait_full(dve, key)
                drains(nc.vector.tensor_tensor(otok[:, c, :].rearrange("p (h n) -> p h n", n=HD),
                                               bank(key).rearrange("p (h n) -> p h n", n=HD),
                                               prec[:, 8 * c:8 * c + 8].unsqueeze(2).to_broadcast([P, 8, HD]), ALU.mult), key)
            dve.wait_ge(mt_clear, 1)

            def gated(b, q):
                key = ("br", b, q)
                wait_full(dve, key)
                g = gates[:, 8 * b + 2 * q:8 * b + 2 * q + 2, :]
                drains(nc.vector.tensor_tensor(g, bank(key).rearrange("p (a t) -> p a t", a=2), g, ALU.mult), key)

            keep_u = con("keep").bitcast(U32)
            id4 = ident.unsqueeze(1).to_broadcast([P, 4, P])
            for c in range(C):
                for h in range(8):
                    key = ("mt", c, h)
                    wait_full(dve, key)
                    drains(nc.vector.copy_predicated(MT[:, h, :], keep_u, bank(key)[:, :]), key)
                for hf in range(2):
                    hs = slice(4 * hf, 4 * hf + 4)
                    key = ("t1", c, 1, hf)
                    wait_full(dve, key)
                    drains(nc.vector.tensor_tensor(Xm[:, hs, :], id4, bank(key).rearrange("p (a t) -> p a t", a=4),
                                                   ALU.subtract), key)
                    nc.vector.tensor_tensor(XT[:, c, hs, :], id4, CT[:, hs, :], ALU.subtract).then_inc(x_first, 1)
                for lv in range(2, 8):
                    for hf in range(2):
                        hs = slice(4 * hf, 4 * hf + 4)
                        for name, dst in (("xa", Xm[:, hs, :]), ("xb", XT[:, c, hs, :])):
                            if lv == 7 and name == "xa":
                                continue
                            key = (name, c, lv, hf)
                            wait_full(dve, key)
                            if lv == 2:
                                dve.wait_ge(x_first, 2 * c + hf + 1)
                                wait_drained(dve, ("t1", c, 1, hf))
                            else:
                                wait_drained(dve, (name, c, lv - 1, hf))
                            drains(nc.vector.tensor_tensor(dst, dst, bank(key).rearrange("p (a t) -> p a t", a=4),
                                                           ALU.subtract), key)
                    if c == 1 and lv < 4:
                        gated(0, lv - 2)
                for par in range(2):
                    key = ("rh", c, par)
                    wait_full(dve, key)
                    drains(nc.vector.tensor_scalar(rhtok.rearrange("p (a h n) -> p h a n", h=2, n=HD)[:, par],
                                                   bank(key)[:, 0:256].rearrange("p (a n) -> p a n", a=4), -1.0, None,
                                                   ALU.mult), key)
                if c == 0:
                    key = ("z", 0)
                    wait_full(dve, key)
                    for m in range(4):
                        ins = nc.vector.tensor_scalar(zst[:, m, :], banks[4][:, m * HD:(m + 1) * HD],
                                                      epc[:, 2 * m:2 * m + 1], dmid[:, 2 * m + 1:2 * m + 2], ALU.mult,
                                                      ALU.mult)
                    drains(ins, key)
                for par in range(2):
                    wait_drained(dve, ("y", c, par))
                Y = ytok[:, c, :]
                Y8 = Y.rearrange("p (h n) -> p h n", n=HD)
                V8 = vtok[:, c, :].rearrange("p (h n) -> p h n", n=HD)
                R8 = rhtok.rearrange("p (h n) -> p h n", n=HD)
                spread = lambda a: a.unsqueeze(2).to_broadcast([P, 8, HD])
                step(nc.vector.tensor_reduce(gn_a, Y8, AX.X, ALU.add))
                step.join()
                step(nc.vector.tensor_scalar(gn_a, gn_a, 1.0 / HD, None, ALU.mult))
                step.join()
                step(nc.vector.tensor_tensor(Y8, Y8, spread(gn_a), ALU.subtract))
                step.join()
                wait_full(dve, ("sa", c))
                step(nc.vector.tensor_tensor(rhtok, Y, Y, ALU.mult))
                step.join()
                step(nc.vector.tensor_reduce(gn_b, R8, AX.X, ALU.add))
                step.join()
                nc.vector.tensor_scalar(gn_b, gn_b, 1.0 / HD, 64e-5, ALU.mult, ALU.add).then_inc(gn_var, 1)
                dve.wait_ge(gn_root, c + 1)
                step(nc.vector.reciprocal(gn_a, gn_b))
                step.join()
                step(nc.vector.tensor_tensor(Y8, Y8, spread(gn_a), ALU.mult))
                wait_drained(dve, ("bonus", 0))
                step(nc.vector.tensor_tensor(R8, V8, spread(bonus.rearrange("p (c h) -> p c h", c=C)[:, c]), ALU.mult))
                step.join()
                dve.wait_ge(ld_ln, 32)
                step(nc.vector.tensor_tensor(Y, Y, lnw, ALU.mult))
                step(nc.vector.tensor_tensor(rhtok, rhtok, lnb, ALU.add))
                step.join()
                step(nc.vector.tensor_tensor(Y, Y, rhtok, ALU.add))
                step.join()
                nc.vector.tensor_tensor(Y, Y, gtok[:, c, :], ALU.mult).then_inc(or_rows, 1)
            for q in (2, 3):
                gated(0, q)
            for q in range(4):
                gated(1, q)
                wait_drained(dve, ("br", 1, q))
                wait_drained(dve, ("br", 0, q))
                nc.vector.tensor_tensor(mergT[:, 2 * q:2 * q + 2, :], gates[:, 2 * q:2 * q + 2, :],
                                        gates[:, 8 + 2 * q:8 + 2 * q + 2, :], ALU.add).then_inc(merg, 1)
            dve.wait_ge(ld_gt1, 16)
            for n in range(2):
                for c in range(C):
                    key = ("mo", n, c)
                    wait_full(dve, key)
                    ns = slice(512 * n, 512 * n + 512)
                    step(nc.vector.tensor_tensor(ytok[:, c, :], bank(key)[:, :], gt1b[:, ns], ALU.mult))
                    step.join()
                    drains(nc.vector.tensor_tensor(X[:, c, ns], X[:, c, ns], ytok[:, c, :], ALU.add), key)
                    wait_drained(dve, key)
            norm(5, after(("mo", 0, 1), ("mo", 1, 1)), lambda k: gm2[:, k:k + 1], lambda k: col("sh2", k), s=6)

            def run(ins):
                step(ins)
                step.join()

            dve.wait_ge(ld_route, 48)
            key = ("route", 0)
            wait_full(dve, key)
            drains(nc.vector.tensor_copy(lg, bank(key)[:, 0:72].rearrange("p (c n) -> p c n", c=C)), key)
            wait_drained(dve, key)
            io = con("iota")
            b3 = lambda a, n: a.unsqueeze(2).to_broadcast([P, C, n])
            io_c = lambda n: io[:, 0:n].unsqueeze(1).to_broadcast([P, C, n])
            gmax, gsum, pg = rsm[:, 0:2], rsm[:, 2:4], rsm[:, 2:4]
            run(nc.vector.tensor_reduce(gmax, lg[:, :, 0:NG], AX.X, ALU.max))
            G4 = gtmp[:, :, 0:NG]
            nc.vector.tensor_tensor(G4, lg[:, :, 0:NG], b3(gmax, NG), ALU.subtract).then_inc(ge_in, 1)
            dve.wait_ge(ge_exp, 1)
            run(nc.vector.tensor_reduce(gsum, G4, AX.X, ALU.add))
            run(nc.vector.reciprocal(pg, gsum))

            def first_max(oh_out, values, vmax, n, tmp):
                run(nc.vector.tensor_tensor(tmp, values, b3(vmax, n), ALU.is_lt))
                run(nc.vector.scalar_tensor_tensor(tmp, tmp, 1000.0, io_c(n), ALU.mult, ALU.add))
                run(nc.vector.tensor_reduce(rsm[:, 6:8], tmp, AX.X, ALU.min))
                run(nc.vector.tensor_tensor(oh_out, io_c(n), b3(rsm[:, 6:8], n), ALU.is_equal))

            first_max(gtmp[:, :, NG:2 * NG], lg[:, :, 0:NG], gmax, NG, G4)
            run(nc.vector.tensor_scalar(gtmp[:, :, NG:2 * NG], gtmp[:, :, NG:2 * NG], -1.0, -FAR, ALU.add, ALU.mult))
            run(nc.vector.tensor_tensor(elm, lg[:, :, NG:NG + NE], rbias.unsqueeze(1).to_broadcast([P, C, NE]), ALU.add))
            for c in range(C):
                run(nc.vector.tensor_tensor(elm[:, c, :].rearrange("p (g e) -> p g e", e=EPG),
                                            elm[:, c, :].rearrange("p (g e) -> p g e", e=EPG),
                                            gtmp[:, c, NG:2 * NG].unsqueeze(2).to_broadcast([P, NG, EPG]), ALU.add))
            run(nc.vector.tensor_reduce(rsm[:, 8:10], elm, AX.X, ALU.max))
            first_max(oh[:, 0], elm, rsm[:, 8:10], NE, etmp)
            run(nc.vector.scalar_tensor_tensor(elm, oh[:, 0], 3 * FAR, elm, ALU.mult, ALU.add))
            run(nc.vector.tensor_reduce(rsm[:, 10:12], elm, AX.X, ALU.max))
            first_max(oh[:, 1], elm, rsm[:, 10:12], NE, etmp)
            nc.vector.tensor_tensor(msum, oh[:, 0], oh[:, 1], ALU.add).then_inc(picks, 1)
            nc.vector.tensor_tensor(rsm[:, 4:6], rsm[:, 10:12], rsm[:, 8:10], ALU.subtract).then_inc(two_in, 1)
            key = ("count", 0)
            wait_full(dve, key)
            run(nc.vector.tensor_tensor(cnt4, bank(key)[:, 64:96].unsqueeze(2).to_broadcast([P, NE, STEPS]),
                                        con("steps").unsqueeze(1).to_broadcast([P, NE, STEPS]), ALU.is_gt))
            run(nc.vector.tensor_reduce(icl[:, 0, :], cnt4, AX.X, ALU.add))
            run(nc.vector.tensor_tensor_scan(icl[:, 1, :], con("ones")[:, 0:NE], icl[:, 0, :], 0.0, ALU.mult, ALU.add))
            run(nc.vector.tensor_tensor(icl[:, 2, :], icl[:, 1, :], icl[:, 0, :], ALU.subtract))
            run(nc.vector.scalar_tensor_tensor(icl[:, 2, :], icl[:, 2, :], float(SLOT), con("extra_item"), ALU.mult,
                                               ALU.add))
            rank = bank(key)[:, 0:64].rearrange("p (c e) -> p c e", c=C)
            run(nc.vector.tensor_scalar(etmp, rank, float(SLOT), None, ALU.is_ge))
            run(nc.vector.tensor_tensor(etmp, etmp, icl[:, 2, :].unsqueeze(1).to_broadcast([P, C, NE]), ALU.mult))
            drains(nc.vector.tensor_tensor(dest, rank, con("first_item").unsqueeze(1).to_broadcast([P, C, NE]),
                                           ALU.add), key)
            wait_drained(dve, key)
            run(nc.vector.tensor_tensor(dest, dest, etmp, ALU.add))
            for j in range(2):
                run(nc.vector.tensor_tensor(etmp, oh[:, j], dest, ALU.mult))
                run(nc.vector.tensor_reduce(fidx[:, 2 * j:2 * j + 2], etmp, AX.X, ALU.add))
            nc.vector.tensor_copy(idx, fidx[:, 0:4]).then_inc(idx_ready, 1)
            extra_of = fidx[:, 4 + NE:4 + MAX_ITEMS]
            pairs_f = fidx[:, 4 + MAX_ITEMS:5 + MAX_ITEMS]
            more_f = fidx[:, 5 + MAX_ITEMS:6 + MAX_ITEMS]
            step(nc.vector.tensor_copy(fidx[:, 4:4 + NE], io[:, 0:NE]))
            run(nc.vector.tensor_tensor(itm, icl[:, 1, :].unsqueeze(1).to_broadcast([P, EXTRA, NE]),
                                        io[:, 0:EXTRA].unsqueeze(2).to_broadcast([P, EXTRA, NE]), ALU.is_le))
            run(nc.vector.tensor_reduce(extra_of, itm, AX.X, ALU.add))
            step(nc.vector.tensor_scalar(extra_of, extra_of, float(NE - 1), None, ALU.min))
            run(nc.vector.tensor_tensor(itm[:, 0, 0:EXTRA // 2], con("pairs"), icl[:, 1, NE - 1:NE].to_broadcast([P, EXTRA // 2]),
                                        ALU.is_lt))
            run(nc.vector.tensor_reduce(pairs_f, itm[:, 0, 0:EXTRA // 2], AX.X, ALU.add))
            run(nc.vector.tensor_scalar(more_f, pairs_f, float(NE // 2 - 1), None, ALU.add))
            run(nc.vector.tensor_scalar(pairs_f, pairs_f, float(NE // 2), None, ALU.add))
            nc.vector.tensor_copy(eid, fidx[:, 4:4 + MAX_ITEMS + 2]).then_inc(eid_ready, 1)
            dve.wait_ge(two_exp, 1)
            run(nc.vector.tensor_scalar(rsm[:, 12:14], rsm[:, 4:6], 1.0, None, ALU.add))
            run(nc.vector.reciprocal(rsm[:, 12:14], rsm[:, 12:14]))
            run(nc.vector.tensor_tensor(rsm[:, 12:14], rsm[:, 12:14], pg, ALU.mult))
            run(nc.vector.tensor_tensor(rsm[:, 14:16], rsm[:, 12:14], rsm[:, 4:6], ALU.mult))
            dve.wait_ge(eid_ready, 1)
            pairs = nc.vector.value_load(eid[0:1, MAX_ITEMS:MAX_ITEMS + 1], min_val=NE // 2, max_val=MAX_ITEMS // 2)
            with dve.Fori(0, pairs) as i:
                dve.wait_ge(tx_full, i + 1)
                nc.vector.tensor_tensor(xgT, banks[0].rearrange("p (k s) -> p k s", s=2 * SLOT),
                                        gm2.unsqueeze(2).to_broadcast([P, KD, 2 * SLOT]), ALU.mult).then_inc(xg_half, 1)
                dve.wait_ge(xg_half, i + 1)
                nc.vector.tensor_tensor(xgT, xgT, col("sh2", 0, 8).unsqueeze(2).to_broadcast([P, KD, 2 * SLOT]),
                                        ALU.add).then_inc(xg_ready, 1)
                for u in range(2):
                    dve.wait_ge(expert_used, i * 6 + (3 * u + 2))
                    dve.wait_ge(sg_ready, i * 2 + (u + 1))
                    nc.vector.tensor_tensor(hd[:, u, :], banks[3][:, 0:P], sg[:, u, :],
                                            ALU.mult).then_inc(hd_ready, 1)
            dve.wait_ge(ld_gt2, 16)
            tail = fin_steps
            at = 0
            for c in range(C):
                dve.wait_ge(gathered, 32 * (c + 1))
                nc.vector.tensor_scalar(yk[:, c, :], yk[:, c, :], rsm[:, 12 + c:13 + c], None, ALU.mult).then_inc(tail, 1)
                dve.wait_ge(tail, 3 * c + 1)
                nc.vector.scalar_tensor_tensor(yk[:, c, :], yk[:, 2 + c, :], rsm[:, 14 + c:15 + c], yk[:, c, :], ALU.mult,
                                               ALU.add).then_inc(tail, 1)
                dve.wait_ge(tail, 3 * c + 2)
                nc.vector.tensor_tensor(yk[:, c, :], yk[:, c, :], gt2b, ALU.mult).then_inc(tail, 1)
                dve.wait_ge(tail, 3 * c + 3)
                nc.vector.tensor_tensor(X[:, c, :], X[:, c, :], yk[:, c, :], ALU.add).then_inc(fin_c, 1)

        @block.tensor
        def _(pe):
            def slot(t, n=512):
                return ring[t % RING].rearrange("p (k n) -> p k n", n=n)

            def norm(n):
                for c in range(C):
                    pe.wait_ge(xn_ready[c], n + 1)
                    for k in range(KD):
                        key = ("norm", n, k // 2)
                        if c == 0 and k % 2 == 0:
                            wait_free(pe, key)
                        at = (k % 2) * SEQ + c * P
                        mm = pe.transpose(bank(key)[:, at:at + P], xn[:, c, k * P:(k + 1) * P], ident)
                        if c == 1 and k % 2 == 1:
                            fills(mm, key)

            def h_ready(n):
                for b in range(4):
                    wait_drained(pe, ("norm", n, b))

            def cols_group(key, wt, m0, i=None, rhs=None):
                wait_free(pe, key, i)
                for b in range(2):
                    for k in range(KD):
                        mm = pe.matmul(bank(key)[:, b * SEQ:(b + 1) * SEQ], wt[:, k, (m0 + b) * P:(m0 + b + 1) * P],
                                       hT[:, k, :], start=(k == 0), stop=(k == KD - 1))
                fills(mm, key)

            def ada(q, half):
                key = ("ada", q)
                if half == 0:
                    wait_free(pe, key)
                if (q, half) == (0, 0):
                    pe.wait_ge(silu_ready, 1)
                for k in range(4 * half, 4 * half + 4):
                    t = T["ada", q][k // 2]
                    if k % 2 == 0:
                        wait_tile(pe, t)
                    s = slot(t, 2048)
                    for j in range(4):
                        mm = pe.matmul(bank(key)[32 * j:32 * j + 1, :], sil[:, k:k + 1],
                                       s[:, k % 2, 512 * j:512 * j + 512], start=(k == 0), stop=(k == KD - 1))
                    if k % 2:
                        mm.then_inc(tile_used, 1)

            def parts_of(t):
                return tuple(v[:, :].rearrange("p (k n) -> p k n", n=512)
                             for v in (w_hi[split_no[t] % 2], w_lo[t % RING]))

            def wait_part(t, hf, i=None):
                pe.wait_ge(w_lo_ready, at_turn(2 * split_no[t] + hf + 1, 8, i))

            def cols_group3(key, t, h, i=None, lows=None):
                hi, lo = parts_of(t)
                wait_free(pe, key, i)
                for b in range(2):
                    ms = slice((2 * h + b) * P, (2 * h + b + 1) * P)
                    out_ = bank(key)[:, b * SEQ:(b + 1) * SEQ]
                    for k in range(KD):
                        if (h, b) == (0, 0) and k % 4 == 0:
                            wait_part(t, k // 4, i)
                        pe.matmul(out_, hi[:, k, ms], h_hi[:, k, :], start=(k == 0), stop=False)
                        pe.matmul(out_, lo[:, k, ms], h_hi[:, k, :], start=False, stop=False)
                    if b == 0 and lows is not None:
                        h_ready(lows)
                    for k in range(KD):
                        mm = pe.matmul(out_, hi[:, k, ms], h_lo[:, k, :], start=False, stop=(k == KD - 1))
                fills(mm, key)

            def ffn(l):
                with pe.Fori(0, 3) as i:
                    for u in range(2):
                        for j, name in enumerate(("gate", "val")):
                            for h in range(2):
                                cols_group3((name, l, u, h), T["up", l] + 2 * u + j, h, i,
                                            2 * l + 1 if (u, j, h) == (0, 0, 0) else None)
                for n in range(2):
                    for kk in range(3):
                        t = T["down", l][3 * n + kk]
                        if (l, n, kk) == (0, 1, 2):
                            ada(1, 0)
                        hi, lo = parts_of(t)
                        for c in range(C):
                            key = ("down", l, n, c)
                            cs = slice(c * P, (c + 1) * P)
                            if kk == 0:
                                wait_free(pe, key)
                            for k in range(8):
                                kf = 8 * kk + k
                                if c == 0 and k % 4 == 0:
                                    wait_part(t, k // 4)
                                if n == 0 and c == 0 and k % 2 == 0:
                                    pe.wait_ge(ff_ready, 12 * l + kf // 2 + 3)
                                pe.matmul(bank(key)[:, :], ff_hi[:, kf, cs], hi[:, k, :], start=(kf == 0), stop=False)
                                pe.matmul(bank(key)[:, :], ff_hi[:, kf, cs], lo[:, k, :], start=False, stop=False)
                                mm = pe.matmul(bank(key)[:, :], ff_lo[:, kf, cs], hi[:, k, :], start=False,
                                               stop=(kf == KF - 1))
                            if kk == 2:
                                fills(mm, key)
                            elif c == 1:
                                mm.then_inc(tile_used, 1)

            def rows_to_cols(g, loads):
                pe.wait_ge(ld_rows[g], 16 * loads)
                key = ("rows", g)
                wait_free(pe, key)
                fills(pe.transpose(bank(key)[:, 0:P], rowbuf[:, g, :], ident), key)

            pe.wait_ge(ld_ident, 16)
            rows_to_cols(0, 6)
            norm(0)
            pe.wait_ge(h_hi_ready, 4)
            for j in range(4):
                hi, lo = parts_of(T["av"] + j)
                for c in range(C):
                    key = ("av", j, c)
                    cs = slice(c * P, (c + 1) * P)
                    wait_free(pe, key)
                    for k in range(KD):
                        if c == 0 and k % 4 == 0:
                            wait_part(T["av"] + j, k // 4)
                        pe.matmul(bank(key)[:, :], h_hi[:, k, cs], hi[:, k, :], start=(k == 0), stop=False)
                        pe.matmul(bank(key)[:, :], h_hi[:, k, cs], lo[:, k, :], start=False, stop=False)
                    if (j, c) == (0, 0):
                        h_ready(0)
                    for k in range(KD):
                        mm = pe.matmul(bank(key)[:, :], h_lo[:, k, cs], hi[:, k, :], start=False, stop=(k == KD - 1))
                    fills(mm, key)
            for g, loads in ((1, 7), (2, 4), (3, 4), (4, 10)):
                rows_to_cols(g, loads)
            pe.wait_ge(ld_ws, 16)
            for q in range(2):
                key = ("ws", q)
                wait_free(pe, key)
                for g in range(4):
                    mm = pe.transpose(bank(key)[:, g * P:(g + 1) * P], ws_in[:, 4 * q + g, :], ident)
                fills(mm, key)
            for j in range(4):
                for h in range(2):
                    cols_group3(("au", j, h), T["au"] + j, h)
            pe.wait_ge(ws_scaled, 2)
            for c in range(C):
                wait_drained(pe, ("av", 3, c))
            for m in range(16):
                key = ("sv", m // 2)
                if m % 2 == 0:
                    wait_free(pe, key)
                for c in range(C):
                    at = (m % 2) * SEQ + c * P
                    g = m // 2
                    mm = pe.matmul(bank(key)[:, at:at + P], V[:, c, m * P:(m + 1) * P], wsr[:, c, g * P:(g + 1) * P],
                                   start=True, stop=True)
                if m % 2:
                    fills(mm, key)
            for n in range(2):
                for kh in range(2):
                    t = T["ao"][2 * n + kh]
                    if (n, kh) == (1, 1):
                        ada(0, 0)
                    hi, lo = parts_of(t)
                    for c in range(C):
                        key = ("ao", n, c)
                        if kh == 0:
                            wait_free(pe, key)
                        for k in range(8):
                            ku = 8 * kh + k
                            if n == 0 and c == 0 and k % 2 == 0:
                                pe.wait_ge(y_ready, ku // 2 + 1)
                            if c == 0 and k % 4 == 0:
                                wait_part(t, k // 4)
                            pe.matmul(bank(key)[:, :], y_hi[:, ku, c * P:(c + 1) * P], hi[:, k, :], start=(ku == 0),
                                      stop=False)
                            pe.matmul(bank(key)[:, :], y_hi[:, ku, c * P:(c + 1) * P], lo[:, k, :], start=False,
                                      stop=False)
                            mm = pe.matmul(bank(key)[:, :], y_lo[:, c, ku * P:(ku + 1) * P], hi[:, k, :], start=False,
                                           stop=(ku == 15))
                        if kh == 1:
                            fills(mm, key)
                        elif c == 1:
                            mm.then_inc(tile_used, 1)
            ada(0, 1)
            norm(1)
            pe.wait_ge(h_hi_ready, 8)
            ffn(0)
            ada(1, 1)
            norm(2)
            pe.wait_ge(h_hi_ready, 12)
            for q in range(6):
                cols_group3(("bx", q), T["bx"] + q // 2, q % 2, lows=2 if q == 0 else None)
            for j in range(2):
                wait_tile(pe, T["bgate"] + j)
            for h in range(B_H):
                wait_drained(pe, ("bx", h))
                for j, name in enumerate(("br", "bi")):
                    key = (name, h)
                    wt = ring[(T["bgate"] + j) % RING][:, 0:12 * 256].rearrange("p (k e) -> p k e", e=256)
                    wait_free(pe, key)
                    for b in range(2):
                        for k in range(2):
                            mm = pe.matmul(bank(key)[:, b * SEQ:(b + 1) * SEQ], wt[:, 2 * h + k, b * P:(b + 1) * P],
                                           xbT[:, 2 * h + k, :], start=(k == 0), stop=(k == 1))
                    fills(mm, key)
            for q in range(6):
                cols_group3(("bg", q), T["bg"] + q // 2, q % 2)
            for j in range(3):
                t = T["bo"][j]
                if j == 2:
                    ada(2, 0)
                hi, lo = parts_of(t)
                for n in ((j,) if j < 2 else (0, 1)):
                    for c in range(C):
                        key = ("bo", n, c)
                        if j < 2:
                            wait_free(pe, key)
                        for k in range(8 if j < 2 else 4):
                            kb, at = (k, k) if j < 2 else (8 + k, 4 * n + k)
                            if (n, c) == (0, 0) and kb in (0, 6):
                                pe.wait_ge(b_y, 1 + kb // 6)
                            cs = slice(c * P, (c + 1) * P)
                            if c == 0 and at % 4 == 0:
                                wait_part(t, at // 4)
                            pe.matmul(bank(key)[:, :], b_hi[:, kb, cs], hi[:, at, :], start=(kb == 0), stop=False)
                            pe.matmul(bank(key)[:, :], b_hi[:, kb, cs], lo[:, at, :], start=False, stop=False)
                            mm = pe.matmul(bank(key)[:, :], b_lo[:, kb, cs], hi[:, at, :], start=False,
                                           stop=(kb == KB - 1))
                        if j == 2:
                            fills(mm, key)
                        elif c == 1:
                            mm.then_inc(tile_used, 1)
            ada(2, 1)
            norm(3)
            pe.wait_ge(h_hi_ready, 16)
            ffn(1)
            pe.wait_ge(ld_mod, 32)
            key = ("rows", 5)
            wait_free(pe, key)
            fills(pe.transpose(bank(key)[:, 0:32], mod_rows[0:32], ident[0:32, 0:32]), key)
            norm(4)
            h_ready(4)
            t = T["lora"]
            wait_tile(pe, t)
            s = ring[t % RING][:, 0:8 * 328].rearrange("p (k n) -> p k n", n=328)

            def cols_block(dst, wt, n0, n1):
                for k in range(KD):
                    mm = pe.matmul(dst, wt[:, k, n0:n1], hT[:, k, :], start=(k == 0), stop=(k == KD - 1))
                return mm

            wait_free(pe, ("kw", 0))
            fills(cols_block(banks[5][0:40, 0:SEQ], s, 0, 40), ("kw", 0))
            wait_free(pe, ("lora", 0))
            cols_block(banks[6][:, 0:SEQ], s, 40, 168)
            fills(cols_block(banks[6][:, SEQ:2 * SEQ], s, 168, 296), ("lora", 0))
            wait_free(pe, ("lora", 1))
            fills(cols_block(banks[7][0:32, 0:SEQ], s, 296, 328), ("lora", 1))
            for name in "rkv":
                wait_tile(pe, T[name])
                for q in range(2):
                    cols_group((name, q), slot(T[name]), 2 * q)
            pe.wait_ge(ld_mx, 64)
            pe.wait_ge(lora_act, 3)
            for name, r in (("zw", slice(0, HD)), ("za", slice(HD, P))):
                for q in range(2):
                    key = (name, q)
                    wait_free(pe, key)
                    for b in range(2):
                        m = 2 * q + b
                        mm = pe.matmul(bank(key)[:, b * SEQ:(b + 1) * SEQ], wa2[r, m * P:(m + 1) * P], mix[r, 12, :],
                                       start=True, stop=True)
                    fills(mm, key)
            for c in range(C):
                key = ("gg", c)
                ts = slice(c * P, (c + 1) * P)
                wait_free(pe, key)
                pe.matmul(bank(key)[:, :], mix[:, 13, ts], g2[:, 0, :], start=True, stop=False)
                fills(pe.matmul(bank(key)[:, :], mix[0:32, 14, ts], g2[0:32, 1, :], start=False, stop=True), key)
            t = T["q"]
            wait_tile(pe, t)
            for c in range(C):
                key = ("q", c)
                wait_free(pe, key)
                for k in range(KD):
                    mm = pe.matmul(bank(key)[:, :], hT[:, k, c * P:(c + 1) * P], slot(t)[:, k, :], start=(k == 0),
                                   stop=(k == KD - 1))
                fills(mm, key)
            t = T["kv"]
            wait_tile(pe, t)
            wait_free(pe, ("kv", 0))
            for c in range(C):
                for k in range(KD):
                    mm = pe.matmul(banks[6][:, c * SEQ:(c + 1) * SEQ], hT[:, k, c * P:(c + 1) * P],
                                   slot(t)[:, k, 0:256], start=(k == 0), stop=(k == KD - 1))
            fills(mm, ("kv", 0))
            cols_group(("qi", 0), slot(t), 2)
            pe.wait_ge(kx2, 1)
            for q in range(2):
                key = ("kn", q)
                wait_free(pe, key)
                for b in range(2):
                    mm = pe.matmul(bank(key)[:, b * SEQ:(b + 1) * SEQ], con("head_ones"), sq[:, 2 * q + b, :],
                                   start=True, stop=True)
                fills(mm, key)

            def turn(key, b, src):
                return pe.transpose(bank(key)[:, b * P:(b + 1) * P], src, ident)

            def gates(j):
                wait_tile(pe, T["gate", j])
                for h in range(2):
                    cols_group(("ga", 2 * j + h), slot(T["gate", j]), 2 * h)

            gates(0)
            for c in range(C):
                wait_drained(pe, ("q", c))
            for q in range(2):
                key = ("qt", q)
                wait_free(pe, key)
                for b in range(2):
                    for c in range(C):
                        mm = turn(key, 2 * b + c, qn[:, c, (2 * q + b) * P:(2 * q + b + 1) * P])
                fills(mm, key)
            wait_drained(pe, ("kv", 0))
            key = ("kvt", 0)
            wait_free(pe, key)
            for b in range(2):
                for c in range(C):
                    mm = turn(key, 2 * b + c, kvn[:, c, b * P:(b + 1) * P])
            fills(mm, key)
            gates(1)
            t = T["kvup"]
            wait_tile(pe, t)
            wait_drained(pe, ("kvt", 0))
            s = ring[t % RING][:, 0:2 * D].rearrange("p (k n) -> p k n", n=D)
            for name, n0 in (("kr", 0), ("vr", 512)):
                for c in range(C):
                    key = (name, c)
                    wait_free(pe, key)
                    for k in range(2):
                        mm = pe.matmul(bank(key)[:, :], kvnT[:, k, c * P:(c + 1) * P], s[:, k, n0:n0 + 512],
                                       start=(k == 0), stop=(k == 1))
                    fills(mm, key)
            key = ("wi", 0)
            wait_free(pe, key)
            wait_drained(pe, ("kw", 0))
            for c in range(C):
                mm = pe.transpose(bank(key)[:, 8 * c:8 * c + 8], kw_sb[32:40, c * P:(c + 1) * P], ident[32:40, 32:40])
            fills(mm, key)
            pe.wait_ge(ld_rep, 64)
            wait_drained(pe, ("qi", 0))
            for c in range(C):
                S = (c + 1) * P
                for b in range(4):
                    key = ("dot", c, b)
                    wait_free(pe, key)
                    r = slice(32 * b, 32 * b + 32)
                    for j in range(2):
                        mm = pe.matmul(bank(key)[:, j * SEQ:j * SEQ + S], qiT[r, j, c * P:(c + 1) * P], kirep[r, 0:S],
                                       start=True, stop=True)
                    fills(mm, key)
            for c in range(C):
                wait_drained(pe, ("kr", c))
            for q in range(2):
                key = ("kt", q)
                wait_free(pe, key)
                for b in range(2):
                    for c in range(C):
                        mm = turn(key, 2 * b + c, qn[:, c, (2 * q + b) * P:(2 * q + b + 1) * P])
                fills(mm, key)
            gates(2)
            gates(3)
            for q in range(2):
                wait_drained(pe, ("kt", q))
                wait_drained(pe, ("qt", q))
                wait_drained(pe, ("vr", q))

            def logits(c, g):
                S = (c + 1) * P
                key = ("lg", c, g)
                wait_free(pe, key)
                for j in range(2):
                    h = head_of(g, j)
                    r = slice(HD * (h % 2), HD * (h % 2) + HD)
                    mm = pe.matmul(bank(key)[:, j * SEQ:j * SEQ + S], qT[r, h // 2, c * P:(c + 1) * P],
                                   kT[r, h // 2, 0:S], start=True, stop=True)
                fills(mm, key)

            def turn_p(c, g):
                key = ("pt", c, g)
                n = 4 * c + g
                wait_free(pe, key)
                pe.wait_ge(p_ready, 2 * n + 2)
                for j in range(2):
                    for st in range(c + 1):
                        mm = turn(key, j * (c + 1) + st, Pb[:, n % 2, j, st * P:(st + 1) * P])
                fills(mm, key)

            def values(c, g):
                key = ("o", c)
                n = 4 * c + g
                if g == 0:
                    wait_free(pe, key)
                wait_drained(pe, ("pt", c, g))
                for j in range(2):
                    h = head_of(g, j)
                    for st in range(c + 1):
                        mm = pe.matmul(bank(key)[:, h * HD:(h + 1) * HD], pT[:, n % 2, j * (c + 1) + st, :],
                                       Vt[:, st, h * HD:(h + 1) * HD], start=(st == 0), stop=(st == c))
                if g == 3:
                    fills(mm, key)
                else:
                    mm.then_inc(pv_used, 1)
            for c in range(C):
                for g in range(4):
                    logits(c, g)
                    if g > 0:
                        turn_p(c, g - 1)
                        values(c, g - 1)
                turn_p(c, 3)
                values(c, 3)
            for c in range(C):
                wait_drained(pe, ("o", c))
            for q in range(2):
                key = ("oat", q)
                wait_free(pe, key)
                for b in range(2):
                    for c in range(C):
                        mm = turn(key, 2 * b + c, otok[:, c, (2 * q + b) * P:(2 * q + b + 1) * P])
                fills(mm, key)
            for c in range(C):
                key = ("vt", c)
                wait_free(pe, key)
                for q in range(2):
                    wait_drained(pe, ("v", q))
                for m in range(4):
                    mm = turn(key, m, mix[:, 8 + m, c * P:(c + 1) * P])
                fills(mm, key)
            pe.wait_ge(qr_ready, 1)
            for key, src in ((("bt", 0), aS), (("ktt", 0), Kh)):
                wait_free(pe, key)
                for m in range(4):
                    mm = turn(key, m, src[:, m, 0:P])
                fills(mm, key)
            key = ("bonus", 0)
            wait_free(pe, key)
            for c in range(C):
                for m in range(4):
                    mm = pe.matmul(bank(key)[:, 8 * c + 2 * m:8 * c + 2 * m + 2], sq[:, m, c * P:(c + 1) * P],
                                   rkbd[:, m, :], start=True, stop=True)
            fills(mm, key)

            def branch(b, q, src):
                key = ("br", b, q)
                s = ring[(T["branch"] + b) % RING].rearrange("p (k n) -> p k n", n=D)
                wait_free(pe, key)
                for j in range(2):
                    m = 2 * q + j
                    for k in range(4):
                        mm = pe.matmul(bank(key)[:, j * SEQ:(j + 1) * SEQ], s[:, k, m * P:(m + 1) * P], src[:, k, :],
                                       start=(k == 0), stop=(k == 3))
                fills(mm, key)

            for c in range(C):
                ts = slice(c * P, (c + 1) * P)
                for h in range(8):
                    key = ("mt", c, h)
                    r = slice(HD * (h % 2), HD * (h % 2) + HD)
                    wait_free(pe, key)
                    qr = QR[r, 2 * (h // 2) + c, :, :]
                    pe.matmul(bank(key)[:, 0:256].rearrange("p (a t) -> p a t", a=2), aS[r, h // 2, ts], qr, start=True,
                              stop=True)
                    fills(pe.matmul(bank(key)[:, 256:512].rearrange("p (a t) -> p a t", a=2), Kh[r, h // 2, ts], qr,
                                    start=True, stop=True), key)
                for lv in range(1, 8):
                    for hf in range(2):
                        key = ("t1", c, lv, hf)
                        wait_free(pe, key)
                        pe.wait_ge(ct_ready, 14 * c + 2 * (lv - 1) + hf + 1)
                        if lv == 2:
                            wait_drained(pe, ("t1", c, 1, hf))
                            pe.wait_ge(x_first, 2 * c + hf + 1)
                        elif lv > 2:
                            wait_drained(pe, ("xa", c, lv - 1, hf))
                        for b in range(4):
                            h = 4 * hf + b
                            if lv == 1:
                                mm = turn(key, b, CT[:, h, :])
                            else:
                                mm = pe.matmul(bank(key)[:, b * P:(b + 1) * P], CT[:, h, :], Xm[:, h, :], start=True,
                                               stop=True)
                        fills(mm, key)
                    if lv == 1:
                        continue
                    if c == 1 and lv < 4:
                        if lv == 2:
                            wait_tile(pe, T["branch"])
                            for q in range(2):
                                wait_drained(pe, ("oat", q))
                        branch(0, lv - 2, oaT)
                    for hf in range(2):
                        wait_drained(pe, ("t1", c, lv, hf))
                        if lv > 2:
                            wait_drained(pe, ("xb", c, lv - 1, hf))
                        for name in ("xa", "xb"):
                            if lv == 7 and name == "xa":
                                continue
                            key = (name, c, lv, hf)
                            wait_free(pe, key)
                            for b in range(4):
                                h = 4 * hf + b
                                left, right = T1[:, h, :], XT[:, c, h, :]
                                if name == "xa":
                                    left, right = right, left
                                mm = pe.matmul(bank(key)[:, b * P:(b + 1) * P], left, right, start=True, stop=True)
                            fills(mm, key)
                for par in range(2):
                    key = ("rh", c, par)
                    wait_free(pe, key)
                    r = slice(HD * par, HD * par + HD)
                    if c == 1:
                        wait_drained(pe, ("z", 0))
                    for a in range(4):
                        h = 2 * a + par
                        dst = bank(key)[:, a * HD:(a + 1) * HD]
                        if c == 1:
                            pe.matmul(dst, QR[r, 2 * a + c, 0, :], zst[r, a, :], start=True, stop=False)
                        mm = pe.matmul(dst, MT[:, h, 256:384], vtok[:, c, h * HD:(h + 1) * HD], start=(c == 0),
                                       stop=True)
                    fills(mm, key)
                for par in range(2):
                    wait_drained(pe, ("rh", c, par))
                for hf in range(2):
                    wait_drained(pe, ("xb", c, 7, hf))
                key = ("sa", c)
                wait_free(pe, key)
                for h in range(8):
                    mm = pe.matmul(bank(key)[:, h * HD:(h + 1) * HD], XT[:, c, h, :], rhtok[:, h * HD:(h + 1) * HD],
                                   start=True, stop=True)
                fills(mm, key)
                wait_drained(pe, key)
                for par in range(2):
                    key = ("y", c, par)
                    wait_free(pe, key)
                    r = slice(HD * par, HD * par + HD)
                    for a in range(4):
                        h = 2 * a + par
                        hs = slice(h * HD, (h + 1) * HD)
                        dst = bank(key)[:, a * HD:(a + 1) * HD]
                        if c == 1:
                            pe.matmul(dst, QR[r, 2 * a + c, 1, :], zst[r, a, :], start=True, stop=False)
                        pe.matmul(dst, MT[:, h, 128:256], satok[:, c, hs], start=(c == 0), stop=False)
                        mm = pe.matmul(dst, MT[:, h, 384:512], vtok[:, c, hs], start=False, stop=True)
                    fills(mm, key)
                if c == 0:
                    key = ("z", 0)
                    wait_free(pe, key)
                    wait_drained(pe, ("bt", 0))
                    wait_drained(pe, ("ktt", 0))
                    for h in range(8):
                        hs = slice(h * HD, (h + 1) * HD)
                        dst = banks[4][HD * (h % 2):HD * (h % 2) + HD, (h // 2) * HD:(h // 2 + 1) * HD]
                        pe.matmul(dst, btok[:, hs], satok[:, 0, hs], start=True, stop=False)
                        mm = pe.matmul(dst, ktok[:, hs], vtok[:, 0, hs], start=False, stop=True)
                    fills(mm, key)
            for q in (2, 3):
                branch(0, q, oaT)
            pe.wait_ge(or_rows, 2)
            for q in range(2):
                key = ("ort", q)
                wait_free(pe, key)
                for b in range(2):
                    for c in range(C):
                        mm = turn(key, 2 * b + c, ytok[:, c, (2 * q + b) * P:(2 * q + b + 1) * P])
                fills(mm, key)
            wait_tile(pe, T["branch"] + 1)
            for q in range(2):
                wait_drained(pe, ("ort", q))
            for q in range(4):
                branch(1, q, orT)
            for n in range(2):
                t = T["mo"] + n
                wait_tile(pe, t)
                for c in range(C):
                    key = ("mo", n, c)
                    wait_free(pe, key)
                    for k in range(KD):
                        if (n, c) == (0, 0) and k % 2 == 0:
                            pe.wait_ge(merg, k // 2 + 1)
                        mm = pe.matmul(bank(key)[:, :], mergT[:, k, c * P:(c + 1) * P], slot(t)[:, k, :],
                                       start=(k == 0), stop=(k == KD - 1))
                    fills(mm, key)
            norm(5)
            h_ready(5)
            pe.wait_ge(ld_route, 48)
            key = ("route", 0)
            wait_free(pe, key)
            for c in range(C):
                for k in range(KD):
                    mm = pe.matmul(bank(key)[:, 36 * c:36 * c + 36], hT[:, k, c * P:(c + 1) * P], rw[:, k, :],
                                   start=(k == 0), stop=(k == KD - 1))
            fills(mm, key)
            key = ("count", 0)
            wait_free(pe, key)
            pe.wait_ge(picks, 1)
            pe.matmul(bank(key)[:, 0:NE], con("before"), msum[:, 0, :], start=True, stop=True)
            pe.matmul(bank(key)[:, NE:2 * NE], con("ones"), msum[:, 0, :], start=True, stop=False)
            pe.matmul(bank(key)[:, NE:2 * NE], con("before"), msum[:, 1, :], start=False, stop=True)
            pe.matmul(bank(key)[:, 2 * NE:3 * NE], con("ones"), msum[:, 0, :], start=True, stop=False)
            fills(pe.matmul(bank(key)[:, 2 * NE:3 * NE], con("ones"), msum[:, 1, :], start=False, stop=True), key)
            wait_drained(pe, key)
            pe.wait_ge(eid_ready, 1)
            pairs = nc.tensor.value_load(eid[0:1, MAX_ITEMS:MAX_ITEMS + 1], min_val=NE // 2, max_val=MAX_ITEMS // 2)
            with pe.Fori(0, pairs) as i:
                pe.wait_ge(e_x, i * 16 + 16)
                for k in range(KD):
                    mm = pe.matmul(banks[0][:, k * 2 * SLOT:(k + 1) * 2 * SLOT], xsl[0:2 * SLOT, k * P:(k + 1) * P],
                                   ident[0:2 * SLOT, 0:2 * SLOT], start=True, stop=True)
                mm.then_inc(tx_full, 1)
                pe.wait_ge(xg_ready, i + 1)
                for u in range(2):
                    for q in range(2):
                        pe.wait_ge(e_w[3 * u + q], i * 32 + 32)
                        s = slots[3 * u + q].rearrange("p (k n) -> p k n", n=512)
                        for k in range(KD):
                            for n in range(STRIPS):
                                mm = pe.matmul(banks[2 + q][n * SLOT:(n + 1) * SLOT, 0:P],
                                               xgT[:, k, u * SLOT:(u + 1) * SLOT], s[:, k, P * n:P * n + P],
                                               start=(k == 0), stop=(k == KD - 1))
                        mm.then_inc(expert_used, 1)
                    pe.wait_ge(hd_ready, i * 2 + (u + 1))
                    pe.transpose(banks[4 + u][:, 0:P], hd[:, u, :], ident).then_inc(ht_full, 1)
                    pe.wait_ge(ht_ready, i * 2 + (u + 1))
                    pe.wait_ge(e_w[3 * u + 2], i * 32 + 32)
                    s = slots[3 * u + 2].rearrange("p (k n) -> p k n", n=D)
                    for k in range(STRIPS):
                        for n in range(STRIPS):
                            mm = pe.matmul(banks[6 + u][n * SLOT:(n + 1) * SLOT, 0:256],
                                           hTe[:, u, k * SLOT:(k + 1) * SLOT], s[:, k, 256 * n:256 * n + 256],
                                           start=(k == 0), stop=(k == STRIPS - 1))
                    mm.then_inc(expert_used, 1)


def kernel(**inputs):
    import numpy as _np
    import concourse.bacc as _bacc
    from concourse import mybir as _mybir
    from concourse.bass_utils import run_bass_kernel_spmd as _run

    nc = _bacc.Bacc("TRN2", target_bir_lowering=False, num_devices=1)
    arrays = {f"in_{name}": _np.ascontiguousarray(a) for name, a in inputs.items()}
    arrays["in_constants"] = _constants()
    aps = {}
    for name, a in arrays.items():
        aps[name[3:]] = nc.dram_tensor(name, a.shape, _mybir.dt.from_np(a.dtype), kind="ExternalInput").ap()
    out = nc.dram_tensor("out_0", (1, SEQ, D), F32, kind="ExternalOutput").ap()
    scratch = {name: nc.dram_tensor(name, shape, F32, kind="Internal").ap() for name, shape in SCRATCH.items()}
    x = aps.pop("x")
    build(nc, x, aps, out, scratch)
    r = _run(nc, [arrays], core_ids=[0])
    return r.results[0]["out_0"]
```
